# Optimizing a Trainium2 kernel written in Bass

```python
import jax, jax.numpy as jnp
from jax import lax
import numpy as np

D_MODEL = 1024
BATCH = 1
SEQ = 256
DEPTH = 2

N_META = 16
GRID_W = 64
NORM_EPS = 1e-6
SC_WIDTH = D_MODEL // 2
SC_KERNEL = 3
GLA_HEADS = 4
GLA_DV = (D_MODEL // 2) // GLA_HEADS
GLA_DK = GLA_DV // 2
GLA_GATE_RANK = 16
GLA_GATE_TAU = 16.0
GLA_CHUNK = 64
MIX_SPLIT_SIZES = [SC_WIDTH] * 3 + [GLA_HEADS * GLA_DK] * 2 + [GLA_HEADS * GLA_DV] * 2 + [GLA_GATE_RANK] * 2
MIX_IN = sum(MIX_SPLIT_SIZES)
ATT_HEAD_DIM = 64
ATT_HEADS = D_MODEL // ATT_HEAD_DIM
ATT_KV_HEADS = 4
ATT_GROUP = ATT_HEADS // ATT_KV_HEADS
ATT_BLOCK = 128
ROPE_THETA = 10000.0
ATT_IN = ATT_HEADS * ATT_HEAD_DIM + 2 * ATT_KV_HEADS * ATT_HEAD_DIM
MOE_GROUPS = 4
MOE_EXPERTS_PER_GROUP = 8
N_EXPERTS = MOE_GROUPS * MOE_EXPERTS_PER_GROUP
MOE_TOP_K = 2
MOE_D_FF = 256
N_EVEN = (DEPTH + 1) // 2
N_ODD = DEPTH // 2

kernel_name = "hybrid_conv_gla_axialgqa_hmoe_encoder"

def rms_norm(x, g):
    xf = x.astype(jnp.float32)
    y = xf * lax.rsqrt(jnp.mean(xf * xf, axis=-1, keepdims=True) + NORM_EPS)
    return (y * g.astype(jnp.float32)).astype(x.dtype)

def centred_depthwise_conv3(z, w):
    zp = jnp.pad(z, ((0, 0), (1, 1), (0, 0)))
    return w[0] * zp[:, :-2] + w[1] * zp[:, 1:-1] + w[2] * zp[:, 2:]

def gla_chunked(q, k, v, log_a, inclusive):
    b_, L, H, DK = q.shape
    DV = v.shape[-1]
    n = L // GLA_CHUNK

    def chunks(t):
        return t.astype(jnp.float32).reshape(b_, n, GLA_CHUNK, H, t.shape[-1]).transpose(1, 0, 3, 2, 4)

    qc, kc, vc, gc = chunks(q), chunks(k), chunks(v), chunks(log_a)
    cum = jnp.cumsum(gc, axis=3)
    cum_last = cum[:, :, :, -1:, :]
    q_dec = qc * jnp.exp(cum)
    k_inv = kc * jnp.exp(-cum)
    k_end = kc * jnp.exp(cum_last - cum)
    scores = jnp.einsum('nbhcd,nbhsd->nbhcs', q_dec, k_inv)
    mask = jnp.tril(jnp.ones((GLA_CHUNK, GLA_CHUNK), dtype=bool), 0 if inclusive else -1)
    o_intra = jnp.einsum('nbhcs,nbhsv->nbhcv', jnp.where(mask, scores, 0.0), vc)
    kv_chunk = jnp.einsum('nbhcd,nbhcv->nbhdv', k_end, vc)
    chunk_decay = jnp.exp(cum_last[:, :, :, 0, :])

    def step(state, inp):
        q_n, kv_n, dec_n = inp
        o_n = jnp.einsum('bhcd,bhdv->bhcv', q_n, state)
        return dec_n[..., None] * state + kv_n, o_n

    s0 = jnp.zeros((b_, H, DK, DV), jnp.float32)
    _, o_inter = lax.scan(step, s0, (q_dec, kv_chunk, chunk_decay))
    o = o_intra + o_inter
    return o.transpose(1, 0, 3, 2, 4).reshape(b_, L, H, DV)

def pad_meta_chunk(t):
    pad = jnp.zeros((t.shape[0], GLA_CHUNK - N_META) + t.shape[2:], t.dtype)
    return jnp.concatenate([t[:, :N_META], pad, t[:, N_META:]], axis=1)

def conv_gla_mixer(h, w_in, conv_w, wg_f, bg_f, wg_b, bg_b, gla_norm_w, w_out):
    bsz, T, _ = h.shape
    u = h @ w_in
    splits = np.cumsum(MIX_SPLIT_SIZES)[:-1].tolist()
    a_b, a_c, a_x, q, k, v, r, g_f, g_b = jnp.split(u, splits, axis=-1)
    y_a = a_b * centred_depthwise_conv3(a_c * a_x, conv_w)
    log_a_f = jax.nn.log_sigmoid((g_f @ wg_f + bg_f).astype(jnp.float32)) / GLA_GATE_TAU
    log_a_b = jax.nn.log_sigmoid((g_b @ wg_b + bg_b).astype(jnp.float32)) / GLA_GATE_TAU
    heads = lambda t, d: t.reshape(bsz, T, GLA_HEADS, d)
    qh = pad_meta_chunk(heads(q, GLA_DK) * (GLA_DK ** -0.5))
    kh = pad_meta_chunk(heads(k, GLA_DK))
    vh = pad_meta_chunk(heads(v, GLA_DV))
    laf = pad_meta_chunk(heads(log_a_f, GLA_DK))
    lab = pad_meta_chunk(heads(log_a_b, GLA_DK))
    o_fwd = gla_chunked(qh, kh, vh, laf, True)
    flip = lambda t: jnp.flip(t, axis=1)
    o_bwd = flip(gla_chunked(flip(qh), flip(kh), flip(vh), flip(lab), False))
    o = o_fwd + o_bwd
    o = jnp.concatenate([o[:, :N_META], o[:, GLA_CHUNK:]], axis=1)
    o = o * lax.rsqrt(jnp.mean(o * o, axis=-1, keepdims=True) + NORM_EPS) * gla_norm_w.astype(jnp.float32)
    y_b = (o * jax.nn.silu(heads(r, GLA_DV).astype(jnp.float32))).reshape(bsz, T, GLA_HEADS * GLA_DV)
    return jnp.concatenate([y_a, y_b.astype(h.dtype)], axis=-1) @ w_out

def axial_rope_tables(n_tokens):
    rows_n = n_tokens // GRID_W
    rows = jnp.repeat(jnp.arange(rows_n), GRID_W).astype(jnp.float32)
    cols = jnp.tile(jnp.arange(GRID_W), rows_n).astype(jnp.float32)
    axis_dims = ATT_HEAD_DIM // 2
    freqs = ROPE_THETA ** (-jnp.arange(0, axis_dims, 2, dtype=jnp.float32) / axis_dims)
    ang = jnp.concatenate([rows[:, None] * freqs, cols[:, None] * freqs], axis=-1)
    ang = jnp.concatenate([jnp.zeros((N_META, ang.shape[1]), jnp.float32), ang], axis=0)
    return jnp.cos(ang), jnp.sin(ang)

def apply_rope(x, cos, sin):
    xr = x.reshape(x.shape[:-1] + (ATT_HEAD_DIM // 2, 2))
    x0, x1 = xr[..., 0], xr[..., 1]
    c, s = cos[None, :, None, :], sin[None, :, None, :]
    return jnp.stack([x0 * c - x1 * s, x0 * s + x1 * c], axis=-1).reshape(x.shape)

def attend_block(q_blk, k, v):
    s = jnp.einsum('bqhgd,bkhd->bhgqk', q_blk, k) * (ATT_HEAD_DIM ** -0.5)
    p = jax.nn.softmax(s, axis=-1)
    return jnp.einsum('bhgqk,bkhd->bqhgd', p, v)

def gqa_axial_mixer(h, w_in, q_norm, k_norm, w_out, cos, sin, with_meta_queries):
    bsz, T, _ = h.shape
    u = h @ w_in
    nq = ATT_HEADS * ATT_HEAD_DIM
    nkv = ATT_KV_HEADS * ATT_HEAD_DIM
    q = u[..., :nq].reshape(bsz, T, ATT_HEADS, ATT_HEAD_DIM)
    k = u[..., nq:nq + nkv].reshape(bsz, T, ATT_KV_HEADS, ATT_HEAD_DIM)
    v = u[..., nq + nkv:].reshape(bsz, T, ATT_KV_HEADS, ATT_HEAD_DIM).astype(jnp.float32)
    q = apply_rope(rms_norm(q, q_norm).astype(jnp.float32), cos, sin)
    k = apply_rope(rms_norm(k, k_norm).astype(jnp.float32), cos, sin)
    q = q.reshape(bsz, T, ATT_KV_HEADS, ATT_GROUP, ATT_HEAD_DIM)
    n_real = T - N_META
    nb = n_real // ATT_BLOCK
    q_blocks = jnp.moveaxis(q[:, N_META:].reshape(bsz, nb, ATT_BLOCK, ATT_KV_HEADS, ATT_GROUP, ATT_HEAD_DIM), 1, 0)
    o = lax.map(lambda qb: attend_block(qb, k, v), q_blocks)
    o = jnp.moveaxis(o, 0, 1).reshape(bsz, n_real, nq)
    if with_meta_queries:
        o_meta = attend_block(q[:, :N_META], k, v).reshape(bsz, N_META, nq)
        o = jnp.concatenate([o_meta, o], axis=1)
    return o.astype(h.dtype) @ w_out

def hierarchical_moe(h, w_group, b_group, w_expert, b_expert, w_gate, w_up, w_down):
    bsz, T, D = h.shape
    xt = h.reshape(-1, D)
    g_logits = (xt @ w_group + b_group).astype(jnp.float32)
    g_prob = jax.nn.softmax(g_logits, axis=-1)
    g_idx = jnp.argmax(g_logits, axis=-1)
    g_p = jnp.take_along_axis(g_prob, g_idx[:, None], axis=-1)
    e_logits = (xt @ w_expert + b_expert).astype(jnp.float32).reshape(-1, MOE_GROUPS, MOE_EXPERTS_PER_GROUP)
    e_sel = jnp.take_along_axis(e_logits, g_idx[:, None, None], axis=1)[:, 0]
    top_v, top_i = lax.top_k(e_sel, MOE_TOP_K)
    top_w = jax.nn.softmax(top_v, axis=-1) * g_p
    expert_id = g_idx[:, None] * MOE_EXPERTS_PER_GROUP + top_i
    gates = jnp.sum(jax.nn.one_hot(expert_id, N_EXPERTS, dtype=jnp.float32) * top_w[..., None], axis=1)
    out = jnp.zeros(xt.shape, jnp.float32)
    for e in range(N_EXPERTS):
        he = jax.nn.silu(xt @ w_gate[e]) * (xt @ w_up[e])
        out = out + gates[:, e:e + 1] * (he @ w_down[e]).astype(jnp.float32)
    return out.astype(h.dtype).reshape(bsz, T, D)

def setup_inputs(seed: int = 0) -> dict:
    key = jax.random.key(seed)
    ks = jax.random.split(key, 24)
    nrm = lambda k, shape, scale: jax.random.normal(k, shape, jnp.float32) * scale
    gain = lambda k, shape: 1.0 + 0.02 * jax.random.normal(k, shape, jnp.float32)
    D = D_MODEL
    return {
        "x": nrm(ks[0], (BATCH, SEQ, D), 1.0),
        "meta_tokens": nrm(ks[1], (N_META, D), 1.0),
        "norm_mix": gain(ks[2], (DEPTH, D)),
        "norm_ffn": gain(ks[3], (DEPTH, D)),
        "norm_final": gain(ks[4], (D,)),
        "sc_w_in": nrm(ks[5], (N_EVEN, D, MIX_IN), D ** -0.5),
        "sc_conv_w": nrm(ks[6], (N_EVEN, SC_KERNEL, SC_WIDTH), SC_KERNEL ** -0.5),
        "gla_w_gate_fwd": nrm(ks[7], (N_EVEN, GLA_GATE_RANK, GLA_HEADS * GLA_DK), GLA_GATE_RANK ** -0.5),
        "gla_b_gate_fwd": nrm(ks[8], (N_EVEN, GLA_HEADS * GLA_DK), 0.1),
        "gla_w_gate_bwd": nrm(ks[9], (N_EVEN, GLA_GATE_RANK, GLA_HEADS * GLA_DK), GLA_GATE_RANK ** -0.5),
        "gla_b_gate_bwd": nrm(ks[10], (N_EVEN, GLA_HEADS * GLA_DK), 0.1),
        "gla_norm_w": gain(ks[11], (N_EVEN, GLA_DV)),
        "sc_w_out": nrm(ks[12], (N_EVEN, SC_WIDTH + GLA_HEADS * GLA_DV, D), (SC_WIDTH + GLA_HEADS * GLA_DV) ** -0.5),
        "att_w_in": nrm(ks[13], (N_ODD, D, ATT_IN), D ** -0.5),
        "att_q_norm": gain(ks[14], (N_ODD, ATT_HEAD_DIM)),
        "att_k_norm": gain(ks[15], (N_ODD, ATT_HEAD_DIM)),
        "att_w_out": nrm(ks[16], (N_ODD, ATT_HEADS * ATT_HEAD_DIM, D), (ATT_HEADS * ATT_HEAD_DIM) ** -0.5),
        "moe_w_group": nrm(ks[17], (DEPTH, D, MOE_GROUPS), D ** -0.5),
        "moe_b_group": nrm(ks[18], (DEPTH, MOE_GROUPS), 0.01),
        "moe_w_expert": nrm(ks[19], (DEPTH, D, N_EXPERTS), D ** -0.5),
        "moe_b_expert": nrm(ks[20], (DEPTH, N_EXPERTS), 0.01),
        "moe_w_gate": nrm(ks[21], (DEPTH, N_EXPERTS, D, MOE_D_FF), D ** -0.5),
        "moe_w_up": nrm(ks[22], (DEPTH, N_EXPERTS, D, MOE_D_FF), D ** -0.5),
        "moe_w_down": nrm(ks[23], (DEPTH, N_EXPERTS, MOE_D_FF, D), MOE_D_FF ** -0.5),
    }

def reference(x, meta_tokens, norm_mix, norm_ffn, norm_final, sc_w_in, sc_conv_w, gla_w_gate_fwd, gla_b_gate_fwd, gla_w_gate_bwd, gla_b_gate_bwd, gla_norm_w, sc_w_out, att_w_in, att_q_norm, att_k_norm, att_w_out, moe_w_group, moe_b_group, moe_w_expert, moe_b_expert, moe_w_gate, moe_w_up, moe_w_down):
    bsz, n_tokens, D = x.shape
    meta = jnp.broadcast_to(meta_tokens.astype(x.dtype)[None], (bsz, N_META, D))
    h = jnp.concatenate([meta, x], axis=1)
    cos, sin = axial_rope_tables(n_tokens)
    for i in range(DEPTH):
        last = i == DEPTH - 1
        j = i // 2
        hn = rms_norm(h, norm_mix[i])
        if i % 2 == 0:
            h = h + conv_gla_mixer(hn, sc_w_in[j], sc_conv_w[j], gla_w_gate_fwd[j], gla_b_gate_fwd[j],
                                   gla_w_gate_bwd[j], gla_b_gate_bwd[j], gla_norm_w[j], sc_w_out[j])
            if last:
                h = h[:, N_META:]
        else:
            mix = gqa_axial_mixer(hn, att_w_in[j], att_q_norm[j], att_k_norm[j], att_w_out[j], cos, sin,
                                  not last)
            h = (h[:, N_META:] if last else h) + mix
        h = h + hierarchical_moe(rms_norm(h, norm_ffn[i]), moe_w_group[i], moe_b_group[i], moe_w_expert[i],
                                 moe_b_expert[i], moe_w_gate[i], moe_w_up[i], moe_w_down[i])
    return rms_norm(h, norm_final)


_drawn_inputs = setup_inputs


def setup_inputs(seed=0):
    import zlib

    import numpy as np

    out = dict(_drawn_inputs(seed))
    spreads = {}
    factors = {'norm_final': 2.876,
     'att_q_norm': 5.905,
     'att_k_norm': 8.0,
     'moe_b_group': 3.386,
     'moe_b_expert': 4.371}
    for name, (base, spread) in spreads.items():
        noise = np.random.default_rng([zlib.crc32(name.encode()), seed]).standard_normal(out[name].shape)
        drawn = base * np.exp(spread * noise) if base else spread * noise
        out[name] = __import__('jax').numpy.asarray(drawn.astype(out[name].dtype))
    for name, factor in factors.items():
        out[name] = (out[name] * factor).astype(out[name].dtype)
    return out
```

```python
import concourse.bass as bass
from concourse import mybir
from contextlib import ExitStack


def build_program(nc: bass.Bass, A: dict, out: bass.AP):
    f32 = mybir.dt.float32
    u32 = mybir.dt.uint32
    i32 = mybir.dt.int32
    ALU = mybir.AluOpType
    ACT = mybir.ActivationFunctionType
    X = mybir.AxisListType.X

    P = 128
    SEQ, D = A["x"].shape[1], A["x"].shape[2]
    NM = A["meta_tokens"].shape[0]
    T = NM + SEQ
    KC = D // P
    TILE_AT = [0, NM, NM + P]
    TILE_N = [NM, P, P]
    HEADS, DV, DK, C = 4, 128, 64, 64
    RANK = A["gla_w_gate_fwd"].shape[1]
    QH, KVH, HD = 16, 4, 64
    G, EPG, F = 4, 8, 256
    EPS = 1e-6
    TAU = 16.0
    W = 512
    NORM_TILES = [[0, 1, 2], [0, 1, 2], [0, 1, 2], [1, 2], [1, 2]]
    CHUNKS = [(0, 0, NM), (1, 0, C), (1, C, C), (2, 0, C), (2, C, C)]
    MIX0_COLS = [3 * W, 4 * W, 5 * W, 2 * W, W, 0]
    MIX1_COLS = [2 * W, 0, W]
    NMIX = [len(MIX0_COLS) + 2, len(MIX1_COLS) + 2]
    RING = 4
    MOE_SLOT0 = [NMIX[0] % RING, (NMIX[0] + NMIX[1]) % RING]
    MIX1_SLOT0 = MOE_SLOT0[0]
    PRIMED = 1

    ctx = ExitStack()
    with ctx:
        def sb(name, shape, dt=f32):
            return ctx.enter_context(nc.sbuf_tensor(name, shape, dt))

        made = {}

        def sem(name):
            if name not in made:
                made[name] = ctx.enter_context(nc.semaphore(name))
            return made[name]

        h = sb("h", [P, 3, D])
        hn = sb("hn", [P, 3, D])
        hnT = sb("hnT", [P, KC, T])
        gain = sb("gain", [P, D])
        gu_ring = [sb(f"gu_ring{i}", [P, 2 * KC * F]) for i in range(RING)]
        wd_ring = [sb(f"wd_ring{i}", [P, 2, D]) for i in range(RING)]
        consts = sb("consts", [P, A["consts"].shape[1]])
        rope = sb("rope", [P, 2, 3, 32])
        stats = sb("stats", [P, 5, 4, 3])
        scratch = sb("scratch", [P, 15600])
        spent = [0]

        def carve(*shape):
            n = 1
            for s in shape:
                n *= s
            ap = scratch[:, spent[0]:spent[0] + n]
            spent[0] += n
            assert spent[0] <= scratch.shape[1], spent[0]
            if len(shape) == 2:
                return ap.rearrange("p (a b) -> p a b", a=shape[0])
            if len(shape) == 3:
                return ap.rearrange("p (a b c) -> p a b c", a=shape[0], b=shape[1])
            return ap

        ident = consts[:, 0:128]
        fwd_bwd = consts[:, 128:384]
        incl_fwd = consts[:, 128:256]
        strict_bwd = consts[:, 256:384]
        incl_bwd = consts[:, 384:512]
        strict_fwd = consts[:, 512:640]
        before = consts[:, 640:768]
        ones = consts[:, 768:896]
        iota = consts[:, 896:1024]
        valid = consts[:, 1024:1027]

        z = carve(4, T + 2)
        conv = carve(4, T)
        yT = carve(KC, T)
        qT = carve(2, T)
        kT = carve(2, T)
        ktok = carve(3, 256)
        la = carve(3, W)
        decay = carve(4, 5)
        E = carve(4, T)
        Ei = carve(4, T)
        kend = carve(3, W)
        state = carve(8, 2, 128)
        masked = carve(4, 2 * P)
        oss = carve(3, 4, 4)
        la_tmp = E[:, :, :].rearrange("p a b -> p (a b)")
        la_tmp2 = Ei[:, :, :].rearrange("p a b -> p (a b)")
        yb = kend
        v = hn[:, 0:3, 0:W]
        rs = hn[:, 0:3, W:2 * W]
        spent[0] = 0
        qs = carve(2, QH, HD)
        ks = carve(3, KVH, HD)
        ks2 = carve(3, KVH, 2 * HD)
        vs = carve(3, KVH * HD)
        qtmp = carve(2, QH * HD)
        qT1 = carve(8, 2 * P)
        kT1 = carve(KVH, T)
        oT = carve(8, 2 * P)
        probs = carve(4, T)
        pT = carve(2, 4, P)
        pTm = carve(2, 2, P)
        hstat = carve(4, 32)
        spent[0] = 0
        sel = carve(3, P)
        selT = carve(1, T)[:, 0, :]
        xT = carve(KC, P)
        act_g = carve(2, F)
        he = carve(2, F)
        heT = carve(2, 2, P)
        ysum = carve(1, D)[:, 0, :]
        slot_gates = carve(1, EPG)[:, 0, :]
        logits = carve(3, 36)
        padded = carve(3, 8)
        top_g = carve(3, 8)
        top_e = carve(3, 8)
        onehot = carve(3, G)
        expg = carve(3, G)
        esel = carve(3, EPG)
        picked = carve(3, G, EPG)
        gates = carve(3, EPG)
        gtmp = carve(3, EPG)
        key = carve(1, 4)[:, 0, :]
        rstat = carve(12, 4)
        w_g_in = sb("w_g_in", [P, KC, 2 * RANK])
        gT = sb("gT", [2 * RANK + 1, T])
        wgate = sb("wgate", [2 * RANK + 1, W])
        conv_w = sb("conv_w", [P, 3, 4])
        gla_gain = sb("gla_gain", [P, DV])
        qk_gain = sb("qk_gain", [P, 2, HD])
        w_grp = [sb(f"w_grp{l}", [P, KC, G]) for l in range(2)]
        w_exp = [sb(f"w_exp{l}", [P, KC, G * EPG]) for l in range(2)]
        b_route = sb("b_route", [P, 2, 36])
        idx_g = sb("idx_g", [P, 3, 8], u32)
        idx_e = sb("idx_e", [P, 3, 8], u32)
        n_iter = sb("n_iter", [P, 3], i32)
        junk = sb("junk", [P, DV])
        att_max = sb("att_max", [P, 32])
        att_sum = sb("att_sum", [P, 32])
        att_rcp = sb("att_rcp", [P, 32])
        B = [ctx.enter_context(nc.psum_tensor(f"bank{i}", [P, W], f32)) for i in range(8)]

        def chain(eng, name):
            n = [0]

            def link(ins):
                n[0] += 1
                ins.then_inc(sem(name), 1)
                eng.wait_ge(sem(name), n[0])
            return link

        block = ctx.enter_context(nc.Block())

        def upto(n):
            return sum(len(t) for t in NORM_TILES[:n])

        MIX_READ = [[("k_ps", 3), ("v_ps", 3), ("r_ps", 3), ("ax_ps", 4), ("ac_ps", 4), ("ab_ps", 4), ("out0_ps", 3), ("out0_ps", 6)],
                    [("kv_ps", 3), ("q1_ps", 2), ("q1_ps", 4), ("out1_ps", 2), ("out1_ps", 4)]]

        def wait_mix_read(eng, l, b):
            name, count = MIX_READ[l][b]
            eng.wait_ge(sem(name), count)

        @block.sync
        def _(sp):
            sp.dma_start(h[:, 1, :], A["x"][0, 0:P, :]).then_inc(sem("h_in"), 16)
            sp.dma_start(h[:, 2, :], A["x"][0, P:2 * P, :]).then_inc(sem("h_in"), 16)
            sp.dma_start(h[0:NM, 0, :], A["meta_tokens"]).then_inc(sem("h_in"), 16)
            sp.dma_start(consts[:, :], A["consts"]).then_inc(sem("consts_in"), 16)
            sp.dma_start(gain[:, :], A["norm_mix"][0:1, :].broadcast_to([P, D])).then_inc(sem("gain0_in"), 16)

            def mix_block(l, b, slot):
                dst = gu_ring[slot][:, :].rearrange("p (c n) -> p c n", c=KC)
                w_in, w_out = (A["sc_w_in"], A["sc_w_out"]) if l == 0 else (A["att_w_in"], A["att_w_out"])
                cols = MIX0_COLS if l == 0 else MIX1_COLS
                if b < len(cols):
                    src = w_in[0].rearrange("(p c) n -> p c n", c=KC)[:, :, cols[b]:cols[b] + W]
                else:
                    n = b - len(cols)
                    src = w_out[0].rearrange("(c p) n -> p c n", c=KC)[:, :, n * W:(n + 1) * W]
                sp.dma_start(dst, src).then_inc(sem(f"mix_w{slot}"), 16)

            def expert(l, g, e):
                s = (MOE_SLOT0[l] + e) % RING
                gu = gu_ring[s][:, :].rearrange("p (u c n) -> p u c n", u=2, c=KC)
                for u, name in enumerate(("moe_w_gate", "moe_w_up")):
                    src = A[name][l].rearrange("(g e) (p c) n -> g e p c n", g=G, c=KC)[bass.ds(g, 1), e]
                    sp.dma_start(gu[:, u], src.rearrange("g p c n -> p (g c) n")).then_inc(sem(f"gu_w{l}_{e % RING}"), 16)

            def expert_down(l, g, e):
                src = A["moe_w_down"][l].rearrange("(g e) (p c) n -> g e p c n", g=G, c=2)[bass.ds(g, 1), e]
                sp.dma_start(wd_ring[e % RING][:, :, :], src.rearrange("g p c n -> p (g c) n"))\
                  .then_inc(sem(f"wd_w{l}_{e % RING}"), 16)

            for b in range(NMIX[0]):
                if b >= RING:
                    wait_mix_read(sp, 0, b - RING)
                mix_block(0, b, b % RING)

            left0 = None
            for l in range(2):
                if l == 1:
                    for b in range(NMIX[1]):
                        if b < RING:
                            sp.wait_ge(sem("gu_free0"), left0 + 1 + b)
                        else:
                            wait_mix_read(sp, 1, b - RING)
                        mix_block(1, b, (MIX1_SLOT0 + b) % RING)

                def group(g, it, first):
                    for e in range(EPG):
                        if first and e < RING:
                            wait_mix_read(sp, l, NMIX[l] - RING + e)
                        else:
                            sp.wait_ge(sem(f"gu_free{l}"), it * EPG + e - RING + 1)
                        expert(l, g, e)
                        if first and e < RING:
                            if l == 1:
                                sp.wait_ge(sem("wd_free0"), PRIMED + left0 + 1 + e)
                        else:
                            sp.wait_ge(sem(f"wd_free{l}"), PRIMED + it * EPG + e - RING + 1)
                        expert_down(l, g, e)

                group(0, 0, True)
                with sp.Fori(1, G) as g:
                    group(g, g, False)
                sp.wait_ge(sem("n_iter_ready"), l + 1)
                n_next = sp.value_load(n_iter[0:1, l:l + 1], min_val=G, max_val=3 * G)
                with sp.If(n_next > G):
                    with sp.Fori(G, n_next, G) as it0:
                        with sp.Fori(0, G) as g:
                            group(g, it0 + g, False)
                if l == 0:
                    left0 = sp.value_load(n_iter[0:1, 2:3], min_val=G * EPG - RING, max_val=3 * G * EPG - RING)

            for i in range(2):
                sp.wait_ge(sem("hn_ready"), upto(4) + i + 1)
                sp.dma_start(out[0, i * P:(i + 1) * P, :], hn[:, 1 + i, :]).then_inc(sem("out_done"), 16)
            sp.wait_ge(sem("out_done"), 32)

        @block.gpsimd
        def _(pool):
            pool.memset(wgate[:, :], 0.0).then_inc(sem("pool_clear"), 1)
            pool.wait_ge(sem("pool_clear"), 1)
            pool.memset(gT[2 * RANK:2 * RANK + 1, :], 1.0).then_inc(sem("pool_clear"), 1)
            pool.dma_start(w_g_in[:, :, :], A["sc_w_in"][0].rearrange("(p c) n -> p c n", c=KC)[:, :, 6 * W:6 * W + 2 * RANK])\
                .then_inc(sem("w_g_in"), 16)
            pool.dma_start(wgate[0:RANK, 0:256], A["gla_w_gate_fwd"][0]).then_inc(sem("gla_params_in"), 16)
            pool.dma_start(wgate[RANK:2 * RANK, 256:512], A["gla_w_gate_bwd"][0]).then_inc(sem("gla_params_in"), 16)
            pool.dma_start(wgate[2 * RANK:2 * RANK + 1, 0:256], A["gla_b_gate_fwd"]).then_inc(sem("gla_params_in"), 16)
            pool.dma_start(wgate[2 * RANK:2 * RANK + 1, 256:512], A["gla_b_gate_bwd"]).then_inc(sem("gla_params_in"), 16)
            pool.dma_start(gla_gain[:, :], A["gla_norm_w"].broadcast_to([P, DV])).then_inc(sem("gla_params_in"), 16)
            with nc.allow_non_contiguous_dma("1536 single elements, once"):
                for t in range(3):
                    pool.dma_start(conv_w[:, t, :], A["sc_conv_w"][0, t, :].rearrange("(c p) -> p c", p=P)).then_inc(sem("gla_params_in"), 16)
            pool.dma_start(qk_gain[:, 0, :], A["att_q_norm"].broadcast_to([P, HD])).then_inc(sem("att_params_in"), 16)
            pool.dma_start(qk_gain[:, 1, :], A["att_k_norm"].broadcast_to([P, HD])).then_inc(sem("att_params_in"), 16)
            pool.dma_start(rope[:, :, :, :], A["rope"].rearrange("p (a t j) -> p a t j", a=2, t=3)).then_inc(sem("att_params_in"), 16)
            for l in range(2):
                pool.dma_start(w_grp[l][:, :, :], A["moe_w_group"][l].rearrange("(p c) n -> p c n", c=KC)).then_inc(sem(f"route_in{l}"), 16)
                pool.dma_start(w_exp[l][:, :, :], A["moe_w_expert"][l].rearrange("(p c) n -> p c n", c=KC)).then_inc(sem(f"route_in{l}"), 16)
                pool.dma_start(b_route[:, l, 0:G], A["moe_b_group"][l:l + 1, :].broadcast_to([P, G])).then_inc(sem(f"route_in{l}"), 16)
                pool.dma_start(b_route[:, l, G:36], A["moe_b_expert"][l:l + 1, :].broadcast_to([P, 32])).then_inc(sem(f"route_in{l}"), 16)
            for n in range(1, 5):
                src = [None, A["norm_ffn"][0:1, :], A["norm_mix"][1:2, :], A["norm_ffn"][1:2, :],
                       A["norm_final"].rearrange("(a n) -> a n", a=1)][n]
                pool.wait_ge(sem("hn_ready"), upto(n))
                pool.dma_start(gain[:, :], src.broadcast_to([P, D])).then_inc(sem("gain_in"), 16)

        def wait_h(eng, n, i):
            if n == 0:
                eng.wait_ge(sem("h_in"), 48)
            elif n in (1, 3):
                eng.wait_ge(sem(f"h_mixed{n // 2}"), [6, 4][n // 2])
            else:
                eng.wait_ge(sem("h_moe"), n // 2)

        def wait_hnT(eng, n):
            eng.wait_ge(sem("hnT_act"), upto(n + 1))
            eng.wait_ge(sem("hnT_dve"), upto(n + 1))

        @block.scalar
        def _(act):
            link = chain(act, "act_chain")

            def norm(n):
                tiles = NORM_TILES[n]
                for i, t in enumerate(tiles):
                    wait_h(act, n, i)
                    if i == 0:
                        act.wait_ge(sem("clear"), 1)
                    m = TILE_N[t]
                    nc.scalar.activation(hn[0:m, t, :], h[0:m, t, :], ACT.Square,
                                         accum_out=stats[0:m, n, 0, t:t + 1]).then_inc(sem("norm_ss"), 1)
                act.wait_ge(sem("norm_var"), n + 1)
                nc.scalar.activation(stats[:, n, 2, :], stats[:, n, 1, :], ACT.Sqrt).then_inc(sem("norm_std"), 1)

            def transposes_out(n):
                for i, t in enumerate(NORM_TILES[n]):
                    m = TILE_N[t]
                    act.wait_ge(sem("hnT_ps"), 2 * (upto(n) + i) + 1)
                    nc.scalar.activation(hnT[:, 0:4, TILE_AT[t]:TILE_AT[t] + m],
                                         B[0][:, :].rearrange("p (c n) -> p c n", c=4)[:, :, 0:m], ACT.Copy).then_inc(sem("hnT_act"), 1)

            norm(0)
            transposes_out(0)
            act.wait_ge(sem("pool_clear"), 2)
            act.wait_ge(sem("g_ps"), 1)
            nc.scalar.activation(gT[0:2 * RANK, :], B[2][0:2 * RANK, 0:T], ACT.Copy).then_inc(sem("g_ev"), 1)
            for m in range(2):
                act.wait_ge(sem("q_ps"), m + 1)
                nc.scalar.activation(qT[:, m, :], B[3 + m][:, 0:T], ACT.Copy, scale=DK ** -0.5).then_inc(sem("q_ev"), 1)
            for t in range(3):
                n = TILE_N[t]
                act.wait_ge(sem("la_ps"), t + 1)
                if t:
                    act.wait_ge(sem("la_ln"), t)
                link(nc.scalar.activation(la_tmp[0:n, 0:W], B[t][0:n, :], ACT.Abs))
                link(nc.scalar.activation(la_tmp[0:n, 0:W], la_tmp[0:n, 0:W], ACT.Exp, scale=-1.0))
                if t >= 1:
                    act.wait_ge(sem("la_ready"), t)
                nc.scalar.activation(la_tmp2[0:n, 0:W], la_tmp[0:n, 0:W], ACT.Ln, bias=1.0).then_inc(sem("la_ln"), 1)
            for t in range(3):
                n = TILE_N[t]
                act.wait_ge(sem("v_ps"), t + 1)
                nc.scalar.activation(v[0:n, t, :], B[3 + t][0:n, :], ACT.Copy).then_inc(sem("v_ev"), 1)
            for m in range(2):
                act.wait_ge(sem("kT_ps"), m + 1)
                nc.scalar.activation(kT[:, m, :], B[6 + m][:, 0:T], ACT.Copy).then_inc(sem("kT_ev"), 1)
            for t in range(3):
                n = TILE_N[t]
                act.wait_ge(sem("r_ps"), t + 1)
                nc.scalar.activation(rs[0:n, t, :], B[3 + t][0:n, :], ACT.Silu).then_inc(sem("r_ev"), 1)
            for m in range(4):
                act.wait_ge(sem("ax_ps"), m + 1)
                act.wait_ge(sem("clear"), 2)
                nc.scalar.activation(z[:, m, 1:T + 1], B[6 + m % 2][:, 0:T], ACT.Copy).then_inc(sem("ax_ev"), 1)
            for dm in range(4):
                act.wait_ge(sem("cum_ps"), dm + 1)
                act.wait_ge(sem("la_ready"), 3)
                nc.scalar.activation(E[:, dm, :], B[dm][:, 0:T], ACT.Exp).then_inc(sem("E_exp"), 1)
                nc.scalar.activation(Ei[:, dm, :], B[dm][:, 0:T], ACT.Exp, scale=-1.0).then_inc(sem("E_exp"), 1)
            for t in range(3):
                n = TILE_N[t]
                act.wait_ge(sem("kend_ps"), t + 1)
                nc.scalar.activation(kend[0:n, t, :], B[[4, 5, 0][t]][0:n, :], ACT.Exp).then_inc(sem("kend_exp"), 1)
            for i, t in enumerate((1, 2, 0)):
                n = TILE_N[t]
                act.wait_ge(sem("o_ps"), i + 1)
                for hd in range(HEADS):
                    src = B[[6, 0, 6][i] + hd % 2][0:n, (hd // 2) * DV:(hd // 2 + 1) * DV]
                    nc.scalar.activation(junk[0:n, :], src, ACT.Square,
                                         accum_out=oss[0:n, i, 0, hd:hd + 1]).then_inc(sem("o_ss"), 1)
                    act.wait_ge(sem("o_ss"), 4 * i + hd + 1)
                act.wait_ge(sem("o_var"), i + 1)
                nc.scalar.activation(oss[0:n, i, 2, :], oss[0:n, i, 1, :], ACT.Sqrt).then_inc(sem("o_std"), 1)
                act.wait_ge(sem("ybT_ps"), i + 1)
                nc.scalar.activation(yT[:, 4:8, TILE_AT[t]:TILE_AT[t] + n],
                                     B[[6, 0, 6][i]][:, :].rearrange("p (c n) -> p c n", c=4)[:, :, 0:n], ACT.Copy).then_inc(sem("ybT_ev"), 1)

            def moe(l):
                n = 1 + 2 * l
                norm(n)
                transposes_out(n)
                act.wait_ge(sem("gl_shift"), l + 1)
                tiles = NORM_TILES[n]
                a, b = tiles[0], tiles[-1] + 1
                nc.scalar.activation(expg[:, a:b, :], expg[:, a:b, :], ACT.Exp).then_inc(sem("gl_exp"), 1)
                act.wait_ge(sem("top_diff"), l + 1)
                nc.scalar.activation(rstat[:, 4, a:b], rstat[:, 3, a:b], ACT.Exp).then_inc(sem("top_exp"), 1)
                act.wait_ge(sem("n_iter_ready"), l + 1)
                n_it = act.value_load(n_iter[0:1, l:l + 1], min_val=G, max_val=3 * G)
                act.sem_inc(sem(f"heT{l}"), PRIMED)
                act.sem_inc(sem(f"y_act{l}"), PRIMED)
                with act.Fori(0, n_it) as it:
                    act.wait_ge(sem(f"x_ps{l}"), 2 * it + 1)
                    nc.scalar.activation(xT[:, 0:4, :], B[0][:, :].rearrange("p (c n) -> p c n", c=4), ACT.Copy).then_inc(sem(f"x_act{l}"), 1)
                    for e in range(EPG):
                        act.wait_ge(sem(f"gu_ps{l}"), it * EPG + e + 1)
                        if e < 2:
                            act.wait_ge(sem(f"he_ready{l}"), PRIMED + it * EPG)
                        else:
                            act.wait_ge(sem(f"he_ready{l}"), PRIMED + it * EPG + e - 1)
                        nc.scalar.activation(act_g[:, e % 2, :], B[2 + e % 2][:, 0:F], ACT.Silu).then_inc(sem(f"silu{l}"), 1)
                        if e >= 1:
                            heT_out(l, it, e - 1)
                    heT_out(l, it, EPG - 1)
                    act.wait_ge(sem(f"wd_free{l}"), PRIMED + it * EPG + EPG)
                    nc.scalar.activation(ysum[:, 0:W], B[5][:, :], ACT.Copy).then_inc(sem(f"y_act{l}"), 1)

            def heT_out(l, it, e):
                act.wait_ge(sem(f"heT_ps{l}"), it * EPG + e + 1)
                if e >= 2:
                    act.wait_ge(sem(f"wd_free{l}"), PRIMED + it * EPG + e - 1)
                else:
                    act.wait_ge(sem(f"wd_free{l}"), PRIMED + it * EPG)
                nc.scalar.activation(heT[:, e % 2, :, :], B[4][:, 0:2 * P].rearrange("p (c n) -> p c n", c=2), ACT.Copy).then_inc(sem(f"heT{l}"), 1)

            moe(0)

            norm(2)
            transposes_out(2)
            for t in range(3):
                act.wait_ge(sem("kv_ps"), t + 1)
                nc.scalar.activation(ks[:, t, :, :], B[2 + t][:, 0:256].rearrange("p (h d) -> p h d", h=KVH), ACT.Copy).then_inc(sem("kv_raw"), 1)
                nc.scalar.activation(vs[:, t, :], B[2 + t][:, 256:512], ACT.Copy).then_inc(sem("kv_raw"), 1)
            for n in range(2):
                for i in range(2):
                    act.wait_ge(sem("q1_ps"), 2 * n + i + 1)
                    nc.scalar.activation(qs[:, i, 8 * n:8 * n + 8, :], B[[5, 6, 7, 0][2 * n + i]][:, :].rearrange("p (h d) -> p h d", h=8),
                                         ACT.Copy).then_inc(sem("q_raw"), 1)
            act.wait_ge(sem("head_var"), 1)
            nc.scalar.activation(hstat[:, 2, 0:12], hstat[:, 1, 0:12], ACT.Sqrt).then_inc(sem("head_std"), 1)
            act.wait_ge(sem("head_var"), 2)
            nc.scalar.activation(hstat[:, 2, 0:32], hstat[:, 1, 0:32], ACT.Sqrt).then_inc(sem("head_std"), 1)
            for hv in range(KVH):
                act.wait_ge(sem("qk1T_ps"), hv + 1)
                nc.scalar.activation(kT1[:, hv, :], B[[1, 2, 3, 4][hv]][:, 0:T], ACT.Copy).then_inc(sem("qk1T_ev"), 1)
            for i in range(2):
                for m in range(2):
                    act.wait_ge(sem("qk1T_ps"), KVH + 2 * i + m + 1)
                    nc.scalar.activation(qT1[:, 4 * m:4 * m + 4, i * P:(i + 1) * P],
                                         B[[5, 6, 7, 0][2 * i + m]][:, :].rearrange("p (c n) -> p c n", c=4), ACT.Copy).then_inc(sem("qk1T_ev"), 1)
            def exps(u):
                for o in range(2):
                    act.wait_ge(sem("s_max"), 2 * u + o + 1)
                    if u >= 2:
                        act.wait_ge(sem("pT_ps"), u - 1)
                    nc.scalar.activation(probs[:, 2 * (u % 2) + o, :], B[2 * (u % 2) + o][:, 0:T], ACT.Exp,
                                         bias=att_max[:, 2 * u + o:2 * u + o + 1],
                                         accum_out=att_sum[:, 2 * u + o:2 * u + o + 1]).then_inc(sem("p_exp"), 1)

            def pT_out(u):
                act.wait_ge(sem("pT_ps"), u + 1)
                if u >= 2:
                    act.wait_ge(sem("oT_ps"), u - 1)
                nc.scalar.activation(pT[:, u % 2, :, :], B[4 + u % 2][:, :].rearrange("p (c n) -> p c n", c=4), ACT.Copy).then_inc(sem("pT_ev"), 1)

            exps(0)
            for u in range(16):
                if u < 15:
                    exps(u + 1)
                pT_out(u)
            moe(1)
            norm(4)

        @block.vector
        def _(dve):
            link = chain(dve, "dve_chain")

            def norm(n):
                tiles = NORM_TILES[n]
                dve.wait_ge(sem("norm_ss"), upto(n + 1))
                nc.vector.tensor_scalar(stats[:, n, 1, :], stats[:, n, 0, :], 1.0 / D, EPS, ALU.mult, ALU.add).then_inc(sem("norm_var"), 1)
                dve.wait_ge(sem("norm_std"), n + 1)
                link(nc.vector.reciprocal(stats[:, n, 3, :], stats[:, n, 2, :]))
                if n:
                    dve.wait_ge(sem("gain_in"), 16 * n)
                else:
                    dve.wait_ge(sem("gain0_in"), 16)
                for t in tiles:
                    m = TILE_N[t]
                    nc.vector.scalar_tensor_tensor(hn[0:m, t, :], h[0:m, t, :], stats[0:m, n, 3, t:t + 1], gain[0:m, :],
                                                   ALU.mult, ALU.mult).then_inc(sem("hn_ready"), 1)

            def transposes_out(n):
                for i, t in enumerate(NORM_TILES[n]):
                    m = TILE_N[t]
                    dve.wait_ge(sem("hnT_ps"), 2 * (upto(n) + i) + 2)
                    nc.vector.tensor_copy(hnT[:, 4:8, TILE_AT[t]:TILE_AT[t] + m],
                                          B[1][:, :].rearrange("p (c n) -> p c n", c=4)[:, :, 0:m]).then_inc(sem("hnT_dve"), 1)

            nc.vector.memset(stats[:, :, :, :].rearrange("p a b c -> p (a b c)"), 1.0).then_inc(sem("clear"), 1)

            nc.vector.memset(z[:, :, :].rearrange("p a b -> p (a b)"), 0.0).then_inc(sem("clear"), 1)
            norm(0)
            transposes_out(0)
            for t in range(3):
                n = TILE_N[t]
                dve.wait_ge(sem("k_ps"), t + 1)
                nc.vector.tensor_copy(ktok[0:n, t, :], B[5 + t][0:n, 0:256]).then_inc(sem("k_ev"), 1)
            for t in range(3):
                n = TILE_N[t]
                dve.wait_ge(sem("la_ln"), t + 1)
                link(nc.vector.tensor_scalar(la[0:n, t, :], B[t][0:n, :], 0.0, 1.0 / TAU, ALU.min, ALU.mult))
                nc.vector.scalar_tensor_tensor(la[0:n, t, :], la_tmp2[0:n, 0:W], -1.0 / TAU, la[0:n, t, :], ALU.mult, ALU.add).then_inc(sem("la_ready"), 1)
            dve.wait_ge(sem("gla_params_in"), 128)
            for t in range(3):
                n = TILE_N[t]
                dve.wait_ge(sem("r_ev"), t + 1)
                r4 = rs[0:n, t, :].rearrange("p (h d) -> p h d", h=HEADS)
                nc.vector.tensor_tensor(r4, r4, gla_gain[0:n, :].unsqueeze(1).to_broadcast([n, HEADS, DV]), ALU.mult).then_inc(sem("rs_ready"), 1)
            dve.wait_ge(sem("E_exp"), 8)
            link(nc.vector.tensor_copy(decay[:, 0:2, 0:1], E[:, 0:2, NM - 1:NM]))
            link(nc.vector.tensor_copy(decay[:, 0:2, 1:5], E[:, 0:2, NM + C - 1:T:C]))
            link(nc.vector.tensor_copy(decay[:, 2:4, 0:1], E[:, 2:4, 0:1]))
            link(nc.vector.tensor_copy(decay[:, 2:4, 1:5], E[:, 2:4, NM:T:C]))
            dve.wait_ge(sem("q_ev"), 2)
            dve.wait_ge(sem("kT_ev"), 2)
            for d in range(2):
                nc.vector.tensor_tensor(E[:, 2 * d:2 * d + 2, :], E[:, 2 * d:2 * d + 2, :], qT[:, :, :], ALU.mult).then_inc(sem("qk_dec"), 1)
                nc.vector.tensor_tensor(Ei[:, 2 * d:2 * d + 2, :], Ei[:, 2 * d:2 * d + 2, :], kT[:, :, :], ALU.mult).then_inc(sem("qk_dec"), 1)
            for t in range(3):
                n = TILE_N[t]
                dve.wait_ge(sem("kend_exp"), t + 1)
                for d in range(2):
                    ke = kend[0:n, t, 256 * d:256 * d + 256]
                    nc.vector.tensor_tensor(ke, ke, ktok[0:n, t, :], ALU.mult).then_inc(sem("kend"), 1)
            for m in range(4):
                dve.wait_ge(sem("ac_ps"), m + 1)
                dve.wait_ge(sem("ax_ev"), m + 1)
                zz = z[:, m, 1:T + 1]
                nc.vector.tensor_tensor(zz, B[6 + m % 2][:, 0:T], zz, ALU.mult).then_inc(sem("z_ready"), 1)
            dve.wait_ge(sem("z_ready"), 4)
            dve.wait_ge(sem("gla_params_in"), 128)
            for tap in range(3):
                for m in range(4):
                    src = z[:, m, tap:tap + T]
                    if tap == 0:
                        last = nc.vector.tensor_scalar(conv[:, m, :], src, conv_w[:, 0, m:m + 1], None, ALU.mult)
                    else:
                        last = nc.vector.scalar_tensor_tensor(conv[:, m, :], src, conv_w[:, tap, m:m + 1], conv[:, m, :],
                                                       ALU.mult, ALU.add)
                link(last)
            for m in range(4):
                dve.wait_ge(sem("ab_ps"), m + 1)
                nc.vector.tensor_tensor(yT[:, m, :], B[6 + m % 2][:, 0:T], conv[:, m, :], ALU.mult).then_inc(sem("ya_ready"), 1)
            for k in range(8):
                d, i = k % 2, k // 2
                j = i if d == 0 else 4 - i
                dve.wait_ge(sem("kvs_ps"), k + 1)
                if i:
                    dve.wait_ge(sem("state"), 4 * (k - 1))
                for m in range(2):
                    for hh in range(2):
                        rows = slice(64 * hh, 64 * hh + 64)
                        got = B[[1, 2, 3, 4, 5, 0, 1, 2][k]][rows, 256 * m + DV * hh:256 * m + DV * hh + DV]
                        new = state[rows, 4 * d + i, m, :]
                        if i == 0:
                            nc.vector.tensor_copy(new, got).then_inc(sem("state"), 1)
                        else:
                            nc.vector.scalar_tensor_tensor(new, state[rows, 4 * d + i - 1, m, :], decay[rows, 2 * d + m, j:j + 1], got,
                                                           ALU.mult, ALU.add).then_inc(sem("state"), 1)
            def mask_scores(i, t):
                n = TILE_N[t]
                for hd in range(HEADS):
                    dve.wait_ge(sem("sc_ps"), 4 * i + hd + 1)
                    if i:
                        dve.wait_ge(sem("o_ps"), i)
                    nc.vector.tensor_tensor(masked[0:n, hd, :].rearrange("p (d c) -> p d c", d=2)[:, :, 0:n],
                                            B[2 + hd][0:n, 0:256].rearrange("p (d c) -> p d c", d=2)[:, :, 0:n],
                                            fwd_bwd[0:n, :].rearrange("p (d c) -> p d c", d=2)[:, :, 0:n], ALU.mult).then_inc(sem("masked"), 1)

            def head_norm(i, t):
                n = TILE_N[t]
                dve.wait_ge(sem("o_ss"), 4 * i + 4)
                nc.vector.tensor_scalar(oss[0:n, i, 1, :], oss[0:n, i, 0, :], 1.0 / DV, EPS, ALU.mult, ALU.add).then_inc(sem("o_var"), 1)
                dve.wait_ge(sem("o_std"), i + 1)
                link(nc.vector.reciprocal(oss[0:n, i, 3, :], oss[0:n, i, 2, :]))
                dve.wait_ge(sem("rs_ready"), 3)
                for hd in range(HEADS):
                    src = B[[6, 0, 6][i] + hd % 2][0:n, (hd // 2) * DV:(hd // 2 + 1) * DV]
                    nc.vector.scalar_tensor_tensor(yb[0:n, t, hd * DV:(hd + 1) * DV], src, oss[0:n, i, 3, hd:hd + 1],
                                                   rs[0:n, t, hd * DV:(hd + 1) * DV], ALU.mult, ALU.mult).then_inc(sem("yb_ready"), 1)
            mask_scores(0, 1)
            head_norm(0, 1)
            mask_scores(1, 2)
            head_norm(1, 2)
            mask_scores(2, 0)
            head_norm(2, 0)
            for half in range(2):
                for t in range(3):
                    n = TILE_N[t]
                    k = 3 * half + t
                    dve.wait_ge(sem("out0_ps"), k + 1)
                    hh = h[0:n, t, half * W:(half + 1) * W]
                    nc.vector.tensor_tensor(hh, B[[2, 3, 4, 5, 0, 1][k]][0:n, :], hh, ALU.add).then_inc(sem("h_mixed0"), 1)

            def moe(l):
                n = 1 + 2 * l
                tiles = NORM_TILES[n]
                a, b = tiles[0], tiles[-1] + 1
                NT = b - a
                norm(n)
                transposes_out(n)
                dve.wait_ge(sem(f"route_in{l}"), 64)
                link(nc.vector.memset(padded[:, :, :].rearrange("p a b -> p (a b)"), -3.0e38))
                dve.wait_ge(sem("logits_ps"), l + 1)
                link(nc.vector.tensor_tensor(logits[:, a:b, :], B[6][:, 0:108].rearrange("p (t n) -> p t n", t=3)[:, a:b, :],
                                             b_route[:, l, :].unsqueeze(1).to_broadcast([P, NT, 36]), ALU.add))
                link(nc.vector.tensor_copy(padded[:, a:b, 0:G], logits[:, a:b, 0:G]))
                for t in tiles:
                    link(nc.vector.max(top_g[:, t, :], padded[:, t, :]))
                nc.vector.tensor_tensor(expg[:, a:b, :], logits[:, a:b, 0:G], top_g[:, a:b, 0:1].to_broadcast([P, NT, G]),
                                        ALU.subtract).then_inc(sem("gl_shift"), 1)
                for t in tiles:
                    link(nc.vector.max_index(idx_g[:, t, :], top_g[:, t, :], padded[:, t, :]))
                gidx = rstat[:, 0, a:b]
                link(nc.vector.tensor_copy(gidx.unsqueeze(2), idx_g[:, a:b, 0:1]))
                link(nc.vector.tensor_tensor(onehot[:, a:b, :], iota[:, 0:G].unsqueeze(1).to_broadcast([P, NT, G]),
                                             gidx.unsqueeze(2).to_broadcast([P, NT, G]), ALU.is_equal))
                nc.vector.tensor_tensor(onehot[:, a:b, :], onehot[:, a:b, :], valid[:, a:b].unsqueeze(2).to_broadcast([P, NT, G]),
                                        ALU.mult).then_inc(sem("onehot"), 1)
                dve.wait_ge(sem("onehot"), l + 1)
                link(nc.vector.tensor_tensor(picked[:, a:b, :, :], logits[:, a:b, G:36].rearrange("p t (g e) -> p t g e", g=G),
                                             onehot[:, a:b, :].unsqueeze(3).to_broadcast([P, NT, G, EPG]), ALU.mult))
                link(nc.vector.tensor_reduce(esel[:, a:b, :], picked[:, a:b, :, :].rearrange("p t g e -> p t e g"), X, ALU.add))
                for t in tiles:
                    link(nc.vector.max(top_e[:, t, :], esel[:, t, :]))
                nc.vector.tensor_tensor(rstat[:, 3, a:b].unsqueeze(2), top_e[:, a:b, 1:2], top_e[:, a:b, 0:1],
                                        ALU.subtract).then_inc(sem("top_diff"), 1)
                for t in tiles:
                    link(nc.vector.max_index(idx_e[:, t, :], top_e[:, t, :], esel[:, t, :]))
                link(nc.vector.tensor_copy(rstat[:, 1:3, a:b], idx_e[:, a:b, 0:2].rearrange("p t k -> p k t")))
                dve.wait_ge(sem("gl_exp"), l + 1)
                link(nc.vector.tensor_reduce(rstat[:, 5, a:b], expg[:, a:b, :], X, ALU.add))
                link(nc.vector.reciprocal(rstat[:, 5, a:b], rstat[:, 5, a:b]))
                dve.wait_ge(sem("top_exp"), l + 1)
                link(nc.vector.tensor_scalar(rstat[:, 6, a:b], rstat[:, 4, a:b], 1.0, None, ALU.add))
                link(nc.vector.reciprocal(rstat[:, 6, a:b], rstat[:, 6, a:b]))
                link(nc.vector.tensor_tensor(rstat[:, 6, a:b], rstat[:, 6, a:b], rstat[:, 5, a:b], ALU.mult))
                link(nc.vector.tensor_tensor(rstat[:, 7, a:b], rstat[:, 6, a:b], rstat[:, 4, a:b], ALU.mult))
                iota8 = iota[:, 0:EPG].unsqueeze(1).to_broadcast([P, NT, EPG])
                for k, dst in ((0, gates), (1, gtmp)):
                    link(nc.vector.tensor_tensor(dst[:, a:b, :], iota8, rstat[:, 1 + k, a:b].unsqueeze(2).to_broadcast([P, NT, EPG]), ALU.is_equal))
                    link(nc.vector.tensor_tensor(dst[:, a:b, :], dst[:, a:b, :], rstat[:, 6 + k, a:b].unsqueeze(2).to_broadcast([P, NT, EPG]), ALU.mult))
                nc.vector.tensor_tensor(gates[:, a:b, :], gates[:, a:b, :], gtmp[:, a:b, :], ALU.add).then_inc(sem("gates"), 1)
                dve.wait_ge(sem("rank_ps"), l + 1)
                link(nc.vector.tensor_tensor(expg[:, a:b, :], B[7][:, 0:12].rearrange("p (t g) -> p t g", t=3)[:, a:b, :], onehot[:, a:b, :], ALU.mult))
                link(nc.vector.tensor_reduce(rstat[:, 8, a:b], expg[:, a:b, :], X, ALU.add))
                link(nc.vector.tensor_reduce(rstat[:, 9, 0:1], B[7][:, 16:20], X, ALU.max))
                link(nc.vector.tensor_scalar(rstat[:, 9, 1:2], rstat[:, 9, 0:1], float(P), float(G), ALU.is_gt, ALU.mult))
                link(nc.vector.tensor_scalar(rstat[:, 9, 2:3], rstat[:, 9, 0:1], float(2 * P), float(G), ALU.is_gt, ALU.mult))
                link(nc.vector.tensor_tensor(rstat[:, 9, 1:2], rstat[:, 9, 1:2], rstat[:, 9, 2:3], ALU.add))
                if l == 0:
                    link(nc.vector.tensor_scalar(n_iter[:, 2:3], rstat[:, 9, 1:2], float(EPG), float(G * EPG - RING), ALU.mult, ALU.add))
                nc.vector.tensor_scalar(n_iter[:, l:l + 1], rstat[:, 9, 1:2], float(G), None, ALU.add).then_inc(sem("n_iter_ready"), 1)
                link(nc.vector.tensor_scalar(rstat[:, 10, a:b], rstat[:, 8, a:b], float(P), float((G - 1) * P), ALU.is_ge, ALU.mult))
                link(nc.vector.tensor_scalar(rstat[:, 11, a:b], rstat[:, 8, a:b], float(2 * P), float((G - 1) * P), ALU.is_ge, ALU.mult))
                link(nc.vector.tensor_tensor(rstat[:, 10, a:b], rstat[:, 10, a:b], rstat[:, 11, a:b], ALU.add))
                link(nc.vector.tensor_tensor(rstat[:, 10, a:b], rstat[:, 10, a:b], rstat[:, 8, a:b], ALU.add))
                link(nc.vector.scalar_tensor_tensor(key[:, a:b], gidx, float(P), rstat[:, 10, a:b], ALU.mult, ALU.add))
                link(nc.vector.scalar_tensor_tensor(key[:, a:b], key[:, a:b], 1.0, valid[:, a:b], ALU.add, ALU.mult))
                nc.vector.tensor_scalar(key[:, a:b], key[:, a:b], -1.0, None, ALU.add).then_inc(sem(f"key{l}"), 1)
                dve.wait_ge(sem("n_iter_ready"), l + 1)
                n_it = dve.value_load(n_iter[0:1, l:l + 1], min_val=G, max_val=3 * G)
                nadd = 2 * NT
                for name in ("he_ready", "h_added", "y_dve", "selT"):
                    dve.sem_inc(sem(f"{name}{l}"), PRIMED)
                with dve.Fori(0, n_it) as it:
                    dve.wait_ge(sem(f"key{l}"), it + 1)
                    nc.vector.tensor_tensor(sel[:, a:b, :], iota.unsqueeze(1).to_broadcast([P, NT, P]),
                                            key[:, a:b].unsqueeze(2).to_broadcast([P, NT, P]), ALU.is_equal).then_inc(sem(f"sel{l}"), 1)
                    dve.wait_ge(sem(f"sel{l}"), it + 1)
                    nc.vector.tensor_scalar(key[:, a:b], key[:, a:b], -float(P), None, ALU.add).then_inc(sem(f"key{l}"), 1)
                    dve.wait_ge(sem(f"x_ps{l}"), 2 * it + 2)
                    nc.vector.tensor_copy(xT[:, 4:8, :], B[1][:, :].rearrange("p (c n) -> p c n", c=4)).then_inc(sem(f"x_dve{l}"), 1)
                    dve.wait_ge(sem(f"sg_ps{l}"), it + 1)
                    nc.vector.tensor_copy(slot_gates[:, :], B[7][:, 0:EPG]).then_inc(sem(f"slot_gates{l}"), 1)
                    nc.vector.tensor_copy(selT[:, TILE_AT[a]:T], B[7][:, 64 + TILE_AT[a]:64 + T]).then_inc(sem(f"selT{l}"), 1)
                    dve.wait_ge(sem(f"slot_gates{l}"), it + 1)
                    for e in range(EPG):
                        dve.wait_ge(sem(f"silu{l}"), it * EPG + e + 1)
                        if e >= 2:
                            dve.wait_ge(sem(f"heT_ps{l}"), it * EPG + e - 1)
                        nc.vector.scalar_tensor_tensor(he[:, e % 2, :], act_g[:, e % 2, :], slot_gates[:, e:e + 1], B[2 + e % 2][:, F:2 * F],
                                                       ALU.mult, ALU.mult).then_inc(sem(f"he_ready{l}"), 1)
                    dve.wait_ge(sem(f"wd_free{l}"), PRIMED + it * EPG + EPG)
                    nc.vector.tensor_copy(ysum[:, W:D], B[6][:, :]).then_inc(sem(f"y_dve{l}"), 1)
                    for k in range(nadd):
                        half, t = k // NT, tiles[k % NT]
                        n = TILE_N[t]
                        dve.wait_ge(sem(f"sc_ps{l}"), it * nadd + k + 1)
                        if k == 0:
                            dve.wait_ge(sem(f"h_added{l}"), PRIMED + it * nadd)
                        hh = h[0:n, t, half * W:(half + 1) * W]
                        nc.vector.tensor_tensor(hh, B[k % 2][0:n, :], hh, ALU.add).then_inc(sem(f"h_added{l}"), 1)
                dve.wait_ge(sem(f"h_added{l}"), PRIMED + n_it * nadd)
                dve.sem_inc(sem("h_moe"), 1)

            moe(0)

            norm(2)
            transposes_out(2)
            dve.wait_ge(sem("att_params_in"), 48)
            dve.wait_ge(sem("att_params_in"), 48)

            def head_rms(src, sq, nh, nth, scale, gn):
                nt = src.shape[1]
                flat = src.rearrange("p t h d -> p (t h) d")
                nht = nt * nh
                link(nc.vector.tensor_tensor(sq[:, 0:nht, :], flat, flat, ALU.mult))
                link(nc.vector.tensor_reduce(hstat[:, 0, 0:nht], sq[:, 0:nht, :], X, ALU.add))
                nc.vector.tensor_scalar(hstat[:, 1, 0:nht], hstat[:, 0, 0:nht], 1.0 / HD, EPS, ALU.mult, ALU.add).then_inc(sem("head_var"), 1)
                dve.wait_ge(sem("head_std"), nth)
                link(nc.vector.reciprocal(hstat[:, 3, 0:nht], hstat[:, 2, 0:nht]))
                link(nc.vector.tensor_tensor(flat, flat, hstat[:, 3, 0:nht].unsqueeze(2).to_broadcast([P, nht, HD]), ALU.mult))
                link(nc.vector.scalar_tensor_tensor(flat, flat, scale, gn.unsqueeze(1).to_broadcast([P, nht, HD]), ALU.mult, ALU.mult))

            def rotate(x, dst, t, nh, ta, tb, name):
                x0, x1 = x[:, :, 0:HD:2], x[:, :, 1:HD:2]
                c = rope[:, 0, t, :].unsqueeze(1).to_broadcast([P, nh, 32])
                s = rope[:, 1, t, :].unsqueeze(1).to_broadcast([P, nh, 32])
                nc.vector.tensor_tensor(ta[:, 0:nh, 0:32], x0, c, ALU.mult)
                nc.vector.tensor_tensor(ta[:, 0:nh, 32:64], x1, s, ALU.mult)
                nc.vector.tensor_tensor(tb[:, 0:nh, 0:32], x0, s, ALU.mult)
                link(nc.vector.tensor_tensor(tb[:, 0:nh, 32:64], x1, c, ALU.mult))
                nc.vector.tensor_tensor(dst[:, :, 0:HD:2], ta[:, 0:nh, 0:32], ta[:, 0:nh, 32:64], ALU.subtract)
                link(nc.vector.tensor_tensor(dst[:, :, 1:HD:2], tb[:, 0:nh, 0:32], tb[:, 0:nh, 32:64], ALU.add))

            sq = qtmp[:, :, :].rearrange("p i (h d) -> p (i h) d", d=HD)
            dve.wait_ge(sem("kv_raw"), 6)
            head_rms(ks[:, :, :, :], sq, KVH, 1, 1.0, qk_gain[:, 1, :])
            for t in range(3):
                rotate(ks[:, t, :, :], ks2[:, t, :, 0:HD], t, KVH, sq[:, 0:16, :], sq[:, 16:32, :], "k")
                nc.vector.tensor_copy(ks2[:, t, :, HD:2 * HD], ks2[:, t, :, 0:HD]).then_inc(sem("k_rot"), 1)
            dve.wait_ge(sem("q_raw"), 4)
            head_rms(qs[:, :, :, :], sq, QH, 2, HD ** -0.5, qk_gain[:, 0, :])
            for i in range(2):
                rotate(qs[:, i, :, :], qs[:, i, :, :], 1 + i, QH, sq[:, 0:16, :], sq[:, 16:32, :], "q")
                dve.sem_inc(sem("q_rot"), 1)

            def maxima(u):
                for o in range(2):
                    dve.wait_ge(sem("s_ps"), 2 * u + o + 1)
                    nc.vector.tensor_reduce(att_max[:, 2 * u + o:2 * u + o + 1], B[2 * (u % 2) + o][:, 0:T], X, ALU.max, negate=True).then_inc(sem("s_max"), 1)

            def normalise(u):
                dve.wait_ge(sem("p_exp"), 2 * u + 2)
                link(nc.vector.reciprocal(att_rcp[:, 2 * u:2 * u + 2], att_sum[:, 2 * u:2 * u + 2]))
                for o in range(2):
                    pr = probs[:, 2 * (u % 2) + o, :]
                    nc.vector.tensor_scalar(pr, pr, att_rcp[:, 2 * u + o:2 * u + o + 1], None, ALU.mult).then_inc(sem("p_ready"), 1)

            def out_of_psum(u):
                dve.wait_ge(sem("pT_ps"), u + 1)
                if u >= 2:
                    dve.wait_ge(sem("oT_ps"), u - 1)
                nc.vector.tensor_copy(pTm[0:NM, u % 2, :, :], B[6][0:NM, 0:2 * P].rearrange("p (o n) -> p o n", o=2)).then_inc(sem("pTm_ev"), 1)

            def oT_out(u):
                i, pair = u // 8, u % 8
                dve.wait_ge(sem("oT_ps"), u + 1)
                nc.vector.tensor_copy(oT[:, pair, i * P:(i + 1) * P], B[7][:, 0:P]).then_inc(sem("oT_ev"), 1)

            maxima(0)
            for u in range(16):
                if u < 15:
                    maxima(u + 1)
                normalise(u)
                out_of_psum(u)
                if u:
                    oT_out(u - 1)
            oT_out(15)
            for half in range(2):
                for i in range(2):
                    k = 2 * half + i
                    dve.wait_ge(sem("out1_ps"), k + 1)
                    hh = h[:, 1 + i, half * W:(half + 1) * W]
                    nc.vector.tensor_tensor(hh, B[k][:, :], hh, ALU.add).then_inc(sem("h_mixed1"), 1)
            moe(1)
            norm(4)

        @block.tensor
        def _(pe):
            mm = nc.tensor.matmul

            def transposes(n):
                for i, t in enumerate(NORM_TILES[n]):
                    m = TILE_N[t]
                    pe.wait_ge(sem("hn_ready"), upto(n) + i + 1)
                    if i == 0:
                        pe.wait_ge(sem("consts_in"), 16)
                    for half in range(2):
                        if i:
                            pe.wait_ge(sem(f"hnT_{('act', 'dve')[half]}"), upto(n) + i)
                        for c in range(4):
                            last = nc.tensor.transpose(B[half][:, c * P:c * P + m], hn[0:m, t, 4 * half + c:D:KC], ident[0:m, 0:m])
                        last.then_inc(sem("hnT_ps"), 1)

            def block_ready(l, b):
                s = (b if l == 0 else MIX1_SLOT0 + b) % RING
                before_it = [x % RING for x in range(NMIX[0])] if l else []
                use = (before_it + [((MIX1_SLOT0 if l else 0) + x) % RING for x in range(b + 1)]).count(s)
                pe.wait_ge(sem(f"mix_w{s}"), 16 * use)
                return gu_ring[s][:, :].rearrange("p (c n) -> p c n", c=KC)

            transposes(0)
            wait_hnT(pe, 0)
            pe.wait_ge(sem("w_g_in"), 16)
            for c in range(KC):
                last = mm(B[2][0:2 * RANK, 0:T], w_g_in[:, c, :], hnT[:, c, :], start=(c == 0), stop=(c == KC - 1))
            last.then_inc(sem("g_ps"), 1)

            def feature_major(w, m, bank, name):
                for c in range(KC):
                    last = mm(bank[:, 0:T], w[:, c, m * P:(m + 1) * P], hnT[:, c, :], start=(c == 0), stop=(c == KC - 1))
                last.then_inc(sem(name), 1)
                return last

            def token_major(w, t, lo, hi, bank, name, rows=None):
                n = rows or TILE_N[t]
                for c in range(KC):
                    last = mm(bank[0:n, 0:hi - lo], hnT[:, c, TILE_AT[t]:TILE_AT[t] + n], w[:, c, lo:hi], start=(c == 0), stop=(c == KC - 1))
                last.then_inc(sem(name), 1)
                return last

            w = block_ready(0, 0)
            for m in range(2):
                feature_major(w, m, B[3 + m], "q_ps")
            for t in range(3):
                token_major(w, t, 256, 512, B[5 + t], "k_ps")
            pe.wait_ge(sem("g_ev"), 1)
            pe.wait_ge(sem("gla_params_in"), 128)
            for t in range(3):
                n = TILE_N[t]
                mm(B[t][0:n, :], gT[:, TILE_AT[t]:TILE_AT[t] + n], wgate[:, :], start=True, stop=True).then_inc(sem("la_ps"), 1)
            w = block_ready(0, 1)
            for t in range(3):
                pe.wait_ge(sem("q_ev"), t + 1) if t < 2 else pe.wait_ge(sem("k_ev"), 1)
                token_major(w, t, 0, W, B[3 + t], "v_ps")
            pe.wait_ge(sem("k_ev"), 3)
            for m in range(2):
                for t in range(3):
                    n = TILE_N[t]
                    last = nc.tensor.transpose(B[6 + m][:, TILE_AT[t]:TILE_AT[t] + n], ktok[0:n, t, m * P:(m + 1) * P], ident[0:n, 0:n])
                last.then_inc(sem("kT_ps"), 1)
            w = block_ready(0, 2)
            for t in range(3):
                pe.wait_ge(sem("v_ev"), t + 1)
                token_major(w, t, 0, W, B[3 + t], "r_ps")
            w = block_ready(0, 3)
            for m in range(4):
                pe.wait_ge(sem("kT_ev"), m + 1) if m < 2 else pe.wait_ge(sem("ax_ev"), m - 1)
                feature_major(w, m, B[6 + m % 2], "ax_ps")
            pe.wait_ge(sem("la_ready"), 3)
            for dm in range(4):
                if dm == 3:
                    pe.wait_ge(sem("r_ev"), 1)
                for t in range(3):
                    n = TILE_N[t]
                    last = mm(B[dm][:, TILE_AT[t]:TILE_AT[t] + n], la[0:n, t, dm * P:(dm + 1) * P],
                              (incl_fwd, incl_bwd)[dm // 2][0:n, 0:n], start=True, stop=True)
                last.then_inc(sem("cum_ps"), 1)
            for t in range(3):
                n = TILE_N[t]
                bank = B[[4, 5, 0][t]]
                pe.wait_ge(sem("r_ev"), t + 2) if t < 2 else pe.wait_ge(sem("E_exp"), 2)
                mm(bank[0:n, 0:256], strict_bwd[0:n, 0:n], la[0:n, t, 0:256], start=True, stop=True)
                mm(bank[0:n, 256:512], strict_fwd[0:n, 0:n], la[0:n, t, 256:512], start=True, stop=True).then_inc(sem("kend_ps"), 1)
            w = block_ready(0, 4)
            for m in range(4):
                pe.wait_ge(sem("ax_ev"), m + 3) if m < 2 else pe.wait_ge(sem("z_ready"), m - 1)
                feature_major(w, m, B[6 + m % 2], "ac_ps")
            w = block_ready(0, 5)
            for m in range(4):
                pe.wait_ge(sem("z_ready"), m + 3) if m < 2 else pe.wait_ge(sem("ya_ready"), m - 1)
                feature_major(w, m, B[6 + m % 2], "ab_ps")
            pe.wait_ge(sem("kend"), 6)
            pe.wait_ge(sem("E_exp"), 8)
            pe.wait_ge(sem("v_ev"), 3)
            for k in range(8):
                d, i = k % 2, k // 2
                t, p0, n = CHUNKS[i if d == 0 else 4 - i]
                if k >= 6:
                    pe.wait_ge(sem("state"), 4 * (k - 5))
                bank = B[[1, 2, 3, 4, 5, 0, 1, 2][k]]
                for m in range(2):
                    last = mm(bank[:, 256 * m:256 * m + 256], kend[p0:p0 + n, t, 256 * d + P * m:256 * d + P * (m + 1)],
                              v[p0:p0 + n, t, 256 * m:256 * m + 256], start=True, stop=True)
                last.then_inc(sem("kvs_ps"), 1)
            pe.wait_ge(sem("state"), 32)
            pe.wait_ge(sem("qk_dec"), 4)

            def scores(i, t):
                n = TILE_N[t]
                at = TILE_AT[t]
                for hd in range(HEADS):
                    m, rows = hd // 2, slice(64 * (hd % 2), 64 * (hd % 2) + 64)
                    if i:
                        pe.wait_ge(sem("masked"), 4 * (i - 1) + hd + 1)
                    for d in range(2):
                        last = mm(B[2 + hd][0:n, d * P:d * P + n], Ei[rows, 2 * d + m, at:at + n], E[rows, 2 * d + m, at:at + n], start=True, stop=True)
                    last.then_inc(sem("sc_ps"), 1)

            def outputs(i, t):
                n = TILE_N[t]
                at = TILE_AT[t]
                base = [6, 0, 6][i]
                if i == 0:
                    pe.wait_ge(sem("ya_ready"), 4)
                if i == 2:
                    pe.wait_ge(sem("ybT_ev"), 1)
                for hd in range(HEADS):
                    m, hh = hd // 2, hd % 2
                    o = B[base + hh]
                    pe.wait_ge(sem("masked"), 4 * i + hd + 1)
                    for d in range(2):
                        mm(o[0:n, m * DV:(m + 1) * DV], masked[0:n, hd, d * P:d * P + n], v[0:n, t, hd * DV:(hd + 1) * DV],
                           start=(m == 0 and d == 0), stop=False, skip_group_check=True)
                for hd in range(HEADS):
                    m, hh = hd // 2, hd % 2
                    o = B[base + hh]
                    rows = slice(64 * hh, 64 * hh + 64)
                    for j, (tt, p0, cn) in enumerate(CHUNKS):
                        if tt != t:
                            continue
                        for d, prev in ((0, j - 1), (1, 3 - j)):
                            if 0 <= prev <= 3:
                                last = mm(o[p0:p0 + cn, m * DV:(m + 1) * DV], E[rows, 2 * d + m, at + p0:at + p0 + cn],
                                          state[rows, 4 * d + prev, m, :], start=False, stop=True, skip_group_check=True)
                last.then_inc(sem("o_ps"), 1)

            def yb_transposes(i, t):
                n = TILE_N[t]
                pe.wait_ge(sem("yb_ready"), 4 * i + 4)
                for hd in range(HEADS):
                    last = nc.tensor.transpose(B[[6, 0, 6][i]][:, hd * P:hd * P + n], yb[0:n, t, hd * P:(hd + 1) * P], ident[0:n, 0:n])
                last.then_inc(sem("ybT_ps"), 1)

            scores(0, 1)
            outputs(0, 1)
            scores(1, 2)
            outputs(1, 2)
            yb_transposes(0, 1)
            scores(2, 0)
            outputs(2, 0)
            yb_transposes(1, 2)
            yb_transposes(2, 0)
            pe.wait_ge(sem("ybT_ev"), 3)
            pe.wait_ge(sem("ya_ready"), 4)
            for half in range(2):
                w = block_ready(0, 6 + half)
                for t in range(3):
                    n = TILE_N[t]
                    for c in range(KC):
                        last = mm(B[[2, 3, 4, 5, 0, 1][3 * half + t]][0:n, :], yT[:, c, TILE_AT[t]:TILE_AT[t] + n], w[:, c, :],
                                  start=(c == 0), stop=(c == KC - 1))
                    last.then_inc(sem("out0_ps"), 1)

            def moe(l):
                n = 1 + 2 * l
                tiles = NORM_TILES[n]
                a, b = tiles[0], tiles[-1] + 1
                NT = b - a
                transposes(n)
                wait_hnT(pe, n)
                pe.wait_ge(sem(f"route_in{l}"), 64)
                for t in tiles:
                    at = TILE_AT[t]
                    for lo, hi, wr in ((0, G, w_grp[l]), (G, 36, w_exp[l])):
                        for c in range(KC):
                            last = mm(B[6][:, 36 * t + lo:36 * t + hi], hnT[:, c, at:at + P], wr[:, c, :], start=(c == 0), stop=(c == KC - 1))
                last.then_inc(sem("logits_ps"), 1)
                pe.wait_ge(sem("onehot"), l + 1)
                for t in tiles:
                    for s in range(a, t + 1):
                        mm(B[7][:, 4 * t:4 * t + 4], before if s == t else ones, onehot[:, s, :], start=(s == a), stop=(s == t))
                for s in tiles:
                    last = mm(B[7][:, 16:20], ones, onehot[:, s, :], start=(s == a), stop=(s == b - 1))
                last.then_inc(sem("rank_ps"), 1)
                pe.wait_ge(sem("gates"), l + 1)
                pe.wait_ge(sem("n_iter_ready"), l + 1)
                n_it = pe.value_load(n_iter[0:1, l:l + 1], min_val=G, max_val=3 * G)
                nadd = 2 * NT

                def gate_up(it, e):
                    s = (MOE_SLOT0[l] + e) % RING
                    pe.wait_ge(sem(f"gu_w{l}_{e % RING}"), it * 64 + 32 * (e // RING + 1))
                    if e < 2:
                        pe.wait_ge(sem(f"he_ready{l}"), PRIMED + it * EPG)
                    else:
                        pe.wait_ge(sem(f"he_ready{l}"), PRIMED + it * EPG + e - 1)
                    wgu = gu_ring[s][:, :].rearrange("p (u c n) -> p u c n", u=2, c=KC)
                    for c in range(KC):
                        last = mm(B[2 + e % 2][:, :], xT[:, c, :], wgu[:, :, c, :], start=(c == 0), stop=(c == KC - 1))
                    last.then_inc(sem(f"gu_ps{l}"), 1)

                def he_transposes(it, e):
                    pe.wait_ge(sem(f"he_ready{l}"), PRIMED + it * EPG + e + 1)
                    pe.wait_ge(sem(f"heT{l}"), PRIMED + it * EPG + e)
                    for c in range(2):
                        last = nc.tensor.transpose(B[4][:, c * P:(c + 1) * P], he[:, e % 2, c:F:2], ident)
                    last.then_inc(sem(f"heT_ps{l}"), 1)
                    pe.sem_inc(sem(f"gu_free{l}"), 1)

                def down(it, e):
                    pe.wait_ge(sem(f"heT{l}"), PRIMED + it * EPG + e + 1)
                    pe.wait_ge(sem(f"wd_w{l}_{e % RING}"), it * 32 + 16 * (e // RING + 1))
                    if e == 0:
                        pe.wait_ge(sem(f"y_act{l}"), PRIMED + it)
                        pe.wait_ge(sem(f"y_dve{l}"), PRIMED + it)
                    for half in range(2):
                        for c in range(2):
                            last = mm(B[5 + half][:, :], heT[:, e % 2, c, :], wd_ring[e % RING][:, c, half * W:(half + 1) * W],
                                      start=(e == 0 and c == 0), stop=(e == EPG - 1 and c == 1))
                    last.then_inc(sem(f"wd_free{l}"), 1)

                pe.sem_inc(sem(f"wd_free{l}"), PRIMED)
                with pe.Fori(0, n_it) as it:
                    pe.wait_ge(sem(f"sel{l}"), it + 1)
                    pe.wait_ge(sem(f"h_added{l}"), PRIMED + it * nadd)
                    for half in range(2):
                        for c in range(4):
                            for t in tiles:
                                m = TILE_N[t]
                                last = mm(B[half][:, c * P:(c + 1) * P], hn[0:m, t, 4 * half + c:D:KC], sel[0:m, t, :],
                                          start=(t == a), stop=(t == b - 1))
                        last.then_inc(sem(f"x_ps{l}"), 1)
                    pe.wait_ge(sem(f"selT{l}"), PRIMED + it)
                    for t in tiles:
                        m = TILE_N[t]
                        mm(B[7][:, 0:EPG], sel[0:m, t, :], gates[0:m, t, :], start=(t == a), stop=(t == b - 1))
                    for t in tiles:
                        m = TILE_N[t]
                        last = nc.tensor.transpose(B[7][:, 64 + TILE_AT[t]:64 + TILE_AT[t] + m], sel[0:m, t, :], ident[0:m, 0:m])
                    last.then_inc(sem(f"sg_ps{l}"), 1)
                    pe.wait_ge(sem(f"x_act{l}"), it + 1)
                    pe.wait_ge(sem(f"x_dve{l}"), it + 1)
                    gate_up(it, 0)
                    gate_up(it, 1)
                    for e in range(EPG):
                        he_transposes(it, e)
                        if e + 2 < EPG:
                            gate_up(it, e + 2)
                        down(it, e)
                    pe.wait_ge(sem(f"selT{l}"), PRIMED + it + 1)
                    pe.wait_ge(sem(f"y_act{l}"), PRIMED + it + 1)
                    pe.wait_ge(sem(f"y_dve{l}"), PRIMED + it + 1)
                    for k in range(nadd):
                        half, t = k // NT, tiles[k % NT]
                        m = TILE_N[t]
                        if k >= 2:
                            pe.wait_ge(sem(f"h_added{l}"), PRIMED + it * nadd + k - 1)
                        mm(B[k % 2][0:m, :], selT[:, TILE_AT[t]:TILE_AT[t] + m], ysum[:, half * W:(half + 1) * W],
                           start=True, stop=True).then_inc(sem(f"sc_ps{l}"), 1)

            moe(0)

            transposes(2)
            wait_hnT(pe, 2)
            w = block_ready(1, 0)
            for t in range(3):
                token_major(w, t, 0, W, B[2 + t], "kv_ps", rows=P)
            for n in range(2):
                w = block_ready(1, 1 + n)
                for i in range(2):
                    token_major(w, 1 + i, 0, W, B[[5, 6, 7, 0][2 * n + i]], "q1_ps")
            pe.wait_ge(sem("k_rot"), 3)
            pe.wait_ge(sem("kv_raw"), 6)
            for hv in range(KVH):
                for t in range(3):
                    m = TILE_N[t]
                    last = nc.tensor.transpose(B[[1, 2, 3, 4][hv]][:, TILE_AT[t]:TILE_AT[t] + m], ks2[0:m, t, hv, :], ident[0:m, 0:m])
                last.then_inc(sem("qk1T_ps"), 1)
            pe.wait_ge(sem("q_raw"), 4)
            for i in range(2):
                pe.wait_ge(sem("q_rot"), i + 1)
                for m in range(2):
                    for c in range(4):
                        pair = 4 * m + c
                        last = nc.tensor.transpose(B[[5, 6, 7, 0][2 * i + m]][:, c * P:(c + 1) * P],
                                                   qs[:, i, 2 * pair:2 * pair + 2, :].rearrange("p h d -> p (h d)"), ident)
                    last.then_inc(sem("qk1T_ps"), 1)
            pe.wait_ge(sem("qk1T_ev"), KVH + 4)

            def att_scores(u):
                i, pair = u // 8, u % 8
                if u >= 2:
                    pe.wait_ge(sem("p_exp"), 2 * (u - 1))
                for o in range(2):
                    rows = slice(64 * o, 64 * o + 64)
                    mm(B[2 * (u % 2) + o][:, 0:T], qT1[rows, pair, i * P:(i + 1) * P], kT1[rows, pair // 2, :],
                       start=True, stop=True).then_inc(sem("s_ps"), 1)

            att_scores(0)
            for u in range(16):
                i, pair = u // 8, u % 8
                hv = pair // 2
                if u < 15:
                    att_scores(u + 1)
                pe.wait_ge(sem("p_ready"), 2 * u + 2)
                if u >= 2:
                    pe.wait_ge(sem("pT_ev"), u - 1)
                for o in range(2):
                    for t in (1, 2):
                        last = nc.tensor.transpose(B[4 + u % 2][:, (2 * o + t - 1) * P:(2 * o + t) * P],
                                                   probs[:, 2 * (u % 2) + o, TILE_AT[t]:TILE_AT[t] + P], ident)
                if u:
                    pe.wait_ge(sem("pTm_ev"), u)
                for o in range(2):
                    last = nc.tensor.transpose(B[6][0:NM, o * P:(o + 1) * P], probs[:, 2 * (u % 2) + o, 0:NM], ident)
                last.then_inc(sem("pT_ps"), 1)
                pe.wait_ge(sem("pT_ev"), u + 1)
                pe.wait_ge(sem("pTm_ev"), u + 1)
                if u:
                    pe.wait_ge(sem("oT_ev"), u)
                for o in range(2):
                    dst = B[7][64 * o:64 * o + 64, 0:P]
                    mm(dst, vs[:, 1, hv * HD:(hv + 1) * HD], pT[:, u % 2, 2 * o, :], start=True, stop=False)
                    mm(dst, vs[:, 2, hv * HD:(hv + 1) * HD], pT[:, u % 2, 2 * o + 1, :], start=False, stop=False)
                    last = mm(dst, vs[0:NM, 0, hv * HD:(hv + 1) * HD], pTm[0:NM, u % 2, o, :], start=False, stop=True)
                last.then_inc(sem("oT_ps"), 1)
            pe.wait_ge(sem("oT_ev"), 16)
            for half in range(2):
                w = block_ready(1, 3 + half)
                for i in range(2):
                    for c in range(KC):
                        last = mm(B[2 * half + i][:, :], oT[:, c, i * P:(i + 1) * P], w[:, c, :], start=(c == 0), stop=(c == KC - 1))
                    last.then_inc(sem("out1_ps"), 1)
            moe(1)


_INS = ["x", "meta_tokens", "norm_mix", "norm_ffn", "norm_final", "sc_w_in", "sc_conv_w", "gla_w_gate_fwd",
        "gla_b_gate_fwd", "gla_w_gate_bwd", "gla_b_gate_bwd", "gla_norm_w", "sc_w_out", "att_w_in",
        "att_q_norm", "att_k_norm", "att_w_out", "moe_w_group", "moe_b_group", "moe_w_expert",
        "moe_b_expert", "moe_w_gate", "moe_w_up", "moe_w_down"]


def _constants():
    import numpy as np
    s, c = np.arange(128)[:, None], np.arange(128)[None, :]
    same = s // 64 == c // 64
    valid = np.ones((128, 3))
    valid[16:, 0] = 0
    parts = [s == c, same & (s <= c), same & (s > c), same & (s >= c), same & (s < c), s < c, s >= 0 * c, c + 0 * s, valid]
    consts = np.concatenate([np.broadcast_to(p, (128, p.shape[1])) for p in parts], axis=1).astype(np.float32)
    pos = np.arange(256)
    freqs = (np.float32(10000.0) ** (-np.arange(0, 32, 2, dtype=np.float32) / np.float32(32))).astype(np.float32)
    ang = np.concatenate([(pos // 64).astype(np.float32)[:, None] * freqs, (pos % 64).astype(np.float32)[:, None] * freqs], axis=1)
    ang = np.concatenate([np.zeros((128, 32), np.float32), ang]).astype(np.float32)
    table = np.stack([np.cos(ang), np.sin(ang)]).astype(np.float32).reshape(2, 3, 128, 32).transpose(2, 0, 1, 3)
    return np.ascontiguousarray(consts), np.ascontiguousarray(table.reshape(128, 192))


def kernel(**inputs):
    import numpy as _np
    import concourse.bacc as _bacc
    from concourse import mybir as _mybir
    from concourse.bass_utils import run_bass_kernel_spmd as _run

    nc = _bacc.Bacc("TRN2", target_bir_lowering=False, num_devices=1)
    given = {name: _np.ascontiguousarray(inputs[name]) for name in _INS}
    given["consts"], given["rope"] = _constants()
    arrays, args = {}, {}
    for name, a in given.items():
        arrays[f"in_{name}"] = a
        args[name] = nc.dram_tensor(f"in_{name}", a.shape, _mybir.dt.from_np(a.dtype), kind="ExternalInput").ap()
    shape = given["x"].shape
    out = nc.dram_tensor("out_0", shape, _mybir.dt.from_np(given["x"].dtype), kind="ExternalOutput").ap()
    build_program(nc, args, out)
    r = _run(nc, [arrays], core_ids=[0])
    return r.results[0]["out_0"]
```

```python
import concourse.bass as bass
from concourse import mybir
from contextlib import ExitStack


def build_program(nc: bass.Bass, A: dict, out: bass.AP):
    f32 = mybir.dt.float32
    f32r = mybir.dt.float32r
    u32 = mybir.dt.uint32
    i32 = mybir.dt.int32
    ALU = mybir.AluOpType
    ACT = mybir.ActivationFunctionType
    X = mybir.AxisListType.X

    P = 128
    SEQ, D = A["x"].shape[1], A["x"].shape[2]
    NM = A["meta_tokens"].shape[0]
    T = NM + SEQ
    KC = D // P
    TILE_AT = [0, NM, NM + P]
    TILE_N = [NM, P, P]
    HEADS, DV, DK, C = 4, 128, 64, 64
    RANK = A["gla_w_gate_fwd"].shape[1]
    QH, KVH, HD = 16, 4, 64
    G, EPG, F = 4, 8, 256
    EPS = 1e-6
    TAU = 16.0
    W = 512
    NORM_TILES = [[0, 1, 2], [0, 1, 2], [0, 1, 2], [1, 2], [1, 2]]
    CHUNKS = [(0, 0, NM), (1, 0, C), (1, C, C), (2, 0, C), (2, C, C)]
    MIX0_COLS = [3 * W, 4 * W, 5 * W, 2 * W, W, 0]
    MIX1_COLS = [2 * W, 0, W]
    NMIX = [len(MIX0_COLS) + 2, len(MIX1_COLS) + 2]
    UNIT = 2048
    RING = 8
    BUFS = 4
    MIX_SLOT0 = [0, 2 * NMIX[0] % RING]
    MOE_SLOT0 = [2 * NMIX[0] % RING, 2 * (NMIX[0] + NMIX[1]) % RING]
    UNITS = [("gu", 0, 0), ("gu", 0, 1), ("gu", 1, 0), ("gu", 1, 1)]
    for e in range(EPG):
        if e + 2 < EPG:
            UNITS += [("gu", e + 2, 0), ("gu", e + 2, 1)]
        UNITS += [("d", e, 0)]
    NU = len(UNITS)
    AT = {u: j for j, u in enumerate(UNITS)}
    def used(it, kind, e, half=0):
        return it * NU + AT[kind, e, half] + 1 + BUFS

    POOL_UNITS = [j for j in range(NU) if j % 6 == 3]

    def low_done(j):
        mine = j in POOL_UNITS
        return ("lo_pool" if mine else "lo_dve"), sum((i in POOL_UNITS) == mine for i in range(j + 1)), \
            sum((i in POOL_UNITS) == mine for i in range(NU))

    def raw_count(j):
        same = [16 * (2 if UNITS[i][0] == "gu" else 1) * (i <= j) for i in range(j % RING, NU, RING)]
        return sum(same), sum(16 * (2 if UNITS[i][0] == "gu" else 1) for i in range(j % RING, NU, RING))
    PRIMED = 1

    ctx = ExitStack()
    with ctx:
        def sb(name, shape, dt=f32):
            return ctx.enter_context(nc.sbuf_tensor(name, shape, dt))

        made = {}

        def sem(name):
            if name not in made:
                made[name] = ctx.enter_context(nc.semaphore(name))
            return made[name]

        h = sb("h", [P, 3, D])
        hn = sb("hn", [P, 3, D])
        hnT = sb("hnT", [P, KC, T])
        gain = sb("gain", [P, D])
        raw = [sb(f"raw{i}", [P, UNIT]) for i in range(RING)]
        consts = sb("consts", [P, A["consts"].shape[1]])
        rope = sb("rope", [P, 2, 3, 32])
        stats = sb("stats", [P, 5, 4, 3])
        w_g_in = sb("w_g_in", [P, KC, 2 * RANK])
        gT = sb("gT", [2 * RANK + 1, T])
        wgate = sb("wgate", [2 * RANK + 1, W])
        conv_w = sb("conv_w", [P, 3, 4])
        gla_gain = sb("gla_gain", [P, DV])
        qk_gain = sb("qk_gain", [P, 2, HD])
        w_route = [sb(f"w_route{l}", [P, KC, 36]) for l in range(2)]
        b_route = sb("b_route", [P, 2, 36])
        idx_g = sb("idx_g", [P, 3, 8], u32)
        idx_e = sb("idx_e", [P, 3, 8], u32)
        n_iter = sb("n_iter", [P, 3], i32)
        junk = sb("junk", [P, DV])
        att_max = sb("att_max", [P, 32])
        att_sum = sb("att_sum", [P, 32])
        att_rcp = sb("att_rcp", [P, 32])
        turns = ExitStack()
        scratch = turns.enter_context(nc.sbuf_tensor("scratch", [P, 15600], f32))
        turns.close()
        moe_scratch = sb("moe_scratch", [P, 3550])
        w_hi = [sb(f"w_hi{i}", [P, UNIT], f32r) for i in range(BUFS)]
        w_lo = [sb(f"w_lo{i}", [P, UNIT], f32r) for i in range(BUFS)]
        x_hi = sb("x_hi", [P, KC, P], f32r)
        x_lo = sb("x_lo", [P, KC, P], f32r)
        heT_hi = sb("heT_hi", [P, 2, 2, P], f32r)
        heT_lo = sb("heT_lo", [P, 2, 2, P], f32r)
        spent = [0]

        area = [scratch]

        def carve(*shape):
            n = 1
            for s in shape:
                n *= s
            ap = area[0][:, spent[0]:spent[0] + n]
            spent[0] += n
            assert spent[0] <= area[0].shape[1], spent[0]
            if len(shape) == 2:
                return ap.rearrange("p (a b) -> p a b", a=shape[0])
            if len(shape) == 3:
                return ap.rearrange("p (a b c) -> p a b c", a=shape[0], b=shape[1])
            return ap

        ident = consts[:, 0:128]
        fwd_bwd = consts[:, 128:384]
        incl_fwd = consts[:, 128:256]
        strict_bwd = consts[:, 256:384]
        incl_bwd = consts[:, 384:512]
        strict_fwd = consts[:, 512:640]
        before = consts[:, 640:768]
        ones = consts[:, 768:896]
        iota = consts[:, 896:1024]
        valid = consts[:, 1024:1027]

        z = carve(4, T + 2)
        conv = carve(4, T)
        yT = carve(KC, T)
        qT = carve(2, T)
        kT = carve(2, T)
        ktok = carve(3, 256)
        la = carve(3, W)
        decay = carve(4, 5)
        E = carve(4, T)
        Ei = carve(4, T)
        kend = carve(3, W)
        state = carve(8, 2, 128)
        masked = carve(4, 2 * P)
        oss = carve(3, 4, 4)
        la_tmp = E[:, :, :].rearrange("p a b -> p (a b)")
        la_tmp2 = Ei[:, :, :].rearrange("p a b -> p (a b)")
        yb = kend
        v = hn[:, 0:3, 0:W]
        rs = hn[:, 0:3, W:2 * W]
        spent[0] = 0
        qs = carve(2, QH, HD)
        ks = carve(3, KVH, HD)
        ks2 = carve(3, KVH, 2 * HD)
        vs = carve(3, KVH * HD)
        qtmp = carve(2, QH * HD)
        qT1 = carve(8, 2 * P)
        kT1 = carve(KVH, T)
        oT = carve(8, 2 * P)
        probs = carve(4, T)
        pT = carve(2, 4, P)
        pTm = carve(2, 2, P)
        hstat = carve(4, 32)
        spent[0] = 0
        area[0] = moe_scratch
        sel = carve(3, P)
        selT = carve(1, T)[:, 0, :]
        logitsT = carve(1, T)[:, 0, :]
        act_g = carve(2, F)
        he = carve(2, F)
        ysum = carve(1, D)[:, 0, :]
        slot_gates = carve(1, EPG)[:, 0, :]
        logits = carve(3, 36)
        padded = carve(3, 8)
        top_g = carve(3, 8)
        top_e = carve(3, 8)
        onehot = carve(3, G)
        expg = carve(3, G)
        esel = carve(3, EPG)
        picked = carve(3, G, EPG)
        gates = carve(3, EPG)
        gtmp = carve(3, EPG)
        key = carve(1, 4)[:, 0, :]
        rstat = carve(12, 4)

        B = [ctx.enter_context(nc.psum_tensor(f"bank{i}", [P, W], f32)) for i in range(8)]

        def chain(eng, name):
            n = [0]

            def link(ins):
                n[0] += 1
                ins.then_inc(sem(name), 1)
                eng.wait_ge(sem(name), n[0])
            return link

        block = ctx.enter_context(nc.Block())

        def upto(n):
            return sum(len(t) for t in NORM_TILES[:n])

        MIX_READ = [[("k", 3), ("v", 3), ("r", 3), ("ax", 4), ("ac", 4), ("ab", 4), ("out0", 3), ("out0", 6)],
                    [("kv", 3), ("q1", 2), ("q1", 4), ("out1", 2), ("out1", 4)]]
        PROJ, total = {}, 0
        for kind, count in (("g", 1), ("q", 2), ("k", 3), ("v", 3), ("r", 3), ("ax", 4), ("ac", 4), ("ab", 4),
                            ("out0", 6), ("kv", 3), ("q1", 4), ("out1", 4)):
            PROJ[kind] = total
            total += count

        def wait_mix_read(eng, l, b):
            kind, count = MIX_READ[l][b]
            eng.wait_ge(sem("proj_ps"), PROJ[kind] + count)

        def subtract(eng, ops, l, it, j):
            eng.wait_ge(sem(f"w_hi{l}"), it * NU + j + 1)
            name, _, _ = low_done(j)
            ops.tensor_tensor(w_lo[j % BUFS][:, :], raw[(MOE_SLOT0[l] + j) % RING][:, :], w_hi[j % BUFS][:, :].bitcast(f32),
                              ALU.subtract).then_inc(sem(f"{name}{l}"), 1)

        @block.sync
        def _(sp):
            sp.dma_start(h[:, 1, :], A["x"][0, 0:P, :]).then_inc(sem("h_in"), 16)
            sp.dma_start(h[:, 2, :], A["x"][0, P:2 * P, :]).then_inc(sem("h_in"), 16)
            sp.dma_start(h[0:NM, 0, :], A["meta_tokens"]).then_inc(sem("h_in"), 16)
            sp.dma_start(consts[:, :], A["consts"]).then_inc(sem("consts_in"), 16)
            sp.dma_start(gain[:, :], A["norm_mix"][0:1, :].broadcast_to([P, D])).then_inc(sem("gain0_in"), 16)

            def mix_block(l, b, half):
                slot = (MIX_SLOT0[l] + 2 * b + half) % RING
                dst = raw[slot][:, :].rearrange("p (c n) -> p c n", c=4)
                w_in, w_out = (A["sc_w_in"], A["sc_w_out"]) if l == 0 else (A["att_w_in"], A["att_w_out"])
                cols = MIX0_COLS if l == 0 else MIX1_COLS
                if b < len(cols):
                    src = w_in[0].rearrange("(p c) n -> p c n", c=KC)[:, :, cols[b]:cols[b] + W]
                else:
                    n = b - len(cols)
                    src = w_out[0].rearrange("(c p) n -> p c n", c=KC)[:, :, n * W:(n + 1) * W]
                sp.dma_start(dst, src[:, 4 * half:4 * half + 4, :]).then_inc(sem(f"mix_w{slot}"), 16)

            def unit(l, g, j):
                kind, e, half = UNITS[j]
                dst = raw[(MOE_SLOT0[l] + j) % RING]
                if kind == "gu":
                    gu = dst[:, :].rearrange("p (u c n) -> p u c n", u=2, c=4)
                    for u, name in enumerate(("moe_w_gate", "moe_w_up")):
                        src = A[name][l].rearrange("(g e) (p c) n -> g e p c n", g=G, c=KC)[bass.ds(g, 1), e, :, 4 * half:4 * half + 4, :]
                        sp.dma_start(gu[:, u], src.rearrange("g p c n -> p (g c) n")).then_inc(sem(f"raw{l}_{j % RING}"), 16)
                else:
                    src = A["moe_w_down"][l].rearrange("(g e) (p c) n -> g e p c n", g=G, c=2)[bass.ds(g, 1), e]
                    sp.dma_start(dst[:, :].rearrange("p (c n) -> p c n", c=2), src.rearrange("g p c n -> p (g c) n"))\
                      .then_inc(sem(f"raw{l}_{j % RING}"), 16)

            for b in range(NMIX[0]):
                if 2 * b >= RING:
                    wait_mix_read(sp, 0, b - RING // 2)
                for half in range(2):
                    mix_block(0, b, half)

            before_last0 = None
            for l in range(2):
                if l == 1:
                    for b in range(NMIX[1]):
                        if 2 * b >= RING:
                            wait_mix_read(sp, 1, b - RING // 2)
                        for half in range(2):
                            if 2 * b < RING:
                                name, count, per = low_done(NU - RING + 2 * b + half)
                                sp.wait_ge(sem(f"{name}0"), before_last0 * per + count)
                            mix_block(1, b, half)

                def group(g, it, first):
                    for j in range(NU):
                        if first and j < RING:
                            if j % 2 == 0:
                                wait_mix_read(sp, l, NMIX[l] - RING // 2 + j // 2)
                        elif j < RING:
                            name, count, per = low_done(NU + j - RING)
                            sp.wait_ge(sem(f"{name}{l}"), (it - 1) * per + count)
                        else:
                            name, count, per = low_done(j - RING)
                            sp.wait_ge(sem(f"{name}{l}"), it * per + count)
                        unit(l, g, j)

                group(0, 0, True)
                with sp.Fori(1, G) as g:
                    group(g, g, False)
                sp.wait_ge(sem("n_iter_ready"), l + 1)
                n_next = sp.value_load(n_iter[0:1, l:l + 1], min_val=G, max_val=3 * G)
                with sp.If(n_next > G):
                    with sp.Fori(G, n_next, G) as it0:
                        with sp.Fori(0, G) as g:
                            group(g, it0 + g, False)
                if l == 0:
                    before_last0 = sp.value_load(n_iter[0:1, 2:3], min_val=G - 1, max_val=3 * G - 1)

            for i in range(2):
                sp.wait_ge(sem("hn_ready"), upto(4) + i + 1)
                sp.dma_start(out[0, i * P:(i + 1) * P, :], hn[:, 1 + i, :]).then_inc(sem("out_done"), 16)
            sp.wait_ge(sem("out_done"), 32)

        @block.gpsimd
        def _(pool):
            pool.memset(wgate[:, :], 0.0).then_inc(sem("pool_clear"), 1)
            pool.wait_ge(sem("pool_clear"), 1)
            pool.memset(gT[2 * RANK:2 * RANK + 1, :], 1.0).then_inc(sem("pool_clear"), 1)
            pool.dma_start(w_g_in[:, :, :], A["sc_w_in"][0].rearrange("(p c) n -> p c n", c=KC)[:, :, 6 * W:6 * W + 2 * RANK])\
                .then_inc(sem("w_g_in"), 16)
            pool.dma_start(wgate[0:RANK, 0:256], A["gla_w_gate_fwd"][0]).then_inc(sem("gla_params_in"), 16)
            pool.dma_start(wgate[RANK:2 * RANK, 256:512], A["gla_w_gate_bwd"][0]).then_inc(sem("gla_params_in"), 16)
            pool.dma_start(wgate[2 * RANK:2 * RANK + 1, 0:256], A["gla_b_gate_fwd"]).then_inc(sem("gla_params_in"), 16)
            pool.dma_start(wgate[2 * RANK:2 * RANK + 1, 256:512], A["gla_b_gate_bwd"]).then_inc(sem("gla_params_in"), 16)
            pool.dma_start(gla_gain[:, :], A["gla_norm_w"].broadcast_to([P, DV])).then_inc(sem("gla_params_in"), 16)
            with nc.allow_non_contiguous_dma("1536 single elements, once"):
                for t in range(3):
                    pool.dma_start(conv_w[:, t, :], A["sc_conv_w"][0, t, :].rearrange("(c p) -> p c", p=P)).then_inc(sem("gla_params_in"), 16)
            pool.dma_start(qk_gain[:, 0, :], A["att_q_norm"].broadcast_to([P, HD])).then_inc(sem("att_params_in"), 16)
            pool.dma_start(qk_gain[:, 1, :], A["att_k_norm"].broadcast_to([P, HD])).then_inc(sem("att_params_in"), 16)
            pool.dma_start(rope[:, :, :, :], A["rope"].rearrange("p (a t j) -> p a t j", a=2, t=3)).then_inc(sem("att_params_in"), 16)
            for l in range(2):
                pool.dma_start(w_route[l][:, :, 0:G], A["moe_w_group"][l].rearrange("(p c) n -> p c n", c=KC)).then_inc(sem(f"route_in{l}"), 16)
                pool.dma_start(w_route[l][:, :, G:36], A["moe_w_expert"][l].rearrange("(p c) n -> p c n", c=KC)).then_inc(sem(f"route_in{l}"), 16)
                pool.dma_start(b_route[:, l, 0:G], A["moe_b_group"][l:l + 1, :].broadcast_to([P, G])).then_inc(sem(f"route_in{l}"), 16)
                pool.dma_start(b_route[:, l, G:36], A["moe_b_expert"][l:l + 1, :].broadcast_to([P, 32])).then_inc(sem(f"route_in{l}"), 16)
            for n in range(1, 5):
                src = [None, A["norm_ffn"][0:1, :], A["norm_mix"][1:2, :], A["norm_ffn"][1:2, :],
                       A["norm_final"].rearrange("(a n) -> a n", a=1)][n]
                pool.wait_ge(sem("hn_ready"), upto(n))
                pool.dma_start(gain[:, :], src.broadcast_to([P, D])).then_inc(sem("gain_in"), 16)
                if n in (2, 4):
                    l = n // 2 - 1
                    pool.wait_ge(sem("n_iter_ready"), l + 1)
                    n_it = pool.value_load(n_iter[0:1, l:l + 1], min_val=G, max_val=3 * G)
                    with pool.Fori(0, n_it) as it:
                        for j in POOL_UNITS:
                            subtract(pool, nc.gpsimd, l, it, j)

        def wait_h(eng, n):
            if n == 0:
                eng.wait_ge(sem("h_in"), 48)
            elif n in (1, 3):
                eng.wait_ge(sem(f"h_mixed{n // 2}"), [6, 4][n // 2])
            else:
                eng.wait_ge(sem("h_moe"), n // 2)

        def wait_hnT(eng, n):
            eng.wait_ge(sem("hnT_act"), upto(n + 1))
            eng.wait_ge(sem("hnT_dve"), upto(n + 1))

        @block.scalar
        def _(act):
            link = chain(act, "act_chain")

            def norm(n):
                tiles = NORM_TILES[n]
                for i, t in enumerate(tiles):
                    wait_h(act, n)
                    if i == 0:
                        act.wait_ge(sem("clear"), 1)
                    m = TILE_N[t]
                    nc.scalar.activation(hn[0:m, t, :], h[0:m, t, :], ACT.Square,
                                         accum_out=stats[0:m, n, 0, t:t + 1]).then_inc(sem("norm_ss"), 1)
                act.wait_ge(sem("norm_var"), n + 1)
                nc.scalar.activation(stats[:, n, 2, :], stats[:, n, 1, :], ACT.Sqrt).then_inc(sem("norm_std"), 1)

            def transposes_out(n):
                for i, t in enumerate(NORM_TILES[n]):
                    m = TILE_N[t]
                    act.wait_ge(sem("hnT_ps"), 2 * (upto(n) + i) + 1)
                    nc.scalar.activation(hnT[:, 0:4, TILE_AT[t]:TILE_AT[t] + m],
                                         B[0][:, :].rearrange("p (c n) -> p c n", c=4)[:, :, 0:m], ACT.Copy).then_inc(sem("hnT_act"), 1)

            norm(0)
            transposes_out(0)
            act.wait_ge(sem("pool_clear"), 2)
            act.wait_ge(sem("proj_ps"), PROJ["g"] + 1)
            nc.scalar.activation(gT[0:2 * RANK, :], B[2][0:2 * RANK, 0:T], ACT.Copy).then_inc(sem("g_ev"), 1)
            for m in range(2):
                act.wait_ge(sem("proj_ps"), PROJ["q"] + m + 1)
                nc.scalar.activation(qT[:, m, :], B[3 + m][:, 0:T], ACT.Copy, scale=DK ** -0.5).then_inc(sem("q_ev"), 1)
            for t in range(3):
                n = TILE_N[t]
                act.wait_ge(sem("la_ps"), t + 1)
                if t:
                    act.wait_ge(sem("la_ln"), t)
                link(nc.scalar.activation(la_tmp[0:n, 0:W], B[t][0:n, :], ACT.Abs))
                link(nc.scalar.activation(la_tmp[0:n, 0:W], la_tmp[0:n, 0:W], ACT.Exp, scale=-1.0))
                if t >= 1:
                    act.wait_ge(sem("la_ready"), t)
                nc.scalar.activation(la_tmp2[0:n, 0:W], la_tmp[0:n, 0:W], ACT.Ln, bias=1.0).then_inc(sem("la_ln"), 1)
            for t in range(3):
                n = TILE_N[t]
                act.wait_ge(sem("proj_ps"), PROJ["v"] + t + 1)
                nc.scalar.activation(v[0:n, t, :], B[3 + t][0:n, :], ACT.Copy).then_inc(sem("v_ev"), 1)
            for m in range(2):
                act.wait_ge(sem("kT_ps"), m + 1)
                nc.scalar.activation(kT[:, m, :], B[6 + m][:, 0:T], ACT.Copy).then_inc(sem("kT_ev"), 1)
            for t in range(3):
                n = TILE_N[t]
                act.wait_ge(sem("proj_ps"), PROJ["r"] + t + 1)
                nc.scalar.activation(rs[0:n, t, :], B[3 + t][0:n, :], ACT.Silu).then_inc(sem("r_ev"), 1)
            for m in range(4):
                act.wait_ge(sem("proj_ps"), PROJ["ax"] + m + 1)
                act.wait_ge(sem("clear"), 2)
                nc.scalar.activation(z[:, m, 1:T + 1], B[6 + m % 2][:, 0:T], ACT.Copy).then_inc(sem("ax_ev"), 1)
            for dm in range(4):
                act.wait_ge(sem("cum_ps"), dm + 1)
                act.wait_ge(sem("la_ready"), 3)
                nc.scalar.activation(E[:, dm, :], B[dm][:, 0:T], ACT.Exp).then_inc(sem("E_exp"), 1)
                nc.scalar.activation(Ei[:, dm, :], B[dm][:, 0:T], ACT.Exp, scale=-1.0).then_inc(sem("E_exp"), 1)
            for t in range(3):
                n = TILE_N[t]
                act.wait_ge(sem("kend_ps"), t + 1)
                nc.scalar.activation(kend[0:n, t, :], B[[4, 5, 0][t]][0:n, :], ACT.Exp).then_inc(sem("kend_exp"), 1)
            for i, t in enumerate((1, 2, 0)):
                n = TILE_N[t]
                act.wait_ge(sem("o_ps"), i + 1)
                for hd in range(HEADS):
                    src = B[[6, 0, 6][i] + hd % 2][0:n, (hd // 2) * DV:(hd // 2 + 1) * DV]
                    nc.scalar.activation(junk[0:n, :], src, ACT.Square,
                                         accum_out=oss[0:n, i, 0, hd:hd + 1]).then_inc(sem("o_ss"), 1)
                    act.wait_ge(sem("o_ss"), 4 * i + hd + 1)
                act.wait_ge(sem("o_var"), i + 1)
                nc.scalar.activation(oss[0:n, i, 2, :], oss[0:n, i, 1, :], ACT.Sqrt).then_inc(sem("o_std"), 1)
                act.wait_ge(sem("ybT_ps"), i + 1)
                nc.scalar.activation(yT[:, 4:8, TILE_AT[t]:TILE_AT[t] + n],
                                     B[[6, 0, 6][i]][:, :].rearrange("p (c n) -> p c n", c=4)[:, :, 0:n], ACT.Copy).then_inc(sem("ybT_ev"), 1)

            def moe(l):
                n = 1 + 2 * l
                norm(n)
                transposes_out(n)
                act.wait_ge(sem("gl_shift"), l + 1)
                tiles = NORM_TILES[n]
                a, b = tiles[0], tiles[-1] + 1
                nc.scalar.activation(expg[:, a:b, :], expg[:, a:b, :], ACT.Exp).then_inc(sem("gl_exp"), 1)
                act.wait_ge(sem("top_diff"), l + 1)
                nc.scalar.activation(rstat[:, 4, a:b], rstat[:, 3, a:b], ACT.Exp).then_inc(sem("top_exp"), 1)
                act.wait_ge(sem("n_iter_ready"), l + 1)
                n_it = act.value_load(n_iter[0:1, l:l + 1], min_val=G, max_val=3 * G)
                act.sem_inc(sem(f"y_act{l}"), PRIMED)
                with act.Fori(0, n_it) as it:
                    for j in range(BUFS):
                        round_weights(l, it, j)
                    for half in range(2):
                        act.wait_ge(sem(f"x_ps{l}"), 2 * it + half + 1)
                        nc.scalar.activation(x_hi[:, 4 * half:4 * half + 4, :], B[half][:, :].rearrange("p (c n) -> p c n", c=4),
                                             ACT.Copy).then_inc(sem(f"x_hi{l}"), 1)
                    todo = BUFS
                    for e in range(EPG):
                        while todo < NU and todo - BUFS <= AT["gu", e, 1]:
                            if todo - BUFS == AT["gu", e, 0] and e >= 2:
                                heT_high(l, it, e - 2)
                            round_weights(l, it, todo)
                            todo += 1
                        act.wait_ge(sem(f"w_used{l}"), used(it, "gu", e, 1))
                        if e < 2:
                            act.wait_ge(sem(f"he_ready{l}"), PRIMED + it * EPG)
                        else:
                            act.wait_ge(sem(f"he_ready{l}"), PRIMED + it * EPG + e - 1)
                        nc.scalar.activation(act_g[:, e % 2, :], B[2 + e % 2][:, 0:F], ACT.Silu).then_inc(sem(f"silu{l}"), 1)
                    for e in (EPG - 2, EPG - 1):
                        heT_high(l, it, e)
                    act.wait_ge(sem(f"w_used{l}"), used(it, "d", EPG - 1))
                    nc.scalar.activation(ysum[:, 0:W], B[5][:, :], ACT.Copy).then_inc(sem(f"y_act{l}"), 1)

            def round_weights(l, it, j):
                count, per = raw_count(j)
                act.wait_ge(sem(f"raw{l}_{j % RING}"), it * per + count)
                act.wait_ge(sem(f"w_used{l}"), it * NU + j + 1)
                nc.scalar.activation(w_hi[j % BUFS][:, :], raw[(MOE_SLOT0[l] + j) % RING][:, :], ACT.Copy).then_inc(sem(f"w_hi{l}"), 1)

            def heT_high(l, it, e):
                act.wait_ge(sem(f"heT_ps{l}"), it * EPG + e + 1)
                if e >= 2:
                    act.wait_ge(sem(f"w_used{l}"), used(it, "d", e - 2))
                else:
                    act.wait_ge(sem(f"w_used{l}"), it * NU + BUFS)
                nc.scalar.activation(heT_hi[:, e % 2, :, :], B[4][:, 0:2 * P].rearrange("p (c n) -> p c n", c=2), ACT.Copy)\
                    .then_inc(sem(f"heT_hi{l}"), 1)

            moe(0)

            norm(2)
            transposes_out(2)
            for t in range(3):
                act.wait_ge(sem("proj_ps"), PROJ["kv"] + t + 1)
                nc.scalar.activation(ks[:, t, :, :], B[2 + t][:, 0:256].rearrange("p (h d) -> p h d", h=KVH), ACT.Copy).then_inc(sem("kv_raw"), 1)
                nc.scalar.activation(vs[:, t, :], B[2 + t][:, 256:512], ACT.Copy).then_inc(sem("kv_raw"), 1)
            for n in range(2):
                for i in range(2):
                    act.wait_ge(sem("proj_ps"), PROJ["q1"] + 2 * n + i + 1)
                    nc.scalar.activation(qs[:, i, 8 * n:8 * n + 8, :], B[[5, 6, 7, 0][2 * n + i]][:, :].rearrange("p (h d) -> p h d", h=8),
                                         ACT.Copy).then_inc(sem("q_raw"), 1)
            act.wait_ge(sem("head_var"), 1)
            nc.scalar.activation(hstat[:, 2, 0:12], hstat[:, 1, 0:12], ACT.Sqrt).then_inc(sem("head_std"), 1)
            act.wait_ge(sem("head_var"), 2)
            nc.scalar.activation(hstat[:, 2, 0:32], hstat[:, 1, 0:32], ACT.Sqrt).then_inc(sem("head_std"), 1)
            for hv in range(KVH):
                act.wait_ge(sem("qk1T_ps"), hv + 1)
                nc.scalar.activation(kT1[:, hv, :], B[[1, 2, 3, 4][hv]][:, 0:T], ACT.Copy).then_inc(sem("qk1T_ev"), 1)
            for i in range(2):
                for m in range(2):
                    act.wait_ge(sem("qk1T_ps"), KVH + 2 * i + m + 1)
                    nc.scalar.activation(qT1[:, 4 * m:4 * m + 4, i * P:(i + 1) * P],
                                         B[[5, 6, 7, 0][2 * i + m]][:, :].rearrange("p (c n) -> p c n", c=4), ACT.Copy).then_inc(sem("qk1T_ev"), 1)
            def exps(u):
                for o in range(2):
                    act.wait_ge(sem("s_max"), 2 * u + o + 1)
                    if u >= 2:
                        act.wait_ge(sem("pT_ps"), u - 1)
                    nc.scalar.activation(probs[:, 2 * (u % 2) + o, :], B[2 * (u % 2) + o][:, 0:T], ACT.Exp,
                                         bias=att_max[:, 2 * u + o:2 * u + o + 1],
                                         accum_out=att_sum[:, 2 * u + o:2 * u + o + 1]).then_inc(sem("p_exp"), 1)

            def pT_out(u):
                act.wait_ge(sem("pT_ps"), u + 1)
                if u >= 2:
                    act.wait_ge(sem("oT_ps"), u - 1)
                nc.scalar.activation(pT[:, u % 2, :, :], B[4 + u % 2][:, :].rearrange("p (c n) -> p c n", c=4), ACT.Copy).then_inc(sem("pT_ev"), 1)

            exps(0)
            for u in range(16):
                if u < 15:
                    exps(u + 1)
                pT_out(u)
            moe(1)
            norm(4)

        @block.vector
        def _(dve):
            link = chain(dve, "dve_chain")

            def norm(n):
                tiles = NORM_TILES[n]
                dve.wait_ge(sem("norm_ss"), upto(n + 1))
                nc.vector.tensor_scalar(stats[:, n, 1, :], stats[:, n, 0, :], 1.0 / D, EPS, ALU.mult, ALU.add).then_inc(sem("norm_var"), 1)
                dve.wait_ge(sem("norm_std"), n + 1)
                link(nc.vector.reciprocal(stats[:, n, 3, :], stats[:, n, 2, :]))
                if n:
                    dve.wait_ge(sem("gain_in"), 16 * n)
                else:
                    dve.wait_ge(sem("gain0_in"), 16)
                for t in tiles:
                    m = TILE_N[t]
                    nc.vector.scalar_tensor_tensor(hn[0:m, t, :], h[0:m, t, :], stats[0:m, n, 3, t:t + 1], gain[0:m, :],
                                                   ALU.mult, ALU.mult).then_inc(sem("hn_ready"), 1)

            def transposes_out(n):
                for i, t in enumerate(NORM_TILES[n]):
                    m = TILE_N[t]
                    dve.wait_ge(sem("hnT_ps"), 2 * (upto(n) + i) + 2)
                    nc.vector.tensor_copy(hnT[:, 4:8, TILE_AT[t]:TILE_AT[t] + m],
                                          B[1][:, :].rearrange("p (c n) -> p c n", c=4)[:, :, 0:m]).then_inc(sem("hnT_dve"), 1)

            nc.vector.memset(stats[:, :, :, :].rearrange("p a b c -> p (a b c)"), 1.0).then_inc(sem("clear"), 1)

            nc.vector.memset(z[:, :, :].rearrange("p a b -> p (a b)"), 0.0).then_inc(sem("clear"), 1)
            norm(0)
            transposes_out(0)
            for t in range(3):
                n = TILE_N[t]
                dve.wait_ge(sem("proj_ps"), PROJ["k"] + t + 1)
                nc.vector.tensor_copy(ktok[0:n, t, :], B[5 + t][0:n, 0:256]).then_inc(sem("k_ev"), 1)
            for t in range(3):
                n = TILE_N[t]
                dve.wait_ge(sem("la_ln"), t + 1)
                link(nc.vector.tensor_scalar(la[0:n, t, :], B[t][0:n, :], 0.0, 1.0 / TAU, ALU.min, ALU.mult))
                nc.vector.scalar_tensor_tensor(la[0:n, t, :], la_tmp2[0:n, 0:W], -1.0 / TAU, la[0:n, t, :], ALU.mult, ALU.add).then_inc(sem("la_ready"), 1)
            dve.wait_ge(sem("gla_params_in"), 128)
            for t in range(3):
                n = TILE_N[t]
                dve.wait_ge(sem("r_ev"), t + 1)
                r4 = rs[0:n, t, :].rearrange("p (h d) -> p h d", h=HEADS)
                nc.vector.tensor_tensor(r4, r4, gla_gain[0:n, :].unsqueeze(1).to_broadcast([n, HEADS, DV]), ALU.mult).then_inc(sem("rs_ready"), 1)
            dve.wait_ge(sem("E_exp"), 8)
            link(nc.vector.tensor_copy(decay[:, 0:2, 0:1], E[:, 0:2, NM - 1:NM]))
            link(nc.vector.tensor_copy(decay[:, 0:2, 1:5], E[:, 0:2, NM + C - 1:T:C]))
            link(nc.vector.tensor_copy(decay[:, 2:4, 0:1], E[:, 2:4, 0:1]))
            link(nc.vector.tensor_copy(decay[:, 2:4, 1:5], E[:, 2:4, NM:T:C]))
            dve.wait_ge(sem("q_ev"), 2)
            dve.wait_ge(sem("kT_ev"), 2)
            for d in range(2):
                nc.vector.tensor_tensor(E[:, 2 * d:2 * d + 2, :], E[:, 2 * d:2 * d + 2, :], qT[:, :, :], ALU.mult).then_inc(sem("qk_dec"), 1)
                nc.vector.tensor_tensor(Ei[:, 2 * d:2 * d + 2, :], Ei[:, 2 * d:2 * d + 2, :], kT[:, :, :], ALU.mult).then_inc(sem("qk_dec"), 1)
            for t in range(3):
                n = TILE_N[t]
                dve.wait_ge(sem("kend_exp"), t + 1)
                for d in range(2):
                    ke = kend[0:n, t, 256 * d:256 * d + 256]
                    nc.vector.tensor_tensor(ke, ke, ktok[0:n, t, :], ALU.mult).then_inc(sem("kend"), 1)
            for m in range(4):
                dve.wait_ge(sem("proj_ps"), PROJ["ac"] + m + 1)
                dve.wait_ge(sem("ax_ev"), m + 1)
                zz = z[:, m, 1:T + 1]
                nc.vector.tensor_tensor(zz, B[6 + m % 2][:, 0:T], zz, ALU.mult).then_inc(sem("z_ready"), 1)
            dve.wait_ge(sem("z_ready"), 4)
            dve.wait_ge(sem("gla_params_in"), 128)
            for tap in range(3):
                for m in range(4):
                    src = z[:, m, tap:tap + T]
                    if tap == 0:
                        last = nc.vector.tensor_scalar(conv[:, m, :], src, conv_w[:, 0, m:m + 1], None, ALU.mult)
                    else:
                        last = nc.vector.scalar_tensor_tensor(conv[:, m, :], src, conv_w[:, tap, m:m + 1], conv[:, m, :],
                                                       ALU.mult, ALU.add)
                link(last)
            for m in range(4):
                dve.wait_ge(sem("proj_ps"), PROJ["ab"] + m + 1)
                nc.vector.tensor_tensor(yT[:, m, :], B[6 + m % 2][:, 0:T], conv[:, m, :], ALU.mult).then_inc(sem("ya_ready"), 1)
            for k in range(8):
                d, i = k % 2, k // 2
                j = i if d == 0 else 4 - i
                dve.wait_ge(sem("kvs_ps"), k + 1)
                if i:
                    dve.wait_ge(sem("state"), 4 * (k - 1))
                for m in range(2):
                    for hh in range(2):
                        rows = slice(64 * hh, 64 * hh + 64)
                        got = B[[1, 2, 3, 4, 5, 0, 1, 2][k]][rows, 256 * m + DV * hh:256 * m + DV * hh + DV]
                        new = state[rows, 4 * d + i, m, :]
                        if i == 0:
                            nc.vector.tensor_copy(new, got).then_inc(sem("state"), 1)
                        else:
                            nc.vector.scalar_tensor_tensor(new, state[rows, 4 * d + i - 1, m, :], decay[rows, 2 * d + m, j:j + 1], got,
                                                           ALU.mult, ALU.add).then_inc(sem("state"), 1)
            def mask_scores(i, t):
                n = TILE_N[t]
                for hd in range(HEADS):
                    dve.wait_ge(sem("sc_ps"), 4 * i + hd + 1)
                    if i:
                        dve.wait_ge(sem("o_ps"), i)
                    nc.vector.tensor_tensor(masked[0:n, hd, :].rearrange("p (d c) -> p d c", d=2)[:, :, 0:n],
                                            B[2 + hd][0:n, 0:256].rearrange("p (d c) -> p d c", d=2)[:, :, 0:n],
                                            fwd_bwd[0:n, :].rearrange("p (d c) -> p d c", d=2)[:, :, 0:n], ALU.mult).then_inc(sem("masked"), 1)

            def head_norm(i, t):
                n = TILE_N[t]
                dve.wait_ge(sem("o_ss"), 4 * i + 4)
                nc.vector.tensor_scalar(oss[0:n, i, 1, :], oss[0:n, i, 0, :], 1.0 / DV, EPS, ALU.mult, ALU.add).then_inc(sem("o_var"), 1)
                dve.wait_ge(sem("o_std"), i + 1)
                link(nc.vector.reciprocal(oss[0:n, i, 3, :], oss[0:n, i, 2, :]))
                dve.wait_ge(sem("rs_ready"), 3)
                for hd in range(HEADS):
                    src = B[[6, 0, 6][i] + hd % 2][0:n, (hd // 2) * DV:(hd // 2 + 1) * DV]
                    nc.vector.scalar_tensor_tensor(yb[0:n, t, hd * DV:(hd + 1) * DV], src, oss[0:n, i, 3, hd:hd + 1],
                                                   rs[0:n, t, hd * DV:(hd + 1) * DV], ALU.mult, ALU.mult).then_inc(sem("yb_ready"), 1)
            mask_scores(0, 1)
            head_norm(0, 1)
            mask_scores(1, 2)
            head_norm(1, 2)
            mask_scores(2, 0)
            head_norm(2, 0)
            for half in range(2):
                for t in range(3):
                    n = TILE_N[t]
                    k = 3 * half + t
                    dve.wait_ge(sem("proj_ps"), PROJ["out0"] + k + 1)
                    hh = h[0:n, t, half * W:(half + 1) * W]
                    nc.vector.tensor_tensor(hh, B[[2, 3, 4, 5, 0, 1][k]][0:n, :], hh, ALU.add).then_inc(sem("h_mixed0"), 1)

            def moe(l):
                n = 1 + 2 * l
                tiles = NORM_TILES[n]
                a, b = tiles[0], tiles[-1] + 1
                NT = b - a
                norm(n)
                transposes_out(n)
                dve.wait_ge(sem(f"route_in{l}"), 64)
                link(nc.vector.memset(padded[:, :, :].rearrange("p a b -> p (a b)"), -3.0e38))
                dve.wait_ge(sem("logitsT_ps"), l + 1)
                nc.vector.tensor_copy(logitsT[0:36, TILE_AT[a]:T], B[7][0:36, TILE_AT[a]:T]).then_inc(sem("logitsT"), 1)
                dve.wait_ge(sem("logits_ps"), l + 1)
                link(nc.vector.tensor_tensor(logits[:, a:b, :], B[6][:, 0:108].rearrange("p (t n) -> p t n", t=3)[:, a:b, :],
                                             b_route[:, l, :].unsqueeze(1).to_broadcast([P, NT, 36]), ALU.add))
                link(nc.vector.tensor_copy(padded[:, a:b, 0:G], logits[:, a:b, 0:G]))
                for t in tiles:
                    link(nc.vector.max(top_g[:, t, :], padded[:, t, :]))
                nc.vector.tensor_tensor(expg[:, a:b, :], logits[:, a:b, 0:G], top_g[:, a:b, 0:1].to_broadcast([P, NT, G]),
                                        ALU.subtract).then_inc(sem("gl_shift"), 1)
                for t in tiles:
                    link(nc.vector.max_index(idx_g[:, t, :], top_g[:, t, :], padded[:, t, :]))
                gidx = rstat[:, 0, a:b]
                link(nc.vector.tensor_copy(gidx.unsqueeze(2), idx_g[:, a:b, 0:1]))
                link(nc.vector.tensor_tensor(onehot[:, a:b, :], iota[:, 0:G].unsqueeze(1).to_broadcast([P, NT, G]),
                                             gidx.unsqueeze(2).to_broadcast([P, NT, G]), ALU.is_equal))
                nc.vector.tensor_tensor(onehot[:, a:b, :], onehot[:, a:b, :], valid[:, a:b].unsqueeze(2).to_broadcast([P, NT, G]),
                                        ALU.mult).then_inc(sem("onehot"), 1)
                dve.wait_ge(sem("onehot"), l + 1)
                link(nc.vector.tensor_tensor(picked[:, a:b, :, :], logits[:, a:b, G:36].rearrange("p t (g e) -> p t g e", g=G),
                                             onehot[:, a:b, :].unsqueeze(3).to_broadcast([P, NT, G, EPG]), ALU.mult))
                link(nc.vector.tensor_reduce(esel[:, a:b, :], picked[:, a:b, :, :].rearrange("p t g e -> p t e g"), X, ALU.add))
                for t in tiles:
                    link(nc.vector.max(top_e[:, t, :], esel[:, t, :]))
                nc.vector.tensor_tensor(rstat[:, 3, a:b].unsqueeze(2), top_e[:, a:b, 1:2], top_e[:, a:b, 0:1],
                                        ALU.subtract).then_inc(sem("top_diff"), 1)
                for t in tiles:
                    link(nc.vector.max_index(idx_e[:, t, :], top_e[:, t, :], esel[:, t, :]))
                link(nc.vector.tensor_copy(rstat[:, 1:3, a:b], idx_e[:, a:b, 0:2].rearrange("p t k -> p k t")))
                dve.wait_ge(sem("gl_exp"), l + 1)
                link(nc.vector.tensor_reduce(rstat[:, 5, a:b], expg[:, a:b, :], X, ALU.add))
                link(nc.vector.reciprocal(rstat[:, 5, a:b], rstat[:, 5, a:b]))
                dve.wait_ge(sem("top_exp"), l + 1)
                link(nc.vector.tensor_scalar(rstat[:, 6, a:b], rstat[:, 4, a:b], 1.0, None, ALU.add))
                link(nc.vector.reciprocal(rstat[:, 6, a:b], rstat[:, 6, a:b]))
                link(nc.vector.tensor_tensor(rstat[:, 6, a:b], rstat[:, 6, a:b], rstat[:, 5, a:b], ALU.mult))
                link(nc.vector.tensor_tensor(rstat[:, 7, a:b], rstat[:, 6, a:b], rstat[:, 4, a:b], ALU.mult))
                iota8 = iota[:, 0:EPG].unsqueeze(1).to_broadcast([P, NT, EPG])
                for k, dst in ((0, gates), (1, gtmp)):
                    link(nc.vector.tensor_tensor(dst[:, a:b, :], iota8, rstat[:, 1 + k, a:b].unsqueeze(2).to_broadcast([P, NT, EPG]), ALU.is_equal))
                    link(nc.vector.tensor_tensor(dst[:, a:b, :], dst[:, a:b, :], rstat[:, 6 + k, a:b].unsqueeze(2).to_broadcast([P, NT, EPG]), ALU.mult))
                nc.vector.tensor_tensor(gates[:, a:b, :], gates[:, a:b, :], gtmp[:, a:b, :], ALU.add).then_inc(sem("gates"), 1)
                dve.wait_ge(sem("rank_ps"), l + 1)
                link(nc.vector.tensor_tensor(expg[:, a:b, :], B[7][:, 0:12].rearrange("p (t g) -> p t g", t=3)[:, a:b, :], onehot[:, a:b, :], ALU.mult))
                link(nc.vector.tensor_reduce(rstat[:, 8, a:b], expg[:, a:b, :], X, ALU.add))
                link(nc.vector.tensor_reduce(rstat[:, 9, 0:1], B[7][:, 16:20], X, ALU.max))
                link(nc.vector.tensor_scalar(rstat[:, 9, 1:2], rstat[:, 9, 0:1], float(P), float(G), ALU.is_gt, ALU.mult))
                link(nc.vector.tensor_scalar(rstat[:, 9, 2:3], rstat[:, 9, 0:1], float(2 * P), float(G), ALU.is_gt, ALU.mult))
                link(nc.vector.tensor_tensor(rstat[:, 9, 1:2], rstat[:, 9, 1:2], rstat[:, 9, 2:3], ALU.add))
                if l == 0:
                    link(nc.vector.tensor_scalar(n_iter[:, 2:3], rstat[:, 9, 1:2], float(G - 1), None, ALU.add))
                nc.vector.tensor_scalar(n_iter[:, l:l + 1], rstat[:, 9, 1:2], float(G), None, ALU.add).then_inc(sem("n_iter_ready"), 1)
                link(nc.vector.tensor_scalar(rstat[:, 10, a:b], rstat[:, 8, a:b], float(P), float((G - 1) * P), ALU.is_ge, ALU.mult))
                link(nc.vector.tensor_scalar(rstat[:, 11, a:b], rstat[:, 8, a:b], float(2 * P), float((G - 1) * P), ALU.is_ge, ALU.mult))
                link(nc.vector.tensor_tensor(rstat[:, 10, a:b], rstat[:, 10, a:b], rstat[:, 11, a:b], ALU.add))
                link(nc.vector.tensor_tensor(rstat[:, 10, a:b], rstat[:, 10, a:b], rstat[:, 8, a:b], ALU.add))
                link(nc.vector.scalar_tensor_tensor(key[:, a:b], gidx, float(P), rstat[:, 10, a:b], ALU.mult, ALU.add))
                link(nc.vector.scalar_tensor_tensor(key[:, a:b], key[:, a:b], 1.0, valid[:, a:b], ALU.add, ALU.mult))
                nc.vector.tensor_scalar(key[:, a:b], key[:, a:b], -1.0, None, ALU.add).then_inc(sem(f"key{l}"), 1)
                dve.wait_ge(sem("n_iter_ready"), l + 1)
                n_it = dve.value_load(n_iter[0:1, l:l + 1], min_val=G, max_val=3 * G)
                nadd = 2 * NT
                for name in ("he_ready", "h_added", "y_dve", "selT", "heT"):
                    dve.sem_inc(sem(f"{name}{l}"), PRIMED)
                with dve.Fori(0, n_it) as it:
                    dve.wait_ge(sem(f"key{l}"), it + 1)
                    nc.vector.tensor_tensor(sel[:, a:b, :], iota.unsqueeze(1).to_broadcast([P, NT, P]),
                                            key[:, a:b].unsqueeze(2).to_broadcast([P, NT, P]), ALU.is_equal).then_inc(sem(f"sel{l}"), 1)
                    dve.wait_ge(sem(f"sel{l}"), it + 1)
                    nc.vector.tensor_scalar(key[:, a:b], key[:, a:b], -float(P), None, ALU.add).then_inc(sem(f"key{l}"), 1)
                    todo = 0
                    while todo < 3:
                        todo = lower_weights(l, it, todo)
                    for half in range(2):
                        dve.wait_ge(sem(f"x_hi{l}"), 2 * it + half + 1)
                        part = slice(4 * half, 4 * half + 4)
                        nc.vector.tensor_tensor(x_lo[:, part, :], B[half][:, :].rearrange("p (c n) -> p c n", c=4),
                                                x_hi[:, part, :].bitcast(f32), ALU.subtract).then_inc(sem(f"x_lo{l}"), 1)
                    dve.wait_ge(sem(f"sg_ps{l}"), it + 1)
                    nc.vector.tensor_copy(slot_gates[:, :], B[7][:, 0:EPG]).then_inc(sem(f"slot_gates{l}"), 1)
                    nc.vector.tensor_copy(selT[:, TILE_AT[a]:T], B[7][:, 64 + TILE_AT[a]:64 + T]).then_inc(sem(f"selT{l}"), 1)
                    dve.wait_ge(sem(f"slot_gates{l}"), it + 1)
                    for e in range(EPG):
                        while todo < NU and todo - BUFS <= AT["gu", e, 1]:
                            if todo - BUFS == AT["gu", e, 0] and e >= 2:
                                heT_low(l, it, e - 2)
                            todo = lower_weights(l, it, todo)
                        dve.wait_ge(sem(f"silu{l}"), it * EPG + e + 1)
                        if e >= 2:
                            dve.wait_ge(sem(f"heT_ps{l}"), it * EPG + e - 1)
                        nc.vector.scalar_tensor_tensor(he[:, e % 2, :], act_g[:, e % 2, :], slot_gates[:, e:e + 1], B[2 + e % 2][:, F:2 * F],
                                                       ALU.mult, ALU.mult).then_inc(sem(f"he_ready{l}"), 1)
                    for e in (EPG - 2, EPG - 1):
                        heT_low(l, it, e)
                    dve.wait_ge(sem(f"w_used{l}"), used(it, "d", EPG - 1))
                    nc.vector.tensor_copy(ysum[:, W:D], B[6][:, :]).then_inc(sem(f"y_dve{l}"), 1)
                    for k in range(nadd):
                        half, t = k // NT, tiles[k % NT]
                        n = TILE_N[t]
                        dve.wait_ge(sem(f"sc_ps{l}"), it * nadd + k + 1)
                        if k == 0:
                            dve.wait_ge(sem(f"h_added{l}"), PRIMED + it * nadd)
                        hh = h[0:n, t, half * W:(half + 1) * W]
                        nc.vector.tensor_tensor(hh, B[k % 2][0:n, :], hh, ALU.add).then_inc(sem(f"h_added{l}"), 1)
                dve.wait_ge(sem(f"h_added{l}"), PRIMED + n_it * nadd)
                dve.sem_inc(sem("h_moe"), 1)

            def lower_weights(l, it, j):
                if j not in POOL_UNITS:
                    subtract(dve, nc.vector, l, it, j)
                return j + 1

            def heT_low(l, it, e):
                dve.wait_ge(sem(f"heT_hi{l}"), it * EPG + e + 1)
                nc.vector.tensor_tensor(heT_lo[:, e % 2, :, :], B[4][:, 0:2 * P].rearrange("p (c n) -> p c n", c=2),
                                        heT_hi[:, e % 2, :, :].bitcast(f32), ALU.subtract).then_inc(sem(f"heT{l}"), 1)

            moe(0)

            norm(2)
            transposes_out(2)
            dve.wait_ge(sem("att_params_in"), 48)
            dve.wait_ge(sem("att_params_in"), 48)

            def head_rms(src, sq, nh, nth, scale, gn):
                nt = src.shape[1]
                flat = src.rearrange("p t h d -> p (t h) d")
                nht = nt * nh
                link(nc.vector.tensor_tensor(sq[:, 0:nht, :], flat, flat, ALU.mult))
                link(nc.vector.tensor_reduce(hstat[:, 0, 0:nht], sq[:, 0:nht, :], X, ALU.add))
                nc.vector.tensor_scalar(hstat[:, 1, 0:nht], hstat[:, 0, 0:nht], 1.0 / HD, EPS, ALU.mult, ALU.add).then_inc(sem("head_var"), 1)
                dve.wait_ge(sem("head_std"), nth)
                link(nc.vector.reciprocal(hstat[:, 3, 0:nht], hstat[:, 2, 0:nht]))
                link(nc.vector.tensor_tensor(flat, flat, hstat[:, 3, 0:nht].unsqueeze(2).to_broadcast([P, nht, HD]), ALU.mult))
                link(nc.vector.scalar_tensor_tensor(flat, flat, scale, gn.unsqueeze(1).to_broadcast([P, nht, HD]), ALU.mult, ALU.mult))

            def rotate(x, dst, t, nh, ta, tb, name):
                x0, x1 = x[:, :, 0:HD:2], x[:, :, 1:HD:2]
                c = rope[:, 0, t, :].unsqueeze(1).to_broadcast([P, nh, 32])
                s = rope[:, 1, t, :].unsqueeze(1).to_broadcast([P, nh, 32])
                nc.vector.tensor_tensor(ta[:, 0:nh, 0:32], x0, c, ALU.mult)
                nc.vector.tensor_tensor(ta[:, 0:nh, 32:64], x1, s, ALU.mult)
                nc.vector.tensor_tensor(tb[:, 0:nh, 0:32], x0, s, ALU.mult)
                link(nc.vector.tensor_tensor(tb[:, 0:nh, 32:64], x1, c, ALU.mult))
                nc.vector.tensor_tensor(dst[:, :, 0:HD:2], ta[:, 0:nh, 0:32], ta[:, 0:nh, 32:64], ALU.subtract)
                link(nc.vector.tensor_tensor(dst[:, :, 1:HD:2], tb[:, 0:nh, 0:32], tb[:, 0:nh, 32:64], ALU.add))

            sq = qtmp[:, :, :].rearrange("p i (h d) -> p (i h) d", d=HD)
            dve.wait_ge(sem("kv_raw"), 6)
            head_rms(ks[:, :, :, :], sq, KVH, 1, 1.0, qk_gain[:, 1, :])
            for t in range(3):
                rotate(ks[:, t, :, :], ks2[:, t, :, 0:HD], t, KVH, sq[:, 0:16, :], sq[:, 16:32, :], "k")
                nc.vector.tensor_copy(ks2[:, t, :, HD:2 * HD], ks2[:, t, :, 0:HD]).then_inc(sem("k_rot"), 1)
            dve.wait_ge(sem("q_raw"), 4)
            head_rms(qs[:, :, :, :], sq, QH, 2, HD ** -0.5, qk_gain[:, 0, :])
            for i in range(2):
                rotate(qs[:, i, :, :], qs[:, i, :, :], 1 + i, QH, sq[:, 0:16, :], sq[:, 16:32, :], "q")
                dve.sem_inc(sem("q_rot"), 1)

            def maxima(u):
                for o in range(2):
                    dve.wait_ge(sem("s_ps"), 2 * u + o + 1)
                    nc.vector.tensor_reduce(att_max[:, 2 * u + o:2 * u + o + 1], B[2 * (u % 2) + o][:, 0:T], X, ALU.max, negate=True).then_inc(sem("s_max"), 1)

            def normalise(u):
                dve.wait_ge(sem("p_exp"), 2 * u + 2)
                link(nc.vector.reciprocal(att_rcp[:, 2 * u:2 * u + 2], att_sum[:, 2 * u:2 * u + 2]))
                for o in range(2):
                    pr = probs[:, 2 * (u % 2) + o, :]
                    nc.vector.tensor_scalar(pr, pr, att_rcp[:, 2 * u + o:2 * u + o + 1], None, ALU.mult).then_inc(sem("p_ready"), 1)

            def out_of_psum(u):
                dve.wait_ge(sem("pT_ps"), u + 1)
                if u >= 2:
                    dve.wait_ge(sem("oT_ps"), u - 1)
                nc.vector.tensor_copy(pTm[0:NM, u % 2, :, :], B[6][0:NM, 0:2 * P].rearrange("p (o n) -> p o n", o=2)).then_inc(sem("pTm_ev"), 1)

            def oT_out(u):
                i, pair = u // 8, u % 8
                dve.wait_ge(sem("oT_ps"), u + 1)
                nc.vector.tensor_copy(oT[:, pair, i * P:(i + 1) * P], B[7][:, 0:P]).then_inc(sem("oT_ev"), 1)

            maxima(0)
            for u in range(16):
                if u < 15:
                    maxima(u + 1)
                normalise(u)
                out_of_psum(u)
                if u:
                    oT_out(u - 1)
            oT_out(15)
            for half in range(2):
                for i in range(2):
                    k = 2 * half + i
                    dve.wait_ge(sem("proj_ps"), PROJ["out1"] + k + 1)
                    hh = h[:, 1 + i, half * W:(half + 1) * W]
                    nc.vector.tensor_tensor(hh, B[k][:, :], hh, ALU.add).then_inc(sem("h_mixed1"), 1)
            moe(1)
            norm(4)

        @block.tensor
        def _(pe):
            mm = nc.tensor.matmul

            def transposes(n):
                for i, t in enumerate(NORM_TILES[n]):
                    m = TILE_N[t]
                    pe.wait_ge(sem("hn_ready"), upto(n) + i + 1)
                    if i == 0:
                        pe.wait_ge(sem("consts_in"), 16)
                    for half in range(2):
                        if i:
                            pe.wait_ge(sem(f"hnT_{('act', 'dve')[half]}"), upto(n) + i)
                        for c in range(4):
                            last = nc.tensor.transpose(B[half][:, c * P:c * P + m], hn[0:m, t, 4 * half + c:D:KC], ident[0:m, 0:m])
                        last.then_inc(sem("hnT_ps"), 1)

            def block_ready(l, b):
                for half in range(2):
                    slots = [x % RING for x in range(2 * NMIX[0])] if l else []
                    slots += [(MIX_SLOT0[l] + x) % RING for x in range(2 * b + half + 1)]
                    pe.wait_ge(sem(f"mix_w{slots[-1]}"), 16 * slots.count(slots[-1]))
                s = MIX_SLOT0[l] + 2 * b
                return lambda c, lo, hi: raw[(s + c // 4) % RING][:, c % 4 * W + lo:c % 4 * W + hi]

            transposes(0)
            wait_hnT(pe, 0)
            pe.wait_ge(sem("w_g_in"), 16)
            for c in range(KC):
                last = mm(B[2][0:2 * RANK, 0:T], w_g_in[:, c, :], hnT[:, c, :], start=(c == 0), stop=(c == KC - 1))
            last.then_inc(sem("proj_ps"), 1)

            def feature_major(w, m, bank):
                for c in range(KC):
                    last = mm(bank[:, 0:T], w(c, m * P, (m + 1) * P), hnT[:, c, :], start=(c == 0), stop=(c == KC - 1))
                last.then_inc(sem("proj_ps"), 1)
                return last

            def token_major(w, t, lo, hi, bank, rows=None):
                n = rows or TILE_N[t]
                for c in range(KC):
                    last = mm(bank[0:n, 0:hi - lo], hnT[:, c, TILE_AT[t]:TILE_AT[t] + n], w(c, lo, hi), start=(c == 0), stop=(c == KC - 1))
                last.then_inc(sem("proj_ps"), 1)
                return last

            w = block_ready(0, 0)
            for m in range(2):
                feature_major(w, m, B[3 + m])
            for t in range(3):
                token_major(w, t, 256, 512, B[5 + t])
            pe.wait_ge(sem("g_ev"), 1)
            pe.wait_ge(sem("gla_params_in"), 128)
            for t in range(3):
                n = TILE_N[t]
                mm(B[t][0:n, :], gT[:, TILE_AT[t]:TILE_AT[t] + n], wgate[:, :], start=True, stop=True).then_inc(sem("la_ps"), 1)
            w = block_ready(0, 1)
            for t in range(3):
                pe.wait_ge(sem("q_ev"), t + 1) if t < 2 else pe.wait_ge(sem("k_ev"), 1)
                token_major(w, t, 0, W, B[3 + t])
            pe.wait_ge(sem("k_ev"), 3)
            for m in range(2):
                for t in range(3):
                    n = TILE_N[t]
                    last = nc.tensor.transpose(B[6 + m][:, TILE_AT[t]:TILE_AT[t] + n], ktok[0:n, t, m * P:(m + 1) * P], ident[0:n, 0:n])
                last.then_inc(sem("kT_ps"), 1)
            w = block_ready(0, 2)
            for t in range(3):
                pe.wait_ge(sem("v_ev"), t + 1)
                token_major(w, t, 0, W, B[3 + t])
            w = block_ready(0, 3)
            for m in range(4):
                pe.wait_ge(sem("kT_ev"), m + 1) if m < 2 else pe.wait_ge(sem("ax_ev"), m - 1)
                feature_major(w, m, B[6 + m % 2])
            pe.wait_ge(sem("la_ready"), 3)
            for dm in range(4):
                if dm == 3:
                    pe.wait_ge(sem("r_ev"), 1)
                for t in range(3):
                    n = TILE_N[t]
                    last = mm(B[dm][:, TILE_AT[t]:TILE_AT[t] + n], la[0:n, t, dm * P:(dm + 1) * P],
                              (incl_fwd, incl_bwd)[dm // 2][0:n, 0:n], start=True, stop=True)
                last.then_inc(sem("cum_ps"), 1)
            for t in range(3):
                n = TILE_N[t]
                bank = B[[4, 5, 0][t]]
                pe.wait_ge(sem("r_ev"), t + 2) if t < 2 else pe.wait_ge(sem("E_exp"), 2)
                mm(bank[0:n, 0:256], strict_bwd[0:n, 0:n], la[0:n, t, 0:256], start=True, stop=True)
                mm(bank[0:n, 256:512], strict_fwd[0:n, 0:n], la[0:n, t, 256:512], start=True, stop=True).then_inc(sem("kend_ps"), 1)
            w = block_ready(0, 4)
            for m in range(4):
                pe.wait_ge(sem("ax_ev"), m + 3) if m < 2 else pe.wait_ge(sem("z_ready"), m - 1)
                feature_major(w, m, B[6 + m % 2])
            w = block_ready(0, 5)
            for m in range(4):
                pe.wait_ge(sem("z_ready"), m + 3) if m < 2 else pe.wait_ge(sem("ya_ready"), m - 1)
                feature_major(w, m, B[6 + m % 2])
            pe.wait_ge(sem("kend"), 6)
            pe.wait_ge(sem("E_exp"), 8)
            pe.wait_ge(sem("v_ev"), 3)
            for k in range(8):
                d, i = k % 2, k // 2
                t, p0, n = CHUNKS[i if d == 0 else 4 - i]
                if k >= 6:
                    pe.wait_ge(sem("state"), 4 * (k - 5))
                bank = B[[1, 2, 3, 4, 5, 0, 1, 2][k]]
                for m in range(2):
                    last = mm(bank[:, 256 * m:256 * m + 256], kend[p0:p0 + n, t, 256 * d + P * m:256 * d + P * (m + 1)],
                              v[p0:p0 + n, t, 256 * m:256 * m + 256], start=True, stop=True)
                last.then_inc(sem("kvs_ps"), 1)
            pe.wait_ge(sem("state"), 32)
            pe.wait_ge(sem("qk_dec"), 4)

            def scores(i, t):
                n = TILE_N[t]
                at = TILE_AT[t]
                for hd in range(HEADS):
                    m, rows = hd // 2, slice(64 * (hd % 2), 64 * (hd % 2) + 64)
                    if i:
                        pe.wait_ge(sem("masked"), 4 * (i - 1) + hd + 1)
                    for d in range(2):
                        last = mm(B[2 + hd][0:n, d * P:d * P + n], Ei[rows, 2 * d + m, at:at + n], E[rows, 2 * d + m, at:at + n], start=True, stop=True)
                    last.then_inc(sem("sc_ps"), 1)

            def outputs(i, t):
                n = TILE_N[t]
                at = TILE_AT[t]
                base = [6, 0, 6][i]
                if i == 0:
                    pe.wait_ge(sem("ya_ready"), 4)
                if i == 2:
                    pe.wait_ge(sem("ybT_ev"), 1)
                for hd in range(HEADS):
                    m, hh = hd // 2, hd % 2
                    o = B[base + hh]
                    pe.wait_ge(sem("masked"), 4 * i + hd + 1)
                    for d in range(2):
                        mm(o[0:n, m * DV:(m + 1) * DV], masked[0:n, hd, d * P:d * P + n], v[0:n, t, hd * DV:(hd + 1) * DV],
                           start=(m == 0 and d == 0), stop=False, skip_group_check=True)
                for hd in range(HEADS):
                    m, hh = hd // 2, hd % 2
                    o = B[base + hh]
                    rows = slice(64 * hh, 64 * hh + 64)
                    for j, (tt, p0, cn) in enumerate(CHUNKS):
                        if tt != t:
                            continue
                        for d, prev in ((0, j - 1), (1, 3 - j)):
                            if 0 <= prev <= 3:
                                last = mm(o[p0:p0 + cn, m * DV:(m + 1) * DV], E[rows, 2 * d + m, at + p0:at + p0 + cn],
                                          state[rows, 4 * d + prev, m, :], start=False, stop=True, skip_group_check=True)
                last.then_inc(sem("o_ps"), 1)

            def yb_transposes(i, t):
                n = TILE_N[t]
                pe.wait_ge(sem("yb_ready"), 4 * i + 4)
                for hd in range(HEADS):
                    last = nc.tensor.transpose(B[[6, 0, 6][i]][:, hd * P:hd * P + n], yb[0:n, t, hd * P:(hd + 1) * P], ident[0:n, 0:n])
                last.then_inc(sem("ybT_ps"), 1)

            scores(0, 1)
            outputs(0, 1)
            scores(1, 2)
            outputs(1, 2)
            yb_transposes(0, 1)
            scores(2, 0)
            outputs(2, 0)
            yb_transposes(1, 2)
            yb_transposes(2, 0)
            pe.wait_ge(sem("ybT_ev"), 3)
            pe.wait_ge(sem("ya_ready"), 4)
            for half in range(2):
                w = block_ready(0, 6 + half)
                for t in range(3):
                    n = TILE_N[t]
                    for c in range(KC):
                        last = mm(B[[2, 3, 4, 5, 0, 1][3 * half + t]][0:n, :], yT[:, c, TILE_AT[t]:TILE_AT[t] + n], w(c, 0, W),
                                  start=(c == 0), stop=(c == KC - 1))
                    last.then_inc(sem("proj_ps"), 1)

            def moe(l):
                n = 1 + 2 * l
                tiles = NORM_TILES[n]
                a, b = tiles[0], tiles[-1] + 1
                NT = b - a
                transposes(n)
                wait_hnT(pe, n)
                pe.wait_ge(sem(f"route_in{l}"), 64)
                for c in range(KC):
                    last = mm(B[7][0:36, TILE_AT[a]:T], w_route[l][:, c, :], hnT[:, c, TILE_AT[a]:T], start=(c == 0), stop=(c == KC - 1))
                last.then_inc(sem("logitsT_ps"), 1)
                pe.wait_ge(sem("logitsT"), l + 1)
                for t in tiles:
                    last = nc.tensor.transpose(B[6][:, 36 * t:36 * t + 36], logitsT[0:36, TILE_AT[t]:TILE_AT[t] + P], ident[0:36, 0:36])
                last.then_inc(sem("logits_ps"), 1)
                pe.wait_ge(sem("onehot"), l + 1)
                for t in tiles:
                    for s in range(a, t + 1):
                        mm(B[7][:, 4 * t:4 * t + 4], before if s == t else ones, onehot[:, s, :], start=(s == a), stop=(s == t))
                for s in tiles:
                    last = mm(B[7][:, 16:20], ones, onehot[:, s, :], start=(s == a), stop=(s == b - 1))
                last.then_inc(sem("rank_ps"), 1)
                pe.wait_ge(sem("gates"), l + 1)
                pe.wait_ge(sem("n_iter_ready"), l + 1)
                n_it = pe.value_load(n_iter[0:1, l:l + 1], min_val=G, max_val=3 * G)
                nadd = 2 * NT

                def split_product(dst, left_hi, left_lo, right, j, first, last_one):
                    w_high, w_low = right
                    mm(dst, left_hi, w_high, start=first, stop=False)
                    mm(dst, left_lo, w_high, start=False, stop=False)
                    return mm(dst, left_hi, w_low, start=False, stop=last_one)

                def wait_split(it, j):
                    name, count, per = low_done(j)
                    pe.wait_ge(sem(f"{name}{l}"), it * per + count)

                def gate_up(it, e):
                    if e < 2:
                        pe.wait_ge(sem(f"he_ready{l}"), PRIMED + it * EPG)
                    else:
                        pe.wait_ge(sem(f"he_ready{l}"), PRIMED + it * EPG + e - 1)
                    for half in range(2):
                        j = AT["gu", e, half]
                        wait_split(it, j)
                        parts = [w[j % BUFS][:, :].rearrange("p (u c n) -> p u c n", u=2, c=4) for w in (w_hi, w_lo)]
                        for cc in range(4):
                            c = 4 * half + cc
                            last = split_product(B[2 + e % 2][:, :], x_hi[:, c, :], x_lo[:, c, :], [w[:, :, cc, :] for w in parts], j,
                                                 c == 0, c == KC - 1)
                        last.then_inc(sem(f"w_used{l}"), 1)

                def he_transposes(it, e):
                    pe.wait_ge(sem(f"he_ready{l}"), PRIMED + it * EPG + e + 1)

                    pe.wait_ge(sem(f"heT{l}"), PRIMED + it * EPG + e)
                    for c in range(2):
                        last = nc.tensor.transpose(B[4][:, c * P:(c + 1) * P], he[:, e % 2, c:F:2], ident)
                    last.then_inc(sem(f"heT_ps{l}"), 1)

                def down(it, e):
                    pe.wait_ge(sem(f"heT{l}"), PRIMED + it * EPG + e + 1)
                    j = AT["d", e, 0]
                    wait_split(it, j)
                    if e == 0:
                        pe.wait_ge(sem(f"y_act{l}"), PRIMED + it)
                        pe.wait_ge(sem(f"y_dve{l}"), PRIMED + it)
                    for half in range(2):
                        for c in range(2):
                            at = c * D + half * W
                            last = split_product(B[5 + half][:, :], heT_hi[:, e % 2, c, :], heT_lo[:, e % 2, c, :],
                                                 [w[j % BUFS][:, at:at + W] for w in (w_hi, w_lo)], j,
                                                 e == 0 and c == 0, e == EPG - 1 and c == 1)
                    last.then_inc(sem(f"w_used{l}"), 1)

                pe.sem_inc(sem(f"w_used{l}"), BUFS)
                with pe.Fori(0, n_it) as it:
                    pe.wait_ge(sem(f"sel{l}"), it + 1)
                    pe.wait_ge(sem(f"h_added{l}"), PRIMED + it * nadd)
                    for half in range(2):
                        for c in range(4):
                            for t in tiles:
                                m = TILE_N[t]
                                last = mm(B[half][:, c * P:(c + 1) * P], hn[0:m, t, 4 * half + c:D:KC], sel[0:m, t, :],
                                          start=(t == a), stop=(t == b - 1))
                        last.then_inc(sem(f"x_ps{l}"), 1)
                    pe.wait_ge(sem(f"selT{l}"), PRIMED + it)
                    for t in tiles:
                        m = TILE_N[t]
                        mm(B[7][:, 0:EPG], sel[0:m, t, :], gates[0:m, t, :], start=(t == a), stop=(t == b - 1))
                    for t in tiles:
                        m = TILE_N[t]
                        last = nc.tensor.transpose(B[7][:, 64 + TILE_AT[t]:64 + TILE_AT[t] + m], sel[0:m, t, :], ident[0:m, 0:m])
                    last.then_inc(sem(f"sg_ps{l}"), 1)
                    pe.wait_ge(sem(f"x_lo{l}"), 2 * it + 2)
                    gate_up(it, 0)
                    gate_up(it, 1)
                    for e in range(EPG):
                        he_transposes(it, e)
                        if e + 2 < EPG:
                            gate_up(it, e + 2)
                        down(it, e)
                    pe.wait_ge(sem(f"selT{l}"), PRIMED + it + 1)
                    pe.wait_ge(sem(f"y_act{l}"), PRIMED + it + 1)
                    pe.wait_ge(sem(f"y_dve{l}"), PRIMED + it + 1)
                    for k in range(nadd):
                        half, t = k // NT, tiles[k % NT]
                        m = TILE_N[t]
                        if k >= 2:
                            pe.wait_ge(sem(f"h_added{l}"), PRIMED + it * nadd + k - 1)
                        mm(B[k % 2][0:m, :], selT[:, TILE_AT[t]:TILE_AT[t] + m], ysum[:, half * W:(half + 1) * W],
                           start=True, stop=True).then_inc(sem(f"sc_ps{l}"), 1)

            moe(0)

            transposes(2)
            wait_hnT(pe, 2)
            w = block_ready(1, 0)
            for t in range(3):
                token_major(w, t, 0, W, B[2 + t], rows=P)
            for n in range(2):
                w = block_ready(1, 1 + n)
                for i in range(2):
                    token_major(w, 1 + i, 0, W, B[[5, 6, 7, 0][2 * n + i]])
            pe.wait_ge(sem("k_rot"), 3)
            pe.wait_ge(sem("kv_raw"), 6)
            for hv in range(KVH):
                for t in range(3):
                    m = TILE_N[t]
                    last = nc.tensor.transpose(B[[1, 2, 3, 4][hv]][:, TILE_AT[t]:TILE_AT[t] + m], ks2[0:m, t, hv, :], ident[0:m, 0:m])
                last.then_inc(sem("qk1T_ps"), 1)
            pe.wait_ge(sem("q_raw"), 4)
            for i in range(2):
                pe.wait_ge(sem("q_rot"), i + 1)
                for m in range(2):
                    for c in range(4):
                        pair = 4 * m + c
                        last = nc.tensor.transpose(B[[5, 6, 7, 0][2 * i + m]][:, c * P:(c + 1) * P],
                                                   qs[:, i, 2 * pair:2 * pair + 2, :].rearrange("p h d -> p (h d)"), ident)
                    last.then_inc(sem("qk1T_ps"), 1)
            pe.wait_ge(sem("qk1T_ev"), KVH + 4)

            def att_scores(u):
                i, pair = u // 8, u % 8
                if u >= 2:
                    pe.wait_ge(sem("p_exp"), 2 * (u - 1))
                for o in range(2):
                    rows = slice(64 * o, 64 * o + 64)
                    mm(B[2 * (u % 2) + o][:, 0:T], qT1[rows, pair, i * P:(i + 1) * P], kT1[rows, pair // 2, :],
                       start=True, stop=True).then_inc(sem("s_ps"), 1)

            att_scores(0)
            for u in range(16):
                i, pair = u // 8, u % 8
                hv = pair // 2
                if u < 15:
                    att_scores(u + 1)
                pe.wait_ge(sem("p_ready"), 2 * u + 2)
                if u >= 2:
                    pe.wait_ge(sem("pT_ev"), u - 1)
                for o in range(2):
                    for t in (1, 2):
                        last = nc.tensor.transpose(B[4 + u % 2][:, (2 * o + t - 1) * P:(2 * o + t) * P],
                                                   probs[:, 2 * (u % 2) + o, TILE_AT[t]:TILE_AT[t] + P], ident)
                if u:
                    pe.wait_ge(sem("pTm_ev"), u)
                for o in range(2):
                    last = nc.tensor.transpose(B[6][0:NM, o * P:(o + 1) * P], probs[:, 2 * (u % 2) + o, 0:NM], ident)
                last.then_inc(sem("pT_ps"), 1)
                pe.wait_ge(sem("pT_ev"), u + 1)
                pe.wait_ge(sem("pTm_ev"), u + 1)
                if u:
                    pe.wait_ge(sem("oT_ev"), u)
                for o in range(2):
                    dst = B[7][64 * o:64 * o + 64, 0:P]
                    mm(dst, vs[:, 1, hv * HD:(hv + 1) * HD], pT[:, u % 2, 2 * o, :], start=True, stop=False)
                    mm(dst, vs[:, 2, hv * HD:(hv + 1) * HD], pT[:, u % 2, 2 * o + 1, :], start=False, stop=False)
                    last = mm(dst, vs[0:NM, 0, hv * HD:(hv + 1) * HD], pTm[0:NM, u % 2, o, :], start=False, stop=True)
                last.then_inc(sem("oT_ps"), 1)
            pe.wait_ge(sem("oT_ev"), 16)
            for half in range(2):
                w = block_ready(1, 3 + half)
                for i in range(2):
                    for c in range(KC):
                        last = mm(B[2 * half + i][:, :], oT[:, c, i * P:(i + 1) * P], w(c, 0, W), start=(c == 0), stop=(c == KC - 1))
                    last.then_inc(sem("proj_ps"), 1)
            moe(1)


_INS = ["x", "meta_tokens", "norm_mix", "norm_ffn", "norm_final", "sc_w_in", "sc_conv_w", "gla_w_gate_fwd",
        "gla_b_gate_fwd", "gla_w_gate_bwd", "gla_b_gate_bwd", "gla_norm_w", "sc_w_out", "att_w_in",
        "att_q_norm", "att_k_norm", "att_w_out", "moe_w_group", "moe_b_group", "moe_w_expert",
        "moe_b_expert", "moe_w_gate", "moe_w_up", "moe_w_down"]


def _constants():
    import numpy as np
    s, c = np.arange(128)[:, None], np.arange(128)[None, :]
    same = s // 64 == c // 64
    valid = np.ones((128, 3))
    valid[16:, 0] = 0
    parts = [s == c, same & (s <= c), same & (s > c), same & (s >= c), same & (s < c), s < c, s >= 0 * c, c + 0 * s, valid]
    consts = np.concatenate([np.broadcast_to(p, (128, p.shape[1])) for p in parts], axis=1).astype(np.float32)
    pos = np.arange(256)
    freqs = (np.float32(10000.0) ** (-np.arange(0, 32, 2, dtype=np.float32) / np.float32(32))).astype(np.float32)
    ang = np.concatenate([(pos // 64).astype(np.float32)[:, None] * freqs, (pos % 64).astype(np.float32)[:, None] * freqs], axis=1)
    ang = np.concatenate([np.zeros((128, 32), np.float32), ang]).astype(np.float32)
    table = np.stack([np.cos(ang), np.sin(ang)]).astype(np.float32).reshape(2, 3, 128, 32).transpose(2, 0, 1, 3)
    return np.ascontiguousarray(consts), np.ascontiguousarray(table.reshape(128, 192))


def kernel(**inputs):
    import numpy as _np
    import concourse.bacc as _bacc
    from concourse import mybir as _mybir
    from concourse.bass_utils import run_bass_kernel_spmd as _run

    nc = _bacc.Bacc("TRN2", target_bir_lowering=False, num_devices=1)
    given = {name: _np.ascontiguousarray(inputs[name]) for name in _INS}
    given["consts"], given["rope"] = _constants()
    arrays, args = {}, {}
    for name, a in given.items():
        arrays[f"in_{name}"] = a
        args[name] = nc.dram_tensor(f"in_{name}", a.shape, _mybir.dt.from_np(a.dtype), kind="ExternalInput").ap()
    shape = given["x"].shape
    out = nc.dram_tensor("out_0", shape, _mybir.dt.from_np(given["x"].dtype), kind="ExternalOutput").ap()
    build_program(nc, args, out)
    r = _run(nc, [arrays], core_ids=[0])
    return r.results[0]["out_0"]
```

```python
import concourse.bass as bass
from concourse import mybir
from contextlib import ExitStack


def build_program(nc: bass.Bass, A: dict, out: bass.AP):
    f32 = mybir.dt.float32
    f32r = mybir.dt.float32r
    u32 = mybir.dt.uint32
    i32 = mybir.dt.int32
    ALU = mybir.AluOpType
    ACT = mybir.ActivationFunctionType
    X = mybir.AxisListType.X

    P = 128
    SEQ, D = A["x"].shape[1], A["x"].shape[2]
    NM = A["meta_tokens"].shape[0]
    T = NM + SEQ
    KC = D // P
    TILE_AT = [0, NM, NM + P]
    TILE_N = [NM, P, P]
    HEADS, DV, DK, C = 4, 128, 64, 64
    RANK = A["gla_w_gate_fwd"].shape[1]
    QH, KVH, HD = 16, 4, 64
    G, EPG, F = 4, 8, 256
    EPS = 1e-6
    TAU = 16.0
    W = 512
    NORM_TILES = [[0, 1, 2], [0, 1, 2], [0, 1, 2], [1, 2], [1, 2]]
    CHUNKS = [(0, 0, NM), (1, 0, C), (1, C, C), (2, 0, C), (2, C, C)]
    MIX0_COLS = [3 * W, 4 * W, 5 * W, 2 * W, W, 0]
    MIX1_COLS = [0, 2 * W, W]
    NMIX = [len(MIX0_COLS) + 2, len(MIX1_COLS) + 2]
    UNIT = 2048
    RING = 8
    BUFS = 4
    MIX_BUFS = 3
    MIX_SLOT0 = [0, 2 * NMIX[0] % RING]
    MOE_SLOT0 = [2 * NMIX[0] % RING, 2 * (NMIX[0] + NMIX[1]) % RING]
    UNITS = [("gu", 0, 0), ("gu", 0, 1), ("gu", 1, 0), ("gu", 1, 1)]
    for e in range(EPG):
        if e + 2 < EPG:
            UNITS += [("gu", e + 2, 0), ("gu", e + 2, 1)]
        UNITS += [("d", e, 0)]
    NU = len(UNITS)
    AT = {u: j for j, u in enumerate(UNITS)}
    def used(it, kind, e, half=0):
        return it * NU + AT[kind, e, half] + 1 + BUFS

    POOL_UNITS = [j for j in range(NU) if j % 4 == 3 or j == 1]

    def low_done(j):
        mine = j in POOL_UNITS
        return ("lo_pool" if mine else "lo_dve"), sum((i in POOL_UNITS) == mine for i in range(j + 1)), \
            sum((i in POOL_UNITS) == mine for i in range(NU))

    def raw_count(j):
        same = [16 * (2 if UNITS[i][0] == "gu" else 1) * (i <= j) for i in range(j % RING, NU, RING)]
        return sum(same), sum(16 * (2 if UNITS[i][0] == "gu" else 1) for i in range(j % RING, NU, RING))
    PRIMED = 1

    ctx = ExitStack()
    with ctx:
        def sb(name, shape, dt=f32):
            return ctx.enter_context(nc.sbuf_tensor(name, shape, dt))

        made = {}

        def sem(name):
            if name not in made:
                made[name] = ctx.enter_context(nc.semaphore(name))
            return made[name]

        h = sb("h", [P, 3, D])
        hn = sb("hn", [P, 3, D])
        gain = sb("gain", [P, D])
        with ExitStack() as plain:
            raw = [plain.enter_context(nc.sbuf_tensor(f"raw{i}", [P, UNIT], f32)) for i in range(RING)]
            hnT = plain.enter_context(nc.sbuf_tensor("hnT", [P, KC, T], f32))
            w_g_in = plain.enter_context(nc.sbuf_tensor("w_g_in", [P, KC, 2 * RANK], f32))
        mix_lo = [sb(f"mix_lo{i}", [P, UNIT], f32r) for i in range(RING)]
        hnT_hi = sb("hnT_hi", [P, KC, T], f32r)
        w_g_lo = sb("w_g_lo", [P, KC, 2 * RANK], f32r)
        consts = sb("consts", [P, A["consts"].shape[1]])
        rope = sb("rope", [P, 2, 3, 32])
        stats = sb("stats", [P, 5, 4, 3])
        w_g_hi = sb("w_g_hi", [P, KC, 2 * RANK], f32r)

        conv_w = sb("conv_w", [P, 3, 4])
        gla_gain = sb("gla_gain", [P, DV])
        qk_gain = sb("qk_gain", [P, 2, HD])
        w_route = [sb(f"w_route{l}", [P, KC, 36]) for l in range(2)]
        b_route = sb("b_route", [P, 2, 36])
        idx_g = sb("idx_g", [P, 3, 8], u32)
        idx_e = sb("idx_e", [P, 3, 8], u32)
        n_iter = sb("n_iter", [P, 3], i32)
        junk = sb("junk", [P, DV])
        att_max = sb("att_max", [P, 32])
        att_sum = sb("att_sum", [P, 32])
        att_rcp = sb("att_rcp", [P, 32])
        turns = ExitStack()
        scratch = turns.enter_context(nc.sbuf_tensor("scratch", [P, 15600], f32))
        hnT_lo = turns.enter_context(nc.sbuf_tensor("hnT_lo", [P, KC, T], f32r))
        mix_hi = [turns.enter_context(nc.sbuf_tensor(f"mix_hi{i}", [P, UNIT], f32r)) for i in range(MIX_BUFS)]
        turns.close()
        moe_scratch = sb("moe_scratch", [P, 2250])
        w_hi = [sb(f"w_hi{i}", [P, UNIT], f32r) for i in range(BUFS)]
        w_lo = [sb(f"w_lo{i}", [P, UNIT], f32r) for i in range(BUFS)]
        x_hi = sb("x_hi", [P, KC, P], f32r)
        x_lo = sb("x_lo", [P, KC, P], f32r)
        heT_hi = sb("heT_hi", [P, 2, 2, P], f32r)
        heT_lo = sb("heT_lo", [P, 2, 2, P], f32r)
        ysum_hi = sb("ysum_hi", [P, D], f32r)
        ysum_lo = sb("ysum_lo", [P, D], f32r)
        selT = sb("selT", [P, T], f32r)
        spent = [0]

        area = [scratch]

        def carve(*shape):
            n = 1
            for s in shape:
                n *= s
            ap = area[0][:, spent[0]:spent[0] + n]
            spent[0] += n
            assert spent[0] <= area[0].shape[1], spent[0]
            if len(shape) == 2:
                return ap.rearrange("p (a b) -> p a b", a=shape[0])
            if len(shape) == 3:
                return ap.rearrange("p (a b c) -> p a b c", a=shape[0], b=shape[1])
            return ap

        ident = consts[:, 0:128]
        fwd_bwd = consts[:, 128:384]
        incl_fwd = consts[:, 128:256]
        strict_bwd = consts[:, 256:384]
        incl_bwd = consts[:, 384:512]
        strict_fwd = consts[:, 512:640]
        before = consts[:, 640:768]
        ones = consts[:, 768:896]
        iota = consts[:, 896:1024]
        valid = consts[:, 1024:1027]

        z = carve(4, T + 2)
        conv = carve(4, T)
        gT = carve(1, T)[0:2 * RANK + 1, 0, :]
        wgate = carve(1, W)[0:2 * RANK + 1, 0, :]
        ya = carve(4, T)
        qT = carve(2, T)
        kT = carve(2, T)
        ktok = carve(3, 256)
        la = carve(3, W)
        decay = carve(4, 5)
        E = carve(4, T)
        Ei = carve(4, T)
        kend = carve(3, W)
        state = carve(8, 2, 128)
        masked = carve(2 * HEADS, 2 * P)
        oss = carve(3, 4, 4)
        la_tmp = E[:, :, :].rearrange("p a b -> p (a b)")
        la_tmp2 = Ei[:, :, :].rearrange("p a b -> p (a b)")
        yb = kend
        v = hn[:, 0:3, 0:W]
        rs = hn[:, 0:3, W:2 * W]
        spent[0] = 0
        qs = carve(4, QH // 2, HD)
        ks = carve(3, KVH, HD)
        ks2 = carve(3, KVH, 2 * HD)
        vs = carve(3, KVH * HD)
        rot_dve = carve(2, QH // 2, HD)
        rot_pool = carve(2, QH // 2, HD)
        qT1 = carve(8, 2 * P)
        kT1 = carve(KVH, T)
        qsq = carve(2, QH, HD)
        ksq = rot_pool[:, :, :, :].rearrange("p a h d -> p (a h) d")[:, 0:3 * KVH, :]
        probs = carve(4, T)
        pT = carve(2, 4, P)
        pTm = carve(2, 2, P)
        hstat = carve(4, 48)
        UNIT_OF = [(u // 8, u % 8 // 4, 4 * (u // 8) + u % 4) for u in range(16)]
        spent[0] = 0
        area[0] = moe_scratch
        sel = carve(3, P)

        logitsT = carve(1, T)[:, 0, :]
        act_g = carve(2, F)
        he = carve(2, F)

        slot_gates = carve(1, EPG)[:, 0, :]
        logits = carve(3, 36)
        padded = carve(3, 8)
        top_g = carve(3, 8)
        top_e = carve(3, 8)
        onehot = carve(3, G)
        expg = carve(3, G)
        esel = carve(3, EPG)
        picked = carve(3, G, EPG)
        gates = carve(3, EPG)
        gtmp = carve(3, EPG)
        key = carve(1, 4)[:, 0, :]
        rstat = carve(12, 4)

        B = [ctx.enter_context(nc.psum_tensor(f"bank{i}", [P, W], f32)) for i in range(8)]

        def chain(eng, name):
            n = [0]

            def link(ins):
                n[0] += 1
                ins.then_inc(sem(name), 1)
                eng.wait_ge(sem(name), n[0])
            return link

        block = ctx.enter_context(nc.Block())

        def upto(n):
            return sum(len(t) for t in NORM_TILES[:n])

        def hnT_count(n):
            return sum(len(t) * (1 if i % 2 else 2) for i, t in enumerate(NORM_TILES[:n]))

        MIX_READ = [[("k", 3), ("v", 3), ("r", 3), ("ax", 4), ("ac", 4), ("ab", 4), ("out0", 3), ("out0", 6)],
                    [("q1", 2), ("kv", 3), ("q2", 2), ("out1", 2), ("out1", 4)]]
        PROJ, total = {}, 0
        for kind, count in (("g", 1), ("q", 2), ("k", 3), ("v", 3), ("r", 3), ("ax", 4), ("ac", 4), ("ab", 4),
                            ("out0", 6), ("q1", 2), ("kv", 3), ("q2", 2), ("out1", 4)):
            PROJ[kind] = total
            total += count

        def mix_unit(l, b, half):
            return 2 * (l * NMIX[0] + b) + half

        MIX_POOL = [mix_unit(l, 0, 0) + u for l in range(2) for u in range(2 * NMIX[l]) if u % 2 == 0 or (l, u) in ((0, 13), (1, 5), (1, 7))]

        def mix_low_done(l, u):
            n = mix_unit(l, 0, 0) + u
            mine = n in MIX_POOL
            return ("mix_lo_pool" if mine else "mix_lo_dve"), sum((i in MIX_POOL) == mine for i in range(n + 1))

        def low_mix(eng, ops, l, u):
            n = mix_unit(l, 0, 0) + u
            slot = (MIX_SLOT0[l] + u) % RING
            eng.wait_ge(sem("mix_hi"), n + 1)
            ops.tensor_tensor(mix_lo[slot][:, :], raw[slot][:, :], mix_hi[u % MIX_BUFS][:, :].bitcast(f32), ALU.subtract)\
               .then_inc(sem(mix_low_done(l, u)[0]), 1)

        def wait_mix_read(eng, l, b):
            kind, count = MIX_READ[l][b]
            eng.wait_ge(sem("proj_ps"), PROJ[kind] + count)

        def scale_heads(link, ops, x, first, gn):
            n = x.shape[1]
            link(ops.tensor_tensor(x, x, hstat[:, 3, first:first + n].unsqueeze(2).to_broadcast([P, n, HD]), ALU.mult))
            link(ops.tensor_tensor(x, x, gn.unsqueeze(1).to_broadcast([P, n, HD]), ALU.mult))

        def rotate(link, ops, x, dst, t, tmp):
            nh = x.shape[1]
            ta, tb = tmp[:, 0, 0:nh, :], tmp[:, 1, 0:nh, :]
            x0, x1 = x[:, :, 0:HD:2], x[:, :, 1:HD:2]
            c = rope[:, 0, t, :].unsqueeze(1).to_broadcast([P, nh, 32])
            s = rope[:, 1, t, :].unsqueeze(1).to_broadcast([P, nh, 32])
            ops.tensor_tensor(ta[:, :, 0:32], x0, c, ALU.mult)
            ops.tensor_tensor(ta[:, :, 32:64], x1, s, ALU.mult)
            ops.tensor_tensor(tb[:, :, 0:32], x0, s, ALU.mult)
            link(ops.tensor_tensor(tb[:, :, 32:64], x1, c, ALU.mult))
            ops.tensor_tensor(dst[:, :, 0:HD:2], ta[:, :, 0:32], ta[:, :, 32:64], ALU.subtract)
            link(ops.tensor_tensor(dst[:, :, 1:HD:2], tb[:, :, 0:32], tb[:, :, 32:64], ALU.add))

        def score_place(i, hd):
            return B[2 + hd][:, 0:2 * P] if i < 2 else B[2 + hd % 2][:, 2 * P * (hd // 2):2 * P * (hd // 2) + 2 * P]

        OUT_BANK = [6, 0, 4]

        def subtract(eng, ops, l, it, j):
            eng.wait_ge(sem(f"w_hi{l}"), it * NU + j + 1)
            name, _, _ = low_done(j)
            ops.tensor_tensor(w_lo[j % BUFS][:, :], raw[(MOE_SLOT0[l] + j) % RING][:, :], w_hi[j % BUFS][:, :].bitcast(f32),
                              ALU.subtract).then_inc(sem(f"{name}{l}"), 1)

        @block.sync
        def _(sp):
            sp.dma_start(h[:, 1, :], A["x"][0, 0:P, :]).then_inc(sem("h_in"), 16)
            sp.dma_start(h[:, 2, :], A["x"][0, P:2 * P, :]).then_inc(sem("h_in"), 16)
            sp.dma_start(h[0:NM, 0, :], A["meta_tokens"]).then_inc(sem("h_in"), 16)
            sp.dma_start(gain[:, :], A["norm_mix"][0:1, :].broadcast_to([P, D])).then_inc(sem("gain0_in"), 16)
            sp.dma_start(consts[:, 0:P], A["consts"][:, 0:P]).then_inc(sem("ident_in"), 16)

            def mix_block(l, b, half):
                slot = (MIX_SLOT0[l] + 2 * b + half) % RING
                dst = raw[slot][:, :].rearrange("p (c n) -> p c n", c=4)
                w_in, w_out = (A["sc_w_in"], A["sc_w_out"]) if l == 0 else (A["att_w_in"], A["att_w_out"])
                cols = MIX0_COLS if l == 0 else MIX1_COLS
                if b < len(cols):
                    src = w_in[0].rearrange("(p c) n -> p c n", c=KC)[:, :, cols[b]:cols[b] + W]
                else:
                    n = b - len(cols)
                    src = w_out[0].rearrange("(c p) n -> p c n", c=KC)[:, :, n * W:(n + 1) * W]
                sp.dma_start(dst, src[:, 4 * half:4 * half + 4, :]).then_inc(sem(f"mix_w{slot}"), 16)

            def unit(l, g, j):
                kind, e, half = UNITS[j]
                dst = raw[(MOE_SLOT0[l] + j) % RING]
                if kind == "gu":
                    gu = dst[:, :].rearrange("p (u c n) -> p u c n", u=2, c=4)
                    for u, name in enumerate(("moe_w_gate", "moe_w_up")):
                        src = A[name][l].rearrange("(g e) (p c) n -> g e p c n", g=G, c=KC)[bass.ds(g, 1), e, :, 4 * half:4 * half + 4, :]
                        sp.dma_start(gu[:, u], src.rearrange("g p c n -> p (g c) n")).then_inc(sem(f"raw{l}_{j % RING}"), 16)
                else:
                    src = A["moe_w_down"][l].rearrange("(g e) (p c) n -> g e p c n", g=G, c=2)[bass.ds(g, 1), e]
                    sp.dma_start(dst[:, :].rearrange("p (c n) -> p c n", c=2), src.rearrange("g p c n -> p (g c) n"))\
                      .then_inc(sem(f"raw{l}_{j % RING}"), 16)

            for b in range(NMIX[0]):
                if b == 1:
                    sp.dma_start(consts[:, P:], A["consts"][:, P:]).then_inc(sem("consts_in"), 16)
                if 2 * b >= RING:
                    wait_mix_read(sp, 0, b - RING // 2)
                for half in range(2):
                    mix_block(0, b, half)

            before_last0 = None
            for l in range(2):
                if l == 1:
                    for b in range(NMIX[1]):
                        if 2 * b >= RING:
                            wait_mix_read(sp, 1, b - RING // 2)
                        for half in range(2):
                            if 2 * b < RING:
                                name, count, per = low_done(NU - RING + 2 * b + half)
                                sp.wait_ge(sem(f"{name}0"), before_last0 * per + count)
                            mix_block(1, b, half)

                def group(g, it, first):
                    for j in range(NU):
                        if first and j < RING:
                            if j % 2 == 0:
                                wait_mix_read(sp, l, NMIX[l] - RING // 2 + j // 2)
                        elif j < RING:
                            name, count, per = low_done(NU + j - RING)
                            sp.wait_ge(sem(f"{name}{l}"), (it - 1) * per + count)
                        else:
                            name, count, per = low_done(j - RING)
                            sp.wait_ge(sem(f"{name}{l}"), it * per + count)
                        unit(l, g, j)

                group(0, 0, True)
                with sp.Fori(1, G) as g:
                    group(g, g, False)
                sp.wait_ge(sem("n_iter_ready"), l + 1)
                n_next = sp.value_load(n_iter[0:1, l:l + 1], min_val=G, max_val=3 * G)
                with sp.If(n_next > G):
                    with sp.Fori(G, n_next, G) as it0:
                        with sp.Fori(0, G) as g:
                            group(g, it0 + g, False)
                if l == 0:
                    before_last0 = sp.value_load(n_iter[0:1, 2:3], min_val=G - 1, max_val=3 * G - 1)

            for i in range(2):
                sp.wait_ge(sem("hn_ready"), upto(4) + i + 1)
                sp.dma_start(out[0, i * P:(i + 1) * P, :], hn[:, 1 + i, :]).then_inc(sem("out_done"), 16)
            sp.wait_ge(sem("out_done"), 32)

        @block.gpsimd
        def _(pool):
            pool.memset(wgate[:, :], 0.0).then_inc(sem("pool_step"), 1)
            pool.wait_ge(sem("pool_step"), 1)
            pool.memset(gT[2 * RANK:2 * RANK + 1, :], 1.0).then_inc(sem("pool_step"), 1)
            pool.wait_ge(sem("pool_step"), 2)
            pool.dma_start(w_g_in[:, :, :], A["sc_w_in"][0].rearrange("(p c) n -> p c n", c=KC)[:, :, 6 * W:6 * W + 2 * RANK])\
                .then_inc(sem("w_g_in"), 16)
            pool.dma_start(wgate[0:RANK, 0:256], A["gla_w_gate_fwd"][0]).then_inc(sem("gla_params_in"), 16)
            pool.dma_start(wgate[RANK:2 * RANK, 256:512], A["gla_w_gate_bwd"][0]).then_inc(sem("gla_params_in"), 16)
            pool.dma_start(wgate[2 * RANK:2 * RANK + 1, 0:256], A["gla_b_gate_fwd"]).then_inc(sem("gla_params_in"), 16)
            pool.dma_start(wgate[2 * RANK:2 * RANK + 1, 256:512], A["gla_b_gate_bwd"]).then_inc(sem("gla_params_in"), 16)
            pool.dma_start(gla_gain[:, :], A["gla_norm_w"].broadcast_to([P, DV])).then_inc(sem("gla_params_in"), 16)
            with nc.allow_non_contiguous_dma("1536 single elements, once"):
                for t in range(3):
                    pool.dma_start(conv_w[:, t, :], A["sc_conv_w"][0, t, :].rearrange("(c p) -> p c", p=P)).then_inc(sem("gla_params_in"), 16)
            for u in range(0, 2 * NMIX[0], 2):
                if u == 2 * NMIX[0] - 4:
                    pool.wait_ge(sem("feat_hi"), 1)
                    nc.gpsimd.tensor_tensor(hnT_lo[:, 0:4, :], ya[:, :, :], hnT_hi[:, 0:4, :].bitcast(f32), ALU.subtract).then_inc(sem("pool_step"), 1)
                low_mix(pool, nc.gpsimd, 0, u)
                if u == 12:
                    low_mix(pool, nc.gpsimd, 0, 13)
            pool.dma_start(qk_gain[:, 0, :], A["att_q_norm"].broadcast_to([P, HD])).then_inc(sem("att_params_in"), 16)
            pool.dma_start(qk_gain[:, 1, :], A["att_k_norm"].broadcast_to([P, HD])).then_inc(sem("att_params_in"), 16)
            pool.dma_start(rope[:, :, :, :], A["rope"].rearrange("p (a t j) -> p a t j", a=2, t=3)).then_inc(sem("att_params_in"), 16)
            for l in range(2):
                pool.dma_start(w_route[l][:, :, 0:G], A["moe_w_group"][l].rearrange("(p c) n -> p c n", c=KC)).then_inc(sem("route_in"), 16)
                pool.dma_start(w_route[l][:, :, G:36], A["moe_w_expert"][l].rearrange("(p c) n -> p c n", c=KC)).then_inc(sem("route_in"), 16)
                pool.dma_start(b_route[:, l, 0:G], A["moe_b_group"][l:l + 1, :].broadcast_to([P, G])).then_inc(sem("route_in"), 16)
                pool.dma_start(b_route[:, l, G:36], A["moe_b_expert"][l:l + 1, :].broadcast_to([P, 32])).then_inc(sem("route_in"), 16)
            for n in range(1, 5):
                src = [None, A["norm_ffn"][0:1, :], A["norm_mix"][1:2, :], A["norm_ffn"][1:2, :],
                       A["norm_final"].rearrange("(a n) -> a n", a=1)][n]
                pool.wait_ge(sem("hn_ready"), upto(n))
                pool.dma_start(gain[:, :], src.broadcast_to([P, D])).then_inc(sem("gain_in"), 16)
                if n == 3:
                    for u in (0, 2, 4, 5, 6, 7):
                        low_mix(pool, nc.gpsimd, 1, u)
                    link = chain(pool, "pool_chain")
                    pool.wait_ge(sem("head_rstd"), 5)
                    scale_heads(link, nc.gpsimd, qs[:, 2:4].rearrange("p i h d -> p (i h) d"), 32, qk_gain[:, 0, :])
                    for i in range(2):
                        rotate(link, nc.gpsimd, qs[:, 2 + i], qs[:, 2 + i], 1 + i, rot_pool)
                    pool.sem_inc(sem("pool_step"), 1)
                    low_mix(pool, nc.gpsimd, 1, 8)
                if n in (2, 4):
                    l = n // 2 - 1
                    pool.wait_ge(sem("n_iter_ready"), l + 1)
                    n_it = pool.value_load(n_iter[0:1, l:l + 1], min_val=G, max_val=3 * G)
                    with pool.Fori(0, n_it) as it:
                        for j in POOL_UNITS:
                            subtract(pool, nc.gpsimd, l, it, j)

        def wait_h(eng, n, i, steps):
            tiles = len(NORM_TILES[n - 1]) if n else 3
            if n == 0:
                eng.wait_ge(sem("h_in"), 48)
            elif n in (1, 3):
                eng.wait_ge(sem(f"h_mixed{n // 2}"), [3, 2][n // 2] + i + 1)
            else:
                eng.wait_ge(sem(f"h_added{n // 2 - 1}"), PRIMED + steps * 2 * tiles + tiles + i + 1)

        def wait_hnT(eng, n):
            eng.wait_ge(sem("hnT_act"), hnT_count(n + 1))
            eng.wait_ge(sem("hnT_dve"), hnT_count(n + 1))

        @block.scalar
        def _(act):
            link = chain(act, "act_chain")

            def norm(n, steps=None):
                tiles = NORM_TILES[n]
                act.wait_ge(sem("clear"), 1)
                link(nc.scalar.activation(junk[:, 0:3], stats[:, n, 1, :], ACT.Sqrt))
                def root(i):
                    t = tiles[i]
                    m = TILE_N[t]
                    act.wait_ge(sem("norm_var"), upto(n) + i + 1)
                    nc.scalar.activation(stats[0:m, n, 2, t:t + 1], stats[0:m, n, 1, t:t + 1], ACT.Sqrt).then_inc(sem("norm_std"), 1)

                ahead = 0 if n % 2 else 1
                for i, t in enumerate(tiles):
                    wait_h(act, n, i, steps)
                    m = TILE_N[t]
                    nc.scalar.activation(hn[0:m, t, :], h[0:m, t, :], ACT.Square,
                                         accum_out=stats[0:m, n, 0, t:t + 1]).then_inc(sem("norm_ss"), 1)
                    if i >= ahead:
                        root(i - ahead)
                if ahead:
                    root(len(tiles) - 1)

            def transposes_out(n):
                for i, t in enumerate(NORM_TILES[n]):
                    m = TILE_N[t]
                    for half in range(1 if n % 2 else 2):
                        act.wait_ge(sem("hnT_ps"), 2 * (upto(n) + i) + half + 1)
                        dst = hnT if n % 2 else hnT_hi
                        nc.scalar.activation(dst[:, 4 * half:4 * half + 4, TILE_AT[t]:TILE_AT[t] + m],
                                             B[half][:, :].rearrange("p (c n) -> p c n", c=4)[:, :, 0:m], ACT.Copy).then_inc(sem("hnT_act"), 1)

            def round_mix(l, b, half):
                u = 2 * b + half
                slots = [x % RING for x in range(2 * NMIX[0])] if l else []
                slots += [(MIX_SLOT0[l] + x) % RING for x in range(u + 1)]
                act.wait_ge(sem(f"mix_w{slots[-1]}"), 16 * slots.count(slots[-1]))
                if u >= MIX_BUFS:
                    b0, half0 = (u - MIX_BUFS) // 2, (u - MIX_BUFS) % 2
                    if half0 == 0:
                        act.wait_ge(sem("mix_used"), l * NMIX[0] + b0 + 1)
                    else:
                        wait_mix_read(act, l, b0)
                nc.scalar.activation(mix_hi[u % MIX_BUFS][:, :], raw[slots[-1]][:, :], ACT.Copy).then_inc(sem("mix_hi"), 1)

            norm(0)
            round_mix(0, 0, 0)
            transposes_out(0)
            round_mix(0, 0, 1)
            round_mix(0, 1, 0)
            act.wait_ge(sem("pool_step"), 2)
            act.wait_ge(sem("proj_ps"), PROJ["g"] + 1)
            nc.scalar.activation(gT[0:2 * RANK, :], B[2][0:2 * RANK, 0:T], ACT.Copy).then_inc(sem("g_ev"), 1)
            for m in range(2):
                act.wait_ge(sem("proj_ps"), PROJ["q"] + m + 1)
                nc.scalar.activation(qT[:, m, :], B[3 + m][:, 0:T], ACT.Copy, scale=DK ** -0.5).then_inc(sem("q_ev"), 1)
            round_mix(0, 1, 1)
            round_mix(0, 2, 0)
            for t in range(3):
                n = TILE_N[t]
                act.wait_ge(sem("la_ps"), t + 1)
                if t:
                    act.wait_ge(sem("la_ln"), t)
                link(nc.scalar.activation(la_tmp[0:n, 0:W], B[t][0:n, :], ACT.Abs))
                link(nc.scalar.activation(la_tmp[0:n, 0:W], la_tmp[0:n, 0:W], ACT.Exp, scale=-1.0))
                if t >= 1:
                    act.wait_ge(sem("la_ready"), t)
                nc.scalar.activation(la_tmp2[0:n, 0:W], la_tmp[0:n, 0:W], ACT.Ln, bias=1.0).then_inc(sem("la_ln"), 1)
            for t in range(3):
                n = TILE_N[t]
                if t == 2:
                    round_mix(0, 2, 1)
                act.wait_ge(sem("proj_ps"), PROJ["v"] + t + 1)
                nc.scalar.activation(v[0:n, t, :], B[3 + t][0:n, :], ACT.Copy).then_inc(sem("v_ev"), 1)
            round_mix(0, 3, 0)
            for m in range(2):
                act.wait_ge(sem("kT_ps"), m + 1)
                nc.scalar.activation(kT[:, m, :], B[6 + m][:, 0:T], ACT.Copy).then_inc(sem("kT_ev"), 1)
            for t in range(3):
                n = TILE_N[t]
                if t == 2:
                    round_mix(0, 3, 1)
                act.wait_ge(sem("proj_ps"), PROJ["r"] + t + 1)
                nc.scalar.activation(rs[0:n, t, :], B[3 + t][0:n, :], ACT.Silu).then_inc(sem("r_ev"), 1)
            round_mix(0, 4, 0)
            for m in range(4):
                if m == 3:
                    round_mix(0, 4, 1)
                act.wait_ge(sem("proj_ps"), PROJ["ax"] + m + 1)
                act.wait_ge(sem("clear"), 2)
                nc.scalar.activation(z[:, m, 1:T + 1], B[6 + m % 2][:, 0:T], ACT.Copy).then_inc(sem("ax_ev"), 1)
            for dm in range(4):
                act.wait_ge(sem("cum_ps"), dm + 1)
                act.wait_ge(sem("la_ready"), 3)
                nc.scalar.activation(E[:, dm, :], B[dm][:, 0:T], ACT.Exp).then_inc(sem("E_exp"), 1)
                nc.scalar.activation(Ei[:, dm, :], B[dm][:, 0:T], ACT.Exp, scale=-1.0).then_inc(sem("E_exp"), 1)
            for t in range(3):
                n = TILE_N[t]
                act.wait_ge(sem("kend_ps"), t + 1)
                nc.scalar.activation(kend[0:n, t, :], B[[4, 5, 0][t]][0:n, :], ACT.Exp).then_inc(sem("kend_exp"), 1)
            round_mix(0, 5, 0)
            round_mix(0, 5, 1)
            round_mix(0, 6, 0)
            act.wait_ge(sem("proj_ps"), PROJ["ab"] + 4)
            act.wait_ge(sem("ya_ready"), 4)
            nc.scalar.activation(hnT_hi[:, 0:4, :], ya[:, :, :], ACT.Copy).then_inc(sem("feat_hi"), 1)
            round_mix(0, 6, 1)
            round_mix(0, 7, 0)
            def head_squares(i, t):
                n = TILE_N[t]
                act.wait_ge(sem("o_ps"), i + 1)
                for hd in range(HEADS):
                    src = B[OUT_BANK[i] + hd % 2][0:n, (hd // 2) * DV:(hd // 2 + 1) * DV]
                    nc.scalar.activation(junk[0:n, :], src, ACT.Square,
                                         accum_out=oss[0:n, i, 0, hd:hd + 1]).then_inc(sem("o_ss"), 1)
                    act.wait_ge(sem("o_ss"), 4 * i + hd + 1)
                act.wait_ge(sem("o_var"), i + 1)
                nc.scalar.activation(oss[0:n, i, 2, :], oss[0:n, i, 1, :], ACT.Sqrt).then_inc(sem("o_std"), 1)

            def ybT_high(i, t):
                n = TILE_N[t]
                act.wait_ge(sem("ybT_ps"), i + 1)
                nc.scalar.activation(hnT_hi[:, 4:8, TILE_AT[t]:TILE_AT[t] + n],
                                     B[OUT_BANK[i]][:, :].rearrange("p (c n) -> p c n", c=4)[:, :, 0:n], ACT.Copy).then_inc(sem("feat_hi"), 1)

            link(nc.scalar.activation(junk[:, 0:3], stats[:, 0, 1, :], ACT.Sqrt))
            head_squares(0, 1)
            head_squares(1, 2)
            head_squares(2, 0)
            ybT_high(0, 1)
            ybT_high(1, 2)
            ybT_high(2, 0)
            round_mix(0, 7, 1)

            def moe(l):
                n = 1 + 2 * l
                norm(n)
                transposes_out(n)
                round_weights(l, 0, 0)
                act.wait_ge(sem("gl_shift"), l + 1)
                tiles = NORM_TILES[n]
                a, b = tiles[0], tiles[-1] + 1
                nc.scalar.activation(expg[:, a:b, :], expg[:, a:b, :], ACT.Exp).then_inc(sem("gl_exp"), 1)
                for j in range(1, BUFS):
                    round_weights(l, 0, j)
                x_high(l, 0, 0)
                act.wait_ge(sem("top_diff"), l + 1)
                nc.scalar.activation(rstat[:, 4, a:b], rstat[:, 3, a:b], ACT.Exp).then_inc(sem("top_exp"), 1)
                x_high(l, 0, 1)
                act.wait_ge(sem("n_iter_ready"), l + 1)
                n_it = act.value_load(n_iter[0:1, l:l + 1], min_val=G, max_val=3 * G)
                nadd = 2 * len(tiles)
                with act.Fori(0, n_it) as it:
                    y_out(l, it, nadd)
                    todo = BUFS
                    for e in range(EPG):
                        while todo < NU and todo - BUFS <= AT["gu", e, 1]:
                            if todo - BUFS == AT["gu", e, 0] and e >= 2:
                                heT_high(l, it, e - 2)
                            round_weights(l, it, todo)
                            todo += 1
                        act.wait_ge(sem(f"w_used{l}"), used(it, "gu", e, 1))
                        if e < 2:
                            act.wait_ge(sem(f"he_ready{l}"), PRIMED + it * EPG)
                        else:
                            act.wait_ge(sem(f"he_ready{l}"), PRIMED + it * EPG + e - 1)
                        nc.scalar.activation(act_g[:, e % 2, :], B[2 + e % 2][:, 0:F], ACT.Silu).then_inc(sem(f"silu{l}"), 1)
                    for half in range(2):
                        if half == 0:
                            with act.If(n_it > it + 1):
                                round_weights(l, it + 1, 0)
                        heT_high(l, it, EPG - 2 + half)
                        if half == 0:
                            with act.If(n_it > it + 1):
                                round_weights(l, it + 1, 1)
                        with act.If(n_it > it + 1):
                            x_high(l, it + 1, half)
                    with act.If(n_it > it + 1):
                        round_weights(l, it + 1, 2)
                        round_weights(l, it + 1, 3)
                y_out(l, n_it, nadd)
                return n_it

            def x_high(l, it, half):
                act.wait_ge(sem(f"x_ps{l}"), 2 * it + half + 1)
                nc.scalar.activation(x_hi[:, 4 * half:4 * half + 4, :], B[half][:, :].rearrange("p (c n) -> p c n", c=4),
                                     ACT.Copy).then_inc(sem(f"x_hi{l}"), 1)

            def y_out(l, s, nadd):
                act.wait_ge(sem(f"w_used{l}"), s * NU + BUFS)
                act.wait_ge(sem(f"sc_ps{l}"), PRIMED + s * nadd)
                for half in range(2):
                    nc.scalar.activation(ysum_hi[:, half * W:(half + 1) * W], B[5 + half][:, :], ACT.Copy).then_inc(sem(f"y_hi{l}"), 1)

            def round_weights(l, it, j):
                count, per = raw_count(j)
                act.wait_ge(sem(f"raw{l}_{j % RING}"), it * per + count)
                act.wait_ge(sem(f"w_used{l}"), it * NU + j + 1)
                nc.scalar.activation(w_hi[j % BUFS][:, :], raw[(MOE_SLOT0[l] + j) % RING][:, :], ACT.Copy).then_inc(sem(f"w_hi{l}"), 1)

            def heT_high(l, it, e):
                act.wait_ge(sem(f"heT_ps{l}"), it * EPG + e + 1)
                if e >= 2:
                    act.wait_ge(sem(f"w_used{l}"), used(it, "d", e - 2))
                else:
                    act.wait_ge(sem(f"w_used{l}"), it * NU + BUFS)
                nc.scalar.activation(heT_hi[:, e % 2, :, :], B[4][:, 0:2 * P].rearrange("p (c n) -> p c n", c=2), ACT.Copy)\
                    .then_inc(sem(f"heT_hi{l}"), 1)

            steps = moe(0)

            norm(2, steps)
            round_mix(1, 0, 0)
            transposes_out(2)
            round_mix(1, 0, 1)
            round_mix(1, 1, 0)

            def head_root(nth, lo, hi):
                act.wait_ge(sem("head_var"), nth)
                nc.scalar.activation(hstat[:, 2, lo:hi], hstat[:, 1, lo:hi], ACT.Sqrt).then_inc(sem("head_std"), 1)

            def q_raw(n, i):
                act.wait_ge(sem("proj_ps"), PROJ[("q1", "q2")[n]] + i + 1)
                qb = B[[5, 6, 0, 7][2 * n + i]][:, :].rearrange("p (h d) -> p h d", h=8)
                nc.scalar.activation(qsq[:, n, 8 * i:8 * i + 8, :], qb, ACT.Square).then_inc(sem("q_raw"), 1)
                nc.scalar.activation(qs[:, 2 * n + i], qb, ACT.Copy).then_inc(sem("q_raw"), 1)

            def kv_raw(t):
                act.wait_ge(sem("proj_ps"), PROJ["kv"] + t + 1)
                kb = B[2 + t][:, 0:256].rearrange("p (h d) -> p h d", h=KVH)
                nc.scalar.activation(ksq[:, KVH * t:KVH * t + KVH, :], kb, ACT.Square).then_inc(sem("kv_raw"), 1)
                nc.scalar.activation(ks[:, t, :, :], kb, ACT.Copy).then_inc(sem("kv_raw"), 1)
                nc.scalar.activation(vs[:, t, :], B[2 + t][:, 256:512], ACT.Copy).then_inc(sem("kv_raw"), 1)

            def qT_out(n):
                for i in range(2):
                    act.wait_ge(sem("qk1T_ps"), KVH + 2 * n + i + 1)
                    nc.scalar.activation(qT1[:, 4 * n:4 * n + 4, i * P:(i + 1) * P],
                                         B[[5, 6, 0, 1][2 * n + i]][:, :].rearrange("p (c n) -> p c n", c=4), ACT.Copy).then_inc(sem("qk1T_ev"), 1)

            q_raw(0, 0)
            round_mix(1, 1, 1)
            q_raw(0, 1)
            head_root(1, 16, 32)
            round_mix(1, 2, 0)
            kv_raw(0)
            kv_raw(1)
            head_root(2, 0, KVH)
            round_mix(1, 2, 1)
            head_root(3, KVH, 2 * KVH)
            kv_raw(2)
            round_mix(1, 3, 0)
            head_root(4, 2 * KVH, 3 * KVH)
            q_raw(1, 0)
            for hv in range(KVH):
                act.wait_ge(sem("qk1T_ps"), hv + 1)
                nc.scalar.activation(kT1[:, hv, :], B[[1, 2, 3, 4][hv]][:, 0:T], ACT.Copy).then_inc(sem("qk1T_ev"), 1)
            qT_out(0)
            def exps(u):
                for o in range(2):
                    act.wait_ge(sem("s_max"), 2 * u + o + 1)
                    if u >= 2:
                        act.wait_ge(sem("pT_ps"), u - 1)
                    nc.scalar.activation(probs[:, 2 * (u % 2) + o, :], B[2 * (u % 2) + o][:, 0:T], ACT.Exp,
                                         bias=att_max[:, 2 * u + o:2 * u + o + 1],
                                         accum_out=att_sum[:, 2 * u + o:2 * u + o + 1]).then_inc(sem("p_exp"), 1)

            def pT_out(u):
                act.wait_ge(sem("pT_ps"), u + 1)
                if u >= 2:
                    act.wait_ge(sem("oT_ps"), u - 1)
                nc.scalar.activation(pT[:, u % 2, :, :], B[4 + u % 2][:, :].rearrange("p (c n) -> p c n", c=4), ACT.Copy).then_inc(sem("pT_ev"), 1)

            def oT_high(u):
                _, i, pair = UNIT_OF[u]
                act.wait_ge(sem("oT_ps"), u + 1)
                nc.scalar.activation(hnT_hi[:, pair, i * P:(i + 1) * P], B[7][:, 0:P], ACT.Copy).then_inc(sem("feat_hi"), 1)

            exps(0)
            exps(1)
            round_mix(1, 3, 1)
            q_raw(1, 1)
            for u in range(16):
                if 0 < u < 15:
                    exps(u + 1)
                pT_out(u)
                if u:
                    oT_high(u - 1)
                if u == 1:
                    head_root(5, 32, 48)
                if u == 8:
                    round_mix(1, 4, 0)
                if u == 6:
                    qT_out(1)
            oT_high(15)
            round_mix(1, 4, 1)
            steps = moe(1)
            norm(4, steps)

        @block.vector
        def _(dve):
            link = chain(dve, "dve_chain")

            def mean_square(n, i):
                t = NORM_TILES[n][i]
                m = TILE_N[t]
                dve.wait_ge(sem("norm_ss"), upto(n) + i + 1)
                nc.vector.tensor_scalar(stats[0:m, n, 1, t:t + 1], stats[0:m, n, 0, t:t + 1], 1.0 / D, EPS, ALU.mult, ALU.add)\
                  .then_inc(sem("norm_var"), 1)

            def scale_tile(n, i):
                t = NORM_TILES[n][i]
                m = TILE_N[t]
                dve.wait_ge(sem("norm_std"), upto(n) + i + 1)
                link(nc.vector.reciprocal(stats[0:m, n, 3, t:t + 1], stats[0:m, n, 2, t:t + 1]))
                if i == 0 and n:
                    dve.wait_ge(sem("gain_in"), 16 * n)
                elif i == 0:
                    dve.wait_ge(sem("gain0_in"), 16)
                nc.vector.scalar_tensor_tensor(hn[0:m, t, :], h[0:m, t, :], stats[0:m, n, 3, t:t + 1], gain[0:m, :],
                                               ALU.mult, ALU.mult).then_inc(sem("hn_ready"), 1)

            def norm_tile(n, i):
                mean_square(n, i)
                scale_tile(n, i)

            def norm(n):
                tiles = len(NORM_TILES[n])
                mean_square(n, 0)
                for i in range(tiles):
                    if i + 1 < tiles:
                        mean_square(n, i + 1)
                    scale_tile(n, i)

            def transposes_out(n):
                for i, t in enumerate(NORM_TILES[n]):
                    m = TILE_N[t]
                    if n % 2 == 0:
                        for half in range(2):
                            part = slice(4 * half, 4 * half + 4)
                            dve.wait_ge(sem("hnT_act"), hnT_count(n) + 2 * i + half + 1)
                            nc.vector.tensor_tensor(hnT_lo[:, part, TILE_AT[t]:TILE_AT[t] + m],
                                                    B[half][:, :].rearrange("p (c n) -> p c n", c=4)[:, :, 0:m],
                                                    hnT_hi[:, part, TILE_AT[t]:TILE_AT[t] + m].bitcast(f32), ALU.subtract).then_inc(sem("hnT_dve"), 1)
                        continue
                    dve.wait_ge(sem("hnT_ps"), 2 * (upto(n) + i) + 2)
                    nc.vector.tensor_copy(hnT[:, 4:8, TILE_AT[t]:TILE_AT[t] + m],
                                          B[1][:, :].rearrange("p (c n) -> p c n", c=4)[:, :, 0:m]).then_inc(sem("hnT_dve"), 1)

            nc.vector.memset(stats[:, :, :, :].rearrange("p a b c -> p (a b c)"), 1.0).then_inc(sem("clear"), 1)

            nc.vector.memset(z[:, :, :].rearrange("p a b -> p (a b)"), 0.0).then_inc(sem("clear"), 1)
            norm(0)
            dve.wait_ge(sem("w_g_in"), 16)
            link(nc.vector.tensor_copy(w_g_hi[:, :, :], w_g_in[:, :, :]))
            nc.vector.tensor_tensor(w_g_lo[:, :, :], w_g_in[:, :, :], w_g_hi[:, :, :].bitcast(f32), ALU.subtract).then_inc(sem("clear"), 1)
            transposes_out(0)
            low_mix(dve, nc.vector, 0, 1)
            for t in range(3):
                n = TILE_N[t]
                if t == 2:
                    low_mix(dve, nc.vector, 0, 3)
                dve.wait_ge(sem("proj_ps"), PROJ["k"] + t + 1)
                nc.vector.tensor_copy(ktok[0:n, t, :], B[5 + t][0:n, 0:256]).then_inc(sem("k_ev"), 1)
            for t in range(3):
                n = TILE_N[t]
                dve.wait_ge(sem("la_ln"), t + 1)
                link(nc.vector.tensor_scalar(la[0:n, t, :], B[t][0:n, :], 0.0, 1.0 / TAU, ALU.min, ALU.mult))
                nc.vector.scalar_tensor_tensor(la[0:n, t, :], la_tmp2[0:n, 0:W], -1.0 / TAU, la[0:n, t, :], ALU.mult, ALU.add).then_inc(sem("la_ready"), 1)
            low_mix(dve, nc.vector, 0, 5)
            dve.wait_ge(sem("gla_params_in"), 128)
            for t in range(3):
                n = TILE_N[t]
                if t == 2:
                    low_mix(dve, nc.vector, 0, 7)
                dve.wait_ge(sem("r_ev"), t + 1)
                r4 = rs[0:n, t, :].rearrange("p (h d) -> p h d", h=HEADS)
                nc.vector.tensor_tensor(r4, r4, gla_gain[0:n, :].unsqueeze(1).to_broadcast([n, HEADS, DV]), ALU.mult).then_inc(sem("rs_ready"), 1)
            low_mix(dve, nc.vector, 0, 9)
            dve.wait_ge(sem("E_exp"), 8)
            link(nc.vector.tensor_copy(decay[:, 0:2, 0:1], E[:, 0:2, NM - 1:NM]))
            link(nc.vector.tensor_copy(decay[:, 0:2, 1:5], E[:, 0:2, NM + C - 1:T:C]))
            link(nc.vector.tensor_copy(decay[:, 2:4, 0:1], E[:, 2:4, 0:1]))
            link(nc.vector.tensor_copy(decay[:, 2:4, 1:5], E[:, 2:4, NM:T:C]))
            dve.wait_ge(sem("q_ev"), 2)
            dve.wait_ge(sem("kT_ev"), 2)
            for d in range(2):
                nc.vector.tensor_tensor(E[:, 2 * d:2 * d + 2, :], E[:, 2 * d:2 * d + 2, :], qT[:, :, :], ALU.mult).then_inc(sem("qk_dec"), 1)
                nc.vector.tensor_tensor(Ei[:, 2 * d:2 * d + 2, :], Ei[:, 2 * d:2 * d + 2, :], kT[:, :, :], ALU.mult).then_inc(sem("qk_dec"), 1)
            for t in range(3):
                n = TILE_N[t]
                dve.wait_ge(sem("kend_exp"), t + 1)
                for d in range(2):
                    ke = kend[0:n, t, 256 * d:256 * d + 256]
                    nc.vector.tensor_tensor(ke, ke, ktok[0:n, t, :], ALU.mult).then_inc(sem("kend"), 1)
            for m in range(4):
                if m == 3:
                    low_mix(dve, nc.vector, 0, 11)
                dve.wait_ge(sem("proj_ps"), PROJ["ac"] + m + 1)
                dve.wait_ge(sem("ax_ev"), m + 1)
                zz = z[:, m, 1:T + 1]
                nc.vector.tensor_tensor(zz, B[6 + m % 2][:, 0:T], zz, ALU.mult).then_inc(sem("z_ready"), 1)
            dve.wait_ge(sem("z_ready"), 4)
            dve.wait_ge(sem("gla_params_in"), 128)
            for tap in range(3):
                for m in range(4):
                    src = z[:, m, tap:tap + T]
                    if tap == 0:
                        last = nc.vector.tensor_scalar(conv[:, m, :], src, conv_w[:, 0, m:m + 1], None, ALU.mult)
                    else:
                        last = nc.vector.scalar_tensor_tensor(conv[:, m, :], src, conv_w[:, tap, m:m + 1], conv[:, m, :],
                                                       ALU.mult, ALU.add)
                link(last)
            for m in range(4):
                dve.wait_ge(sem("proj_ps"), PROJ["ab"] + m + 1)
                nc.vector.tensor_tensor(ya[:, m, :], B[6 + m % 2][:, 0:T], conv[:, m, :], ALU.mult).then_inc(sem("ya_ready"), 1)
            for k in range(8):

                d, i = k % 2, k // 2
                j = i if d == 0 else 4 - i
                dve.wait_ge(sem("kvs_ps"), k + 1)
                if i:
                    dve.wait_ge(sem("state"), 4 * (k - 1))
                for m in range(2):
                    for hh in range(2):
                        rows = slice(64 * hh, 64 * hh + 64)
                        got = B[[2, 3, 4, 5, 0, 1, 0, 1][k]][rows, 256 * m + DV * hh:256 * m + DV * hh + DV]
                        new = state[rows, 4 * d + i, m, :]
                        if i == 0:
                            nc.vector.tensor_copy(new, got).then_inc(sem("state"), 1)
                        else:
                            nc.vector.scalar_tensor_tensor(new, state[rows, 4 * d + i - 1, m, :], decay[rows, 2 * d + m, j:j + 1], got,
                                                           ALU.mult, ALU.add).then_inc(sem("state"), 1)
            def mask_scores(i, t):
                n = TILE_N[t]
                for hd in range(HEADS):
                    dve.wait_ge(sem("sc_ps"), 4 * i + hd + 1 if i < 2 else 12)
                    if i == 2:
                        dve.wait_ge(sem("o_ps"), 1)
                    nc.vector.tensor_tensor(masked[0:n, HEADS * (i % 2) + hd, :].rearrange("p (d c) -> p d c", d=2)[:, :, 0:n],
                                            score_place(i, hd)[0:n, :].rearrange("p (d c) -> p d c", d=2)[:, :, 0:n],
                                            fwd_bwd[0:n, :].rearrange("p (d c) -> p d c", d=2)[:, :, 0:n], ALU.mult).then_inc(sem("masked"), 1)

            def head_norm(i, t):
                n = TILE_N[t]
                dve.wait_ge(sem("o_ss"), 4 * i + 4)
                nc.vector.tensor_scalar(oss[0:n, i, 1, :], oss[0:n, i, 0, :], 1.0 / DV, EPS, ALU.mult, ALU.add).then_inc(sem("o_var"), 1)
                dve.wait_ge(sem("o_std"), i + 1)
                link(nc.vector.reciprocal(oss[0:n, i, 3, :], oss[0:n, i, 2, :]))
                dve.wait_ge(sem("rs_ready"), 3)
                for hd in range(HEADS):
                    src = B[OUT_BANK[i] + hd % 2][0:n, (hd // 2) * DV:(hd // 2 + 1) * DV]
                    nc.vector.scalar_tensor_tensor(yb[0:n, t, hd * DV:(hd + 1) * DV], src, oss[0:n, i, 3, hd:hd + 1],
                                                   rs[0:n, t, hd * DV:(hd + 1) * DV], ALU.mult, ALU.mult).then_inc(sem("yb_ready"), 1)
            def ybT_low(i, t):
                n = TILE_N[t]
                dve.wait_ge(sem("feat_hi"), 1 + i + 1)
                at = slice(TILE_AT[t], TILE_AT[t] + n)
                nc.vector.tensor_tensor(hnT_lo[:, 4:8, at], B[OUT_BANK[i]][:, :].rearrange("p (c n) -> p c n", c=4)[:, :, 0:n],
                                        hnT_hi[:, 4:8, at].bitcast(f32), ALU.subtract).then_inc(sem("ybT_ev"), 1)

            mask_scores(0, 1)
            mask_scores(1, 2)
            head_norm(0, 1)
            mask_scores(2, 0)
            head_norm(1, 2)
            head_norm(2, 0)
            ybT_low(0, 1)
            ybT_low(1, 2)
            ybT_low(2, 0)
            for half in range(2):
                for t in range(3):
                    n = TILE_N[t]
                    k = 3 * half + t
                    if k == 2:
                        low_mix(dve, nc.vector, 0, 15)
                    dve.wait_ge(sem("proj_ps"), PROJ["out0"] + k + 1)
                    hh = h[0:n, t, half * W:(half + 1) * W]
                    nc.vector.tensor_tensor(hh, B[2 + k][0:n, :], hh, ALU.add).then_inc(sem("h_mixed0"), 1)
                    if half == 1:
                        norm_tile(1, t)

            def moe(l):
                n = 1 + 2 * l
                tiles = NORM_TILES[n]
                a, b = tiles[0], tiles[-1] + 1
                NT = b - a
                transposes_out(n)
                nc.vector.tensor_tensor(selT[:, TILE_AT[a]:T], consts[:, TILE_AT[a]:T], consts[:, TILE_AT[a]:T],
                                        ALU.subtract).then_inc(sem(f"selT{l}"), 1)
                def select(it):
                    dve.wait_ge(sem(f"key{l}"), it + 1)
                    nc.vector.tensor_tensor(sel[:, a:b, :], iota.unsqueeze(1).to_broadcast([P, NT, P]),
                                            key[:, a:b].unsqueeze(2).to_broadcast([P, NT, P]), ALU.is_equal).then_inc(sem(f"sel{l}"), 1)
                    dve.wait_ge(sem(f"sel{l}"), it + 1)
                    nc.vector.tensor_scalar(key[:, a:b], key[:, a:b], -float(P), None, ALU.add).then_inc(sem(f"key{l}"), 1)

                def x_low(it, half):
                    dve.wait_ge(sem(f"x_hi{l}"), 2 * it + half + 1)
                    part = slice(4 * half, 4 * half + 4)
                    nc.vector.tensor_tensor(x_lo[:, part, :], B[half][:, :].rearrange("p (c n) -> p c n", c=4),
                                            x_hi[:, part, :].bitcast(f32), ALU.subtract).then_inc(sem(f"x_lo{l}"), 1)

                dve.wait_ge(sem("route_in"), 128)
                link(nc.vector.memset(padded[:, :, :].rearrange("p a b -> p (a b)"), -3.0e38))
                dve.wait_ge(sem("logitsT_ps"), l + 1)
                nc.vector.tensor_copy(logitsT[0:36, TILE_AT[a]:T], B[7][0:36, TILE_AT[a]:T]).then_inc(sem("logitsT"), 1)
                dve.wait_ge(sem("logits_ps"), l + 1)
                link(nc.vector.tensor_tensor(logits[:, a:b, :], B[6][:, 0:108].rearrange("p (t n) -> p t n", t=3)[:, a:b, :],
                                             b_route[:, l, :].unsqueeze(1).to_broadcast([P, NT, 36]), ALU.add))
                link(nc.vector.tensor_copy(padded[:, a:b, 0:G], logits[:, a:b, 0:G]))
                for t in tiles:
                    link(nc.vector.max(top_g[:, t, :], padded[:, t, :]))
                nc.vector.tensor_tensor(expg[:, a:b, :], logits[:, a:b, 0:G], top_g[:, a:b, 0:1].to_broadcast([P, NT, G]),
                                        ALU.subtract).then_inc(sem("gl_shift"), 1)
                for t in tiles:
                    link(nc.vector.max_index(idx_g[:, t, :], top_g[:, t, :], padded[:, t, :]))
                gidx = rstat[:, 0, a:b]
                link(nc.vector.tensor_copy(gidx.unsqueeze(2), idx_g[:, a:b, 0:1]))
                link(nc.vector.tensor_tensor(onehot[:, a:b, :], iota[:, 0:G].unsqueeze(1).to_broadcast([P, NT, G]),
                                             gidx.unsqueeze(2).to_broadcast([P, NT, G]), ALU.is_equal))
                nc.vector.tensor_tensor(onehot[:, a:b, :], onehot[:, a:b, :], valid[:, a:b].unsqueeze(2).to_broadcast([P, NT, G]),
                                        ALU.mult).then_inc(sem("onehot"), 1)
                dve.wait_ge(sem("onehot"), l + 1)
                dve.wait_ge(sem("rank_ps"), l + 1)
                link(nc.vector.tensor_tensor(gtmp[:, a:b, 0:G], B[7][:, 0:12].rearrange("p (t g) -> p t g", t=3)[:, a:b, :], onehot[:, a:b, :], ALU.mult))
                link(nc.vector.tensor_reduce(rstat[:, 8, a:b], gtmp[:, a:b, 0:G], X, ALU.add))
                link(nc.vector.tensor_scalar(rstat[:, 10, a:b], rstat[:, 8, a:b], float(P), float((G - 1) * P), ALU.is_ge, ALU.mult))
                link(nc.vector.tensor_scalar(rstat[:, 11, a:b], rstat[:, 8, a:b], float(2 * P), float((G - 1) * P), ALU.is_ge, ALU.mult))
                link(nc.vector.tensor_tensor(rstat[:, 10, a:b], rstat[:, 10, a:b], rstat[:, 11, a:b], ALU.add))
                link(nc.vector.tensor_tensor(rstat[:, 10, a:b], rstat[:, 10, a:b], rstat[:, 8, a:b], ALU.add))
                link(nc.vector.scalar_tensor_tensor(key[:, a:b], gidx, float(P), rstat[:, 10, a:b], ALU.mult, ALU.add))
                link(nc.vector.scalar_tensor_tensor(key[:, a:b], key[:, a:b], 1.0, valid[:, a:b], ALU.add, ALU.mult))
                nc.vector.tensor_scalar(key[:, a:b], key[:, a:b], -1.0, None, ALU.add).then_inc(sem(f"key{l}"), 1)
                for name in ("he_ready", "h_added", "heT"):
                    dve.sem_inc(sem(f"{name}{l}"), PRIMED)
                select(0)
                link(nc.vector.tensor_reduce(rstat[:, 9, 0:1], B[7][:, 16:20], X, ALU.max))
                link(nc.vector.tensor_scalar(rstat[:, 9, 1:2], rstat[:, 9, 0:1], float(P), float(G), ALU.is_gt, ALU.mult))
                link(nc.vector.tensor_scalar(rstat[:, 9, 2:3], rstat[:, 9, 0:1], float(2 * P), float(G), ALU.is_gt, ALU.mult))
                link(nc.vector.tensor_tensor(rstat[:, 9, 1:2], rstat[:, 9, 1:2], rstat[:, 9, 2:3], ALU.add))
                if l == 0:
                    link(nc.vector.tensor_scalar(n_iter[:, 2:3], rstat[:, 9, 1:2], float(G - 1), None, ALU.add))
                nc.vector.tensor_scalar(n_iter[:, l:l + 1], rstat[:, 9, 1:2], float(G), None, ALU.add).then_inc(sem("n_iter_ready"), 1)
                lower_weights(l, 0, 0)
                lower_weights(l, 0, 2)
                x_low(0, 0)
                link(nc.vector.tensor_tensor(picked[:, a:b, :, :], logits[:, a:b, G:36].rearrange("p t (g e) -> p t g e", g=G),
                                             onehot[:, a:b, :].unsqueeze(3).to_broadcast([P, NT, G, EPG]), ALU.mult))
                link(nc.vector.tensor_reduce(esel[:, a:b, :], picked[:, a:b, :, :].rearrange("p t g e -> p t e g"), X, ALU.add))
                for t in tiles:
                    link(nc.vector.max(top_e[:, t, :], esel[:, t, :]))
                nc.vector.tensor_tensor(rstat[:, 3, a:b].unsqueeze(2), top_e[:, a:b, 1:2], top_e[:, a:b, 0:1],
                                        ALU.subtract).then_inc(sem("top_diff"), 1)
                for t in tiles:
                    link(nc.vector.max_index(idx_e[:, t, :], top_e[:, t, :], esel[:, t, :]))
                link(nc.vector.tensor_copy(rstat[:, 1:3, a:b], idx_e[:, a:b, 0:2].rearrange("p t k -> p k t")))
                x_low(0, 1)
                dve.wait_ge(sem("gl_exp"), l + 1)
                link(nc.vector.tensor_reduce(rstat[:, 5, a:b], expg[:, a:b, :], X, ALU.add))
                link(nc.vector.reciprocal(rstat[:, 5, a:b], rstat[:, 5, a:b]))
                dve.wait_ge(sem("top_exp"), l + 1)
                link(nc.vector.tensor_scalar(rstat[:, 6, a:b], rstat[:, 4, a:b], 1.0, None, ALU.add))
                link(nc.vector.reciprocal(rstat[:, 6, a:b], rstat[:, 6, a:b]))
                link(nc.vector.tensor_tensor(rstat[:, 6, a:b], rstat[:, 6, a:b], rstat[:, 5, a:b], ALU.mult))
                link(nc.vector.tensor_tensor(rstat[:, 7, a:b], rstat[:, 6, a:b], rstat[:, 4, a:b], ALU.mult))
                iota8 = iota[:, 0:EPG].unsqueeze(1).to_broadcast([P, NT, EPG])
                for k, dst in ((0, gates), (1, gtmp)):
                    link(nc.vector.tensor_tensor(dst[:, a:b, :], iota8, rstat[:, 1 + k, a:b].unsqueeze(2).to_broadcast([P, NT, EPG]), ALU.is_equal))
                    link(nc.vector.tensor_tensor(dst[:, a:b, :], dst[:, a:b, :], rstat[:, 6 + k, a:b].unsqueeze(2).to_broadcast([P, NT, EPG]), ALU.mult))
                nc.vector.tensor_tensor(gates[:, a:b, :], gates[:, a:b, :], gtmp[:, a:b, :], ALU.add).then_inc(sem("gates"), 1)

                dve.wait_ge(sem("n_iter_ready"), l + 1)
                n_it = dve.value_load(n_iter[0:1, l:l + 1], min_val=G, max_val=3 * G)
                nadd = 2 * NT

                def slot_gates_out(it):
                    dve.wait_ge(sem(f"gates_ps{l}"), it + 1)
                    nc.vector.tensor_copy(slot_gates[:, :], B[7][:, 0:EPG]).then_inc(sem(f"slot_gates{l}"), 1)

                def y_out(s):
                    for half in range(2):
                        dve.wait_ge(sem(f"y_hi{l}"), 2 * s + half + 1)
                        part = slice(half * W, (half + 1) * W)
                        nc.vector.tensor_tensor(ysum_lo[:, part], B[5 + half][:, :], ysum_hi[:, part].bitcast(f32),
                                                ALU.subtract).then_inc(sem(f"y_lo{l}"), 1)

                def add_tokens(s, part):
                    for k in (2 * part, 2 * part + 1):
                        half, t = k // NT, tiles[k % NT]
                        n = TILE_N[t]
                        dve.wait_ge(sem(f"sc_ps{l}"), PRIMED + s * nadd + k + 1)
                        dve.wait_ge(sem(f"h_added{l}"), PRIMED + s * nadd)
                        hh = h[0:n, t, half * W:(half + 1) * W]
                        nc.vector.tensor_tensor(hh, B[k % 2][0:n, :], hh, ALU.add).then_inc(sem(f"h_added{l}"), 1)

                with dve.Fori(0, n_it) as it:
                    y_out(it)
                    todo = BUFS
                    for e in range(EPG):
                        while todo < NU and todo - BUFS <= AT["gu", e, 1]:
                            if todo - BUFS == AT["gu", e, 0] and e >= 2:
                                heT_low(l, it, e - 2)
                            todo = lower_weights(l, it, todo)
                        if e == 0:
                            dve.wait_ge(sem(f"he_ready{l}"), PRIMED + it * EPG)
                            slot_gates_out(it)
                            dve.wait_ge(sem(f"slot_gates{l}"), it + 1)
                        dve.wait_ge(sem(f"silu{l}"), it * EPG + e + 1)
                        if e >= 2:
                            dve.wait_ge(sem(f"heT_ps{l}"), it * EPG + e - 1)
                        nc.vector.scalar_tensor_tensor(he[:, e % 2, :], act_g[:, e % 2, :], slot_gates[:, e:e + 1], B[2 + e % 2][:, F:2 * F],
                                                       ALU.mult, ALU.mult).then_inc(sem(f"he_ready{l}"), 1)
                        if 1 <= e <= NT:
                            add_tokens(it, e - 1)
                        if e == 3:
                            dve.wait_ge(sem(f"selT_ps{l}"), it + 1)
                            nc.vector.tensor_copy(selT[:, TILE_AT[a]:T], B[7][:, 64 + TILE_AT[a]:64 + T]).then_inc(sem(f"selT{l}"), 1)
                        if e == 5:
                            select(it + 1)
                    with dve.If(n_it > it + 1):
                        lower_weights(l, it + 1, 0)
                    heT_low(l, it, EPG - 2)
                    with dve.If(n_it > it + 1):
                        x_low(it + 1, 0)
                    heT_low(l, it, EPG - 1)
                    with dve.If(n_it > it + 1):
                        x_low(it + 1, 1)
                        lower_weights(l, it + 1, 2)

                y_out(n_it)
                for part in range(NT):
                    add_tokens(n_it, part)
                dve.wait_ge(sem(f"h_added{l}"), PRIMED + n_it * nadd + nadd)

            def lower_weights(l, it, j):
                if j not in POOL_UNITS:
                    subtract(dve, nc.vector, l, it, j)
                return j + 1

            def heT_low(l, it, e):
                dve.wait_ge(sem(f"heT_hi{l}"), it * EPG + e + 1)
                nc.vector.tensor_tensor(heT_lo[:, e % 2, :, :], B[4][:, 0:2 * P].rearrange("p (c n) -> p c n", c=2),
                                        heT_hi[:, e % 2, :, :].bitcast(f32), ALU.subtract).then_inc(sem(f"heT{l}"), 1)

            moe(0)

            norm(2)
            transposes_out(2)
            low_mix(dve, nc.vector, 1, 1)
            dve.wait_ge(sem("att_params_in"), 48)
            link(nc.vector.tensor_scalar(qk_gain[:, 0, :], qk_gain[:, 0, :], HD ** -0.5, None, ALU.mult))

            def head_var(sq, first):
                at = slice(first, first + sq.shape[1])
                link(nc.vector.tensor_reduce(hstat[:, 0, at], sq, X, ALU.add))
                nc.vector.tensor_scalar(hstat[:, 1, at], hstat[:, 0, at], 1.0 / HD, EPS, ALU.mult, ALU.add).then_inc(sem("head_var"), 1)

            def head_rstd(sq, first, nth):
                at = slice(first, first + sq.shape[1])
                dve.wait_ge(sem("head_std"), nth)
                nc.vector.reciprocal(hstat[:, 3, at], hstat[:, 2, at]).then_inc(sem("head_rstd"), 1)
                dve.wait_ge(sem("head_rstd"), nth)

            low_mix(dve, nc.vector, 1, 3)
            dve.wait_ge(sem("q_raw"), 4)
            head_var(qsq[:, 0], 16)
            head_rstd(qsq[:, 0], 16, 1)
            scale_heads(link, nc.vector, qs[:, 0:2].rearrange("p i h d -> p (i h) d"), 16, qk_gain[:, 0, :])
            for i in range(2):
                rotate(link, nc.vector, qs[:, i], qs[:, i], 1 + i, rot_dve)
                dve.sem_inc(sem("rotated"), 1)
            for t in range(3):
                dve.wait_ge(sem("kv_raw"), 3 * t + 3)
                head_var(ksq[:, KVH * t:KVH * t + KVH, :], KVH * t)
                head_rstd(ksq[:, KVH * t:KVH * t + KVH, :], KVH * t, 2 + t)
                scale_heads(link, nc.vector, ks[:, t, :, :], KVH * t, qk_gain[:, 1, :])
                rotate(link, nc.vector, ks[:, t, :, :], ks2[:, t, :, 0:HD], t, rot_dve)
                nc.vector.tensor_copy(ks2[:, t, :, HD:2 * HD], ks2[:, t, :, 0:HD]).then_inc(sem("rotated"), 1)

            def maxima(u):
                for o in range(2):
                    dve.wait_ge(sem("s_ps"), 2 * u + o + 1)
                    nc.vector.tensor_reduce(att_max[:, 2 * u + o:2 * u + o + 1], B[2 * (u % 2) + o][:, 0:T], X, ALU.max, negate=True).then_inc(sem("s_max"), 1)

            def normalise(u):
                dve.wait_ge(sem("p_exp"), 2 * u + 2)
                link(nc.vector.reciprocal(att_rcp[:, 2 * u:2 * u + 2], att_sum[:, 2 * u:2 * u + 2]))
                for o in range(2):
                    pr = probs[:, 2 * (u % 2) + o, :]
                    nc.vector.tensor_scalar(pr, pr, att_rcp[:, 2 * u + o:2 * u + o + 1], None, ALU.mult).then_inc(sem("p_ready"), 1)

            def out_of_psum(u):
                dve.wait_ge(sem("pT_ps"), u + 1)
                if u >= 2:
                    dve.wait_ge(sem("oT_ps"), u - 1)
                nc.vector.tensor_copy(pTm[0:NM, u % 2, :, :], B[6][0:NM, 0:2 * P].rearrange("p (o n) -> p o n", o=2)).then_inc(sem("pTm_ev"), 1)

            def oT_out(u):
                _, i, pair = UNIT_OF[u]
                dve.wait_ge(sem("feat_hi"), 4 + u + 1)
                nc.vector.tensor_tensor(hnT_lo[:, pair, i * P:(i + 1) * P], B[7][:, 0:P],
                                        hnT_hi[:, pair, i * P:(i + 1) * P].bitcast(f32), ALU.subtract).then_inc(sem("oT_ev"), 1)

            maxima(0)
            normalise(0)
            maxima(1)
            normalise(1)
            for u in range(16):
                if 0 < u < 15:
                    maxima(u + 1)
                if 0 < u < 15:
                    normalise(u + 1)
                out_of_psum(u)
                if u:
                    oT_out(u - 1)
                if u == 0:
                    dve.wait_ge(sem("q_raw"), 8)
                    head_var(qsq[:, 1], 32)
                if u == 1:
                    head_rstd(qsq[:, 1], 32, 5)
            oT_out(15)
            for half in range(2):
                for i in range(2):
                    k = 2 * half + i
                    if k == 1:
                        low_mix(dve, nc.vector, 1, 9)
                    dve.wait_ge(sem("proj_ps"), PROJ["out1"] + k + 1)
                    hh = h[:, 1 + i, half * W:(half + 1) * W]
                    nc.vector.tensor_tensor(hh, B[k][:, :], hh, ALU.add).then_inc(sem("h_mixed1"), 1)
                    if half == 1:
                        norm_tile(3, i)
            moe(1)
            norm(4)

        @block.tensor
        def _(pe):
            mm = nc.tensor.matmul

            def transposes(n):
                for i, t in enumerate(NORM_TILES[n]):
                    m = TILE_N[t]
                    pe.wait_ge(sem("hn_ready"), upto(n) + i + 1)
                    if i == 0:
                        pe.wait_ge(sem("ident_in"), 16)
                    for half in range(2):
                        if i and n % 2:
                            pe.wait_ge(sem(f"hnT_{('act', 'dve')[half]}"), hnT_count(n) + i)
                        elif i:
                            pe.wait_ge(sem("hnT_dve"), hnT_count(n) + 2 * i - 1 + half)
                        for c in range(4):
                            last = nc.tensor.transpose(B[half][:, c * P:c * P + m], hn[0:m, t, 4 * half + c:D:KC], ident[0:m, 0:m])
                        last.then_inc(sem("hnT_ps"), 1)

            def mix_weights(l, b):
                there = [False, False]

                def parts(c, lo, hi):
                    half = c // 4
                    if not there[half]:
                        name, count = mix_low_done(l, 2 * b + half)
                        pe.wait_ge(sem(name), count)
                        there[half] = True
                    u = 2 * b + half
                    cols = slice(c % 4 * W + lo, c % 4 * W + hi)
                    return mix_hi[u % MIX_BUFS][:, cols], mix_lo[(MIX_SLOT0[l] + u) % RING][:, cols]
                return parts

            def split_product(dst, left, right, start, stop):
                mm(dst, left[0], right[0], start=start, stop=False)
                mm(dst, left[1], right[0], start=False, stop=False)
                return mm(dst, left[0], right[1], start=False, stop=stop)

            def features(c, lo, hi):
                return hnT_hi[:, c, lo:hi], hnT_lo[:, c, lo:hi]

            transposes(0)
            wait_hnT(pe, 0)
            pe.wait_ge(sem("clear"), 3)
            for c in range(KC):
                last = split_product(B[2][0:2 * RANK, 0:T], (w_g_hi[:, c, :], w_g_lo[:, c, :]), features(c, 0, T), c == 0, c == KC - 1)
            last.then_inc(sem("proj_ps"), 1)

            def product(dst, sides, closing):
                for c in range(KC):
                    left, right = sides(c)
                    last = split_product(dst, left, right, c == 0, c == KC - 1)
                    if closing and c == KC // 2 - 1:
                        last.then_inc(sem("mix_used"), 1)
                last.then_inc(sem("proj_ps"), 1)

            def feature_major(w, m, bank, closing=False):
                product(bank[:, 0:T], lambda c: (w(c, m * P, (m + 1) * P), features(c, 0, T)), closing)

            def token_major(w, t, lo, hi, bank, rows=None, closing=False, at=None):
                n = rows or TILE_N[t]
                at = TILE_AT[t] if at is None else at
                product(bank[0:n, 0:hi - lo], lambda c: (features(c, at, at + n), w(c, lo, hi)), closing)

            w = mix_weights(0, 0)
            for m in range(2):
                feature_major(w, m, B[3 + m])
            for t in range(3):
                token_major(w, t, 256, 512, B[5 + t], closing=t == 2)
            pe.wait_ge(sem("g_ev"), 1)
            pe.wait_ge(sem("gla_params_in"), 128)
            for t in range(3):
                n = TILE_N[t]
                mm(B[t][0:n, :], gT[:, TILE_AT[t]:TILE_AT[t] + n], wgate[:, :], start=True, stop=True).then_inc(sem("la_ps"), 1)
            w = mix_weights(0, 1)
            for t in range(3):
                pe.wait_ge(sem("q_ev"), t + 1) if t < 2 else pe.wait_ge(sem("k_ev"), 1)
                token_major(w, t, 0, W, B[3 + t], closing=t == 2)
            pe.wait_ge(sem("k_ev"), 3)
            for m in range(2):
                for t in range(3):
                    n = TILE_N[t]
                    last = nc.tensor.transpose(B[6 + m][:, TILE_AT[t]:TILE_AT[t] + n], ktok[0:n, t, m * P:(m + 1) * P], ident[0:n, 0:n])
                last.then_inc(sem("kT_ps"), 1)
            w = mix_weights(0, 2)
            for t in range(3):
                pe.wait_ge(sem("v_ev"), t + 1)
                token_major(w, t, 0, W, B[3 + t], closing=t == 2)
            w = mix_weights(0, 3)
            for m in range(4):
                pe.wait_ge(sem("kT_ev"), m + 1) if m < 2 else pe.wait_ge(sem("ax_ev"), m - 1)
                feature_major(w, m, B[6 + m % 2], closing=m == 3)
            pe.wait_ge(sem("la_ready"), 3)
            pe.wait_ge(sem("consts_in"), 16)
            for dm in range(4):
                if dm == 3:
                    pe.wait_ge(sem("r_ev"), 1)
                for t in range(3):
                    n = TILE_N[t]
                    last = mm(B[dm][:, TILE_AT[t]:TILE_AT[t] + n], la[0:n, t, dm * P:(dm + 1) * P],
                              (incl_fwd, incl_bwd)[dm // 2][0:n, 0:n], start=True, stop=True)
                last.then_inc(sem("cum_ps"), 1)
            for t in range(3):
                n = TILE_N[t]
                bank = B[[4, 5, 0][t]]
                pe.wait_ge(sem("r_ev"), t + 2) if t < 2 else pe.wait_ge(sem("E_exp"), 2)
                mm(bank[0:n, 0:256], strict_bwd[0:n, 0:n], la[0:n, t, 0:256], start=True, stop=True)
                mm(bank[0:n, 256:512], strict_fwd[0:n, 0:n], la[0:n, t, 256:512], start=True, stop=True).then_inc(sem("kend_ps"), 1)
            w = mix_weights(0, 4)
            for m in range(4):
                pe.wait_ge(sem("ax_ev"), m + 3) if m < 2 else pe.wait_ge(sem("z_ready"), m - 1)
                feature_major(w, m, B[6 + m % 2], closing=m == 3)
            w = mix_weights(0, 5)
            for m in range(4):
                pe.wait_ge(sem("z_ready"), m + 3) if m < 2 else pe.wait_ge(sem("ya_ready"), m - 1)
                feature_major(w, m, B[6 + m % 2], closing=m == 3)
            pe.wait_ge(sem("kend"), 6)
            pe.wait_ge(sem("E_exp"), 8)
            pe.wait_ge(sem("v_ev"), 3)

            def chunk_sums(k):
                d, i = k % 2, k // 2
                t, p0, n = CHUNKS[i if d == 0 else 4 - i]
                if k >= 6:
                    pe.wait_ge(sem("state"), 4 * (k - 1))
                bank = B[[2, 3, 4, 5, 0, 1, 0, 1][k]]
                for m in range(2):
                    last = mm(bank[:, 256 * m:256 * m + 256], kend[p0:p0 + n, t, 256 * d + P * m:256 * d + P * (m + 1)],
                              v[p0:p0 + n, t, 256 * m:256 * m + 256], start=True, stop=True)
                last.then_inc(sem("kvs_ps"), 1)

            def scores(i, t):
                n = TILE_N[t]
                at = TILE_AT[t]
                for hd in range(HEADS):
                    m, rows = hd // 2, slice(64 * (hd % 2), 64 * (hd % 2) + 64)
                    if i:
                        pe.wait_ge(sem("masked"), hd + 1 if i == 1 else 8)
                    for d in range(2):
                        last = mm(score_place(i, hd)[0:n, d * P:d * P + n], Ei[rows, 2 * d + m, at:at + n], E[rows, 2 * d + m, at:at + n], start=True, stop=True)
                    last.then_inc(sem("sc_ps"), 1)

            def outputs(i, t):
                n = TILE_N[t]
                at = TILE_AT[t]
                base = OUT_BANK[i]
                if i == 0:
                    pe.wait_ge(sem("ya_ready"), 4)
                for hd in range(HEADS):
                    m, hh = hd // 2, hd % 2
                    o = B[base + hh]
                    pe.wait_ge(sem("masked"), 4 * i + hd + 1)
                    for d in range(2):
                        mm(o[0:n, m * DV:(m + 1) * DV], masked[0:n, HEADS * (i % 2) + hd, d * P:d * P + n], v[0:n, t, hd * DV:(hd + 1) * DV],
                           start=(m == 0 and d == 0), stop=False, skip_group_check=True)
                if i == 0:
                    pe.wait_ge(sem("state"), 32)
                for hd in range(HEADS):
                    m, hh = hd // 2, hd % 2
                    o = B[base + hh]
                    rows = slice(64 * hh, 64 * hh + 64)
                    for j, (tt, p0, cn) in enumerate(CHUNKS):
                        if tt != t:
                            continue
                        for d, prev in ((0, j - 1), (1, 3 - j)):
                            if 0 <= prev <= 3:
                                last = mm(o[p0:p0 + cn, m * DV:(m + 1) * DV], E[rows, 2 * d + m, at + p0:at + p0 + cn],
                                          state[rows, 4 * d + prev, m, :], start=False, stop=True, skip_group_check=True)
                last.then_inc(sem("o_ps"), 1)

            def yb_transposes(i, t):
                n = TILE_N[t]
                pe.wait_ge(sem("yb_ready"), 4 * i + 4)
                for hd in range(HEADS):
                    last = nc.tensor.transpose(B[OUT_BANK[i]][:, hd * P:hd * P + n], yb[0:n, t, hd * P:(hd + 1) * P], ident[0:n, 0:n])
                last.then_inc(sem("ybT_ps"), 1)

            for k in range(6):
                chunk_sums(k)
            pe.wait_ge(sem("state"), 16)
            pe.wait_ge(sem("qk_dec"), 4)
            scores(0, 1)
            chunk_sums(6)
            chunk_sums(7)
            scores(1, 2)
            outputs(0, 1)
            scores(2, 0)
            pe.wait_ge(sem("state"), 32)
            outputs(1, 2)
            outputs(2, 0)
            yb_transposes(0, 1)
            yb_transposes(1, 2)
            yb_transposes(2, 0)
            pe.wait_ge(sem("ybT_ev"), 3)
            pe.wait_ge(sem("pool_step"), 3)
            for half in range(2):
                w = mix_weights(0, 6 + half)
                for t in range(3):
                    token_major(w, t, 0, W, B[2 + 3 * half + t], closing=t == 2)

            def moe(l):
                n = 1 + 2 * l
                tiles = NORM_TILES[n]
                a, b = tiles[0], tiles[-1] + 1
                NT = b - a
                transposes(n)
                mm(B[5][:, :], ident, consts[:, 0:W], start=True, stop=True)
                mm(B[6][:, :], ident, consts[:, 0:W], start=True, stop=True).then_inc(sem(f"w_used{l}"), BUFS)
                wait_hnT(pe, n)
                pe.wait_ge(sem("route_in"), 128)
                for c in range(KC):
                    last = mm(B[7][0:36, TILE_AT[a]:T], w_route[l][:, c, :], hnT[:, c, TILE_AT[a]:T], start=(c == 0), stop=(c == KC - 1))
                last.then_inc(sem("logitsT_ps"), 1)
                pe.wait_ge(sem("logitsT"), l + 1)
                for t in tiles:
                    last = nc.tensor.transpose(B[6][:, 36 * t:36 * t + 36], logitsT[0:36, TILE_AT[t]:TILE_AT[t] + P], ident[0:36, 0:36])
                last.then_inc(sem("logits_ps"), 1)
                pe.wait_ge(sem("onehot"), l + 1)
                for t in tiles:
                    for s in range(a, t + 1):
                        mm(B[7][:, 4 * t:4 * t + 4], before if s == t else ones, onehot[:, s, :], start=(s == a), stop=(s == t))
                for s in tiles:
                    last = mm(B[7][:, 16:20], ones, onehot[:, s, :], start=(s == a), stop=(s == b - 1))
                last.then_inc(sem("rank_ps"), 1)
                nadd = 2 * NT

                def wait_split(it, j):
                    name, count, per = low_done(j)
                    pe.wait_ge(sem(f"{name}{l}"), it * per + count)

                def gate_up(it, e):
                    if e < 2:
                        pe.wait_ge(sem(f"he_ready{l}"), PRIMED + it * EPG)
                    else:
                        pe.wait_ge(sem(f"he_ready{l}"), PRIMED + it * EPG + e - 1)
                    for half in range(2):
                        j = AT["gu", e, half]
                        wait_split(it, j)
                        if e == 0:
                            pe.wait_ge(sem(f"x_lo{l}"), 2 * it + half + 1)
                        parts = [w[j % BUFS][:, :].rearrange("p (u c n) -> p u c n", u=2, c=4) for w in (w_hi, w_lo)]
                        for cc in range(4):
                            c = 4 * half + cc
                            last = split_product(B[2 + e % 2][:, :], (x_hi[:, c, :], x_lo[:, c, :]), [w[:, :, cc, :] for w in parts],
                                                 c == 0, c == KC - 1)
                        last.then_inc(sem(f"w_used{l}"), 1)

                def he_transposes(it, e):
                    pe.wait_ge(sem(f"he_ready{l}"), PRIMED + it * EPG + e + 1)
                    pe.wait_ge(sem(f"heT{l}"), PRIMED + it * EPG + e)
                    for c in range(2):
                        last = nc.tensor.transpose(B[4][:, c * P:(c + 1) * P], he[:, e % 2, c:F:2], ident)
                    last.then_inc(sem(f"heT_ps{l}"), 1)

                def down(it, e):
                    pe.wait_ge(sem(f"heT{l}"), PRIMED + it * EPG + e + 1)
                    j = AT["d", e, 0]
                    wait_split(it, j)
                    if e == 0:
                        pe.wait_ge(sem(f"y_lo{l}"), 2 * it + 2)
                    for half in range(2):
                        for c in range(2):
                            at = c * D + half * W
                            last = split_product(B[5 + half][:, :], (heT_hi[:, e % 2, c, :], heT_lo[:, e % 2, c, :]),
                                                 [w[j % BUFS][:, at:at + W] for w in (w_hi, w_lo)],
                                                 e == 0 and c == 0, e == EPG - 1 and c == 1)
                    last.then_inc(sem(f"w_used{l}"), 1)

                def gather(it, half):
                    pe.wait_ge(sem(f"sel{l}"), it + 1)
                    pe.wait_ge(sem(f"h_added{l}"), PRIMED + it * nadd)
                    for c in range(4):
                        for t in tiles:
                            m = TILE_N[t]
                            last = mm(B[half][:, c * P:(c + 1) * P], hn[0:m, t, 4 * half + c:D:KC], sel[0:m, t, :],
                                      start=(t == a), stop=(t == b - 1))
                    last.then_inc(sem(f"x_ps{l}"), 1)

                def gather_gates(it):
                    pe.wait_ge(sem(f"selT{l}"), it + 1)
                    for t in tiles:
                        m = TILE_N[t]
                        last = mm(B[7][:, 0:EPG], sel[0:m, t, :], gates[0:m, t, :], start=(t == a), stop=(t == b - 1))
                    last.then_inc(sem(f"gates_ps{l}"), 1)

                def transpose_selection(it):
                    pe.wait_ge(sem(f"slot_gates{l}"), it + 1)
                    for t in tiles[::-1]:
                        m = TILE_N[t]
                        last = nc.tensor.transpose(B[7][:, 64 + TILE_AT[t]:64 + TILE_AT[t] + m], sel[0:m, t, :], ident[0:m, 0:m])
                    last.then_inc(sem(f"selT_ps{l}"), 1)

                def scatter(s, part, gathered):
                    if part == 0:
                        pe.wait_ge(sem(f"selT{l}"), s + 1)
                        pe.wait_ge(sem(f"x_lo{l}"), 2 * gathered)
                        pe.wait_ge(sem(f"y_lo{l}"), 2 * s + 2)
                    for k in (2 * part, 2 * part + 1):
                        half, t = k // NT, tiles[k % NT]
                        m = TILE_N[t]
                        if k >= 2:
                            pe.wait_ge(sem(f"h_added{l}"), PRIMED + s * nadd + k - 1)
                        back = selT[:, TILE_AT[t]:TILE_AT[t] + m]
                        mm(B[k % 2][0:m, :], back, ysum_hi[:, half * W:(half + 1) * W], start=True, stop=False)
                        mm(B[k % 2][0:m, :], back, ysum_lo[:, half * W:(half + 1) * W], start=False, stop=True).then_inc(sem(f"sc_ps{l}"), 1)

                pe.sem_inc(sem(f"sc_ps{l}"), PRIMED)
                gather(0, 0)
                gather(0, 1)
                pe.wait_ge(sem("n_iter_ready"), l + 1)
                n_it = pe.value_load(n_iter[0:1, l:l + 1], min_val=G, max_val=3 * G)
                with pe.Fori(0, n_it) as it:
                    gate_up(it, 0)
                    pe.wait_ge(sem("gates"), l + 1)
                    gather_gates(it)
                    gate_up(it, 1)
                    for e in range(EPG):
                        he_transposes(it, e)
                        if e < NT:
                            scatter(it, e, it + 1)
                        if e == 2:
                            transpose_selection(it)
                        if e >= EPG - 2:
                            with pe.If(n_it > it + 1):
                                gather(it + 1, e - (EPG - 2))
                        if e + 2 < EPG:
                            gate_up(it, e + 2)
                        down(it, e)
                for part in range(NT):
                    scatter(n_it, part, n_it)

            moe(0)

            transposes(2)
            wait_hnT(pe, 2)
            w = mix_weights(1, 0)
            for i in range(2):
                token_major(w, 1 + i, 0, W, B[5 + i], closing=i == 1)
            w = mix_weights(1, 1)
            for t in range(3):
                token_major(w, t, 0, W, B[2 + t], rows=P, closing=t == 2)
            w = mix_weights(1, 2)
            token_major(w, 1, 0, W, B[0])
            pe.wait_ge(sem("rotated"), 5)
            pe.wait_ge(sem("kv_raw"), 9)
            for hv in range(KVH):
                for t in range(3):
                    m = TILE_N[t]
                    last = nc.tensor.transpose(B[[1, 2, 3, 4][hv]][:, TILE_AT[t]:TILE_AT[t] + m], ks2[0:m, t, hv, :], ident[0:m, 0:m])
                last.then_inc(sem("qk1T_ps"), 1)

            def q_transposes(n):
                for i in range(2):
                    for c in range(4):
                        last = nc.tensor.transpose(B[[5, 6, 0, 1][2 * n + i]][:, c * P:(c + 1) * P],
                                                   qs[:, 2 * n + i, 2 * c:2 * c + 2, :].rearrange("p h d -> p (h d)"), ident)
                    last.then_inc(sem("qk1T_ps"), 1)

            pe.wait_ge(sem("q_raw"), 6)
            q_transposes(0)
            pe.wait_ge(sem("qk1T_ev"), KVH + 2)

            def att_scores(u):
                _, i, pair = UNIT_OF[u]
                if u == 8:
                    pe.wait_ge(sem("qk1T_ev"), KVH + 4)
                if u >= 2:
                    pe.wait_ge(sem("p_exp"), 2 * (u - 1))
                for o in range(2):
                    rows = slice(64 * o, 64 * o + 64)
                    mm(B[2 * (u % 2) + o][:, 0:T], qT1[rows, pair, i * P:(i + 1) * P], kT1[rows, pair // 2, :],
                       start=True, stop=True).then_inc(sem("s_ps"), 1)

            def att_values(u):
                hv = UNIT_OF[u][2] // 2
                pe.wait_ge(sem("pT_ev"), u + 1)
                pe.wait_ge(sem("pTm_ev"), u + 1)
                if u:
                    pe.wait_ge(sem("oT_ev"), u)
                else:
                    pe.wait_ge(sem("q_raw"), 8)
                for o in range(2):
                    dst = B[7][64 * o:64 * o + 64, 0:P]
                    mm(dst, vs[:, 1, hv * HD:(hv + 1) * HD], pT[:, u % 2, 2 * o, :], start=True, stop=False)
                    mm(dst, vs[:, 2, hv * HD:(hv + 1) * HD], pT[:, u % 2, 2 * o + 1, :], start=False, stop=False)
                    last = mm(dst, vs[0:NM, 0, hv * HD:(hv + 1) * HD], pTm[0:NM, u % 2, o, :], start=False, stop=True)
                last.then_inc(sem("oT_ps"), 1)

            att_scores(0)
            att_scores(1)
            token_major(w, 2, 0, W, B[7], closing=True)
            for u in range(17):
                if 0 < u < 15:
                    att_scores(u + 1)
                if u == 16:
                    att_values(u - 1)
                    break
                pe.wait_ge(sem("p_ready"), 2 * u + 2)
                if u >= 2:
                    pe.wait_ge(sem("pT_ev"), u - 1)
                for o in range(2):
                    for t in (1, 2):
                        last = nc.tensor.transpose(B[4 + u % 2][:, (2 * o + t - 1) * P:(2 * o + t) * P],
                                                   probs[:, 2 * (u % 2) + o, TILE_AT[t]:TILE_AT[t] + P], ident)
                if u:
                    pe.wait_ge(sem("pTm_ev"), u)
                for o in range(2):
                    last = nc.tensor.transpose(B[6][0:NM, o * P:(o + 1) * P], probs[:, 2 * (u % 2) + o, 0:NM], ident)
                last.then_inc(sem("pT_ps"), 1)
                if u:
                    att_values(u - 1)
                if u == 6:
                    pe.wait_ge(sem("p_exp"), 14)
                    pe.wait_ge(sem("pool_step"), 4)
                    q_transposes(1)
            pe.wait_ge(sem("oT_ev"), 16)
            for half in range(2):
                w = mix_weights(1, 3 + half)
                for i in range(2):
                    token_major(w, 1 + i, 0, W, B[2 * half + i], closing=i == 1, at=i * P)
            moe(1)


_INS = ["x", "meta_tokens", "norm_mix", "norm_ffn", "norm_final", "sc_w_in", "sc_conv_w", "gla_w_gate_fwd",
        "gla_b_gate_fwd", "gla_w_gate_bwd", "gla_b_gate_bwd", "gla_norm_w", "sc_w_out", "att_w_in",
        "att_q_norm", "att_k_norm", "att_w_out", "moe_w_group", "moe_b_group", "moe_w_expert",
        "moe_b_expert", "moe_w_gate", "moe_w_up", "moe_w_down"]


def _constants():
    import numpy as np
    s, c = np.arange(128)[:, None], np.arange(128)[None, :]
    same = s // 64 == c // 64
    valid = np.ones((128, 3))
    valid[16:, 0] = 0
    parts = [s == c, same & (s <= c), same & (s > c), same & (s >= c), same & (s < c), s < c, s >= 0 * c, c + 0 * s, valid]
    consts = np.concatenate([np.broadcast_to(p, (128, p.shape[1])) for p in parts], axis=1).astype(np.float32)
    pos = np.arange(256)
    freqs = (np.float32(10000.0) ** (-np.arange(0, 32, 2, dtype=np.float32) / np.float32(32))).astype(np.float32)
    ang = np.concatenate([(pos // 64).astype(np.float32)[:, None] * freqs, (pos % 64).astype(np.float32)[:, None] * freqs], axis=1)
    ang = np.concatenate([np.zeros((128, 32), np.float32), ang]).astype(np.float32)
    table = np.stack([np.cos(ang), np.sin(ang)]).astype(np.float32).reshape(2, 3, 128, 32).transpose(2, 0, 1, 3)
    return np.ascontiguousarray(consts), np.ascontiguousarray(table.reshape(128, 192))


def kernel(**inputs):
    import numpy as _np
    import concourse.bacc as _bacc
    from concourse import mybir as _mybir
    from concourse.bass_utils import run_bass_kernel_spmd as _run

    nc = _bacc.Bacc("TRN2", target_bir_lowering=False, num_devices=1)
    given = {name: _np.ascontiguousarray(inputs[name]) for name in _INS}
    given["consts"], given["rope"] = _constants()
    arrays, args = {}, {}
    for name, a in given.items():
        arrays[f"in_{name}"] = a
        args[name] = nc.dram_tensor(f"in_{name}", a.shape, _mybir.dt.from_np(a.dtype), kind="ExternalInput").ap()
    shape = given["x"].shape
    out = nc.dram_tensor("out_0", shape, _mybir.dt.from_np(given["x"].dtype), kind="ExternalOutput").ap()
    build_program(nc, args, out)
    r = _run(nc, [arrays], core_ids=[0])
    return r.results[0]["out_0"]
```
